# Optimizing a Trainium2 kernel written in Bass

```python
import math
import jax, jax.numpy as jnp
from jax import lax
import numpy as np

D_MODEL = 1024
BATCH = 1
SEQ = 256
DEPTH = 2

F32 = jnp.float32
EPS = 1e-6
N_MEM = 256
N_BRANCH = 4
MAX_POS_OFFSET = 1024

W_A = 512
W_S = 512
S5_GROUP = 16
S5_GROUPS = W_S // S5_GROUP
S5_STATE = 64
MLA_HEADS = 8
Q_LORA = 256
KV_LORA = 256
QK_NOPE = 64
QK_ROPE = 32
V_DIM = 64
ROPE_BASE = 10000.0
Q_BLOCK = 128
W_H = 512
HY_ORDER = 2
HY_EMB = 33
HY_BANDS = (HY_EMB - 1) // 2
HY_FO = 64
HY_FAST_DECAY = 0.3
HY_SLOW_DECAY = 1.5
HY_TARGET = 1e-2
N_IN_A = 3 * W_A
N_IN_S = W_S
N_IN_M = Q_LORA + KV_LORA + QK_ROPE
N_IN_H = 3 * W_H
N_IN_G = N_BRANCH * D_MODEL
N_IN = N_IN_A + N_IN_S + N_IN_M + N_IN_H + N_IN_G
IN_SPLITS = [N_IN_A, N_IN_A + N_IN_S, N_IN_A + N_IN_S + N_IN_M, N_IN_A + N_IN_S + N_IN_M + N_IN_H]
XA_HEADS = 4
XA_DH = 128
N_GROUPS = 4
EXP_PER_GROUP = 8
N_EXPERTS = N_GROUPS * EXP_PER_GROUP
TOP_K = 2
D_FF_E = 256

kernel_name = "hybrid_parallel_gated_encoder"

def rmsnorm(x, g):
    x32 = x.astype(F32)
    y = x32 * lax.rsqrt(jnp.mean(x32 * x32, axis=-1, keepdims=True) + EPS)
    return (y * g.astype(F32)).astype(x.dtype)

def short_conv(u, w):
    up = jnp.pad(u, ((0, 0), (1, 1), (0, 0)))
    return w[0] * up[:, :-2] + w[1] * up[:, 1:-1] + w[2] * up[:, 2:]

def mixer_short_conv(p_a, conv_w, w_out):
    b_gate, c_gate, xin = jnp.split(p_a, 3, axis=-1)
    return (b_gate * short_conv(c_gate * xin, conv_w)) @ w_out

def _linear_recurrence(e1, e2):
    a1, b1 = e1
    a2, b2 = e2
    return a1 * a2, a2 * b1 + b2

def mixer_s5(u, lam_re, lam_im, log_step, b_re, b_im, c_re, c_im, d_skip, w_glu):
    bsz, seqlen, _ = u.shape
    u32 = u.astype(F32)
    ug = u32.reshape(bsz, seqlen, S5_GROUPS, S5_GROUP)
    y = d_skip.astype(F32) * u32
    for direction in range(2):
        lam = lax.complex(lam_re[direction].astype(F32), lam_im[direction].astype(F32))
        delta = jnp.exp(log_step[direction].astype(F32))[:, None]
        lam_bar = jnp.exp(lam * delta)
        b_mat = lax.complex(b_re[direction].astype(F32), b_im[direction].astype(F32))
        b_bar = ((lam_bar - 1.0) / lam)[..., None] * b_mat
        bu = jnp.einsum('blgh,gph->blgp', ug, b_bar)
        a = jnp.broadcast_to(lam_bar, (1, seqlen) + lam_bar.shape)
        _, states = lax.associative_scan(_linear_recurrence, (a, bu), reverse=(direction == 1), axis=1)
        c_mat = lax.complex(c_re[direction].astype(F32), c_im[direction].astype(F32))
        y = y + jnp.real(jnp.einsum('blgp,ghp->blgh', states, c_mat)).reshape(bsz, seqlen, W_S)
    a_half, g_half = jnp.split(jax.nn.gelu(y) @ w_glu.astype(F32), 2, axis=-1)
    return (a_half * jax.nn.sigmoid(g_half)).astype(u.dtype)

def rope(x, cos, sin):
    x1, x2 = jnp.split(x, 2, axis=-1)
    return jnp.concatenate([x1 * cos - x2 * sin, x1 * sin + x2 * cos], axis=-1)

def mixer_mla(p_m, cos, sin, q_norm, w_q_b, kv_norm, w_kv_b, w_o):
    bsz, seqlen, _ = p_m.shape
    c_q, c_kv, k_rope = jnp.split(p_m, [Q_LORA, Q_LORA + KV_LORA], axis=-1)
    q = (rmsnorm(c_q, q_norm) @ w_q_b).reshape(bsz, seqlen, MLA_HEADS, QK_NOPE + QK_ROPE)
    q_nope, q_rope = jnp.split(q, [QK_NOPE], axis=-1)
    q_rope = rope(q_rope, cos[:, :, None], sin[:, :, None])
    k_rope = rope(k_rope, cos, sin)
    kv = (rmsnorm(c_kv, kv_norm) @ w_kv_b).reshape(bsz, seqlen, MLA_HEADS, QK_NOPE + V_DIM)
    k_nope, v = jnp.split(kv, [QK_NOPE], axis=-1)
    scale = (QK_NOPE + QK_ROPE) ** -0.5
    n_blocks = seqlen // Q_BLOCK

    def to_blocks(t):
        return jnp.moveaxis(t.reshape((bsz, n_blocks, Q_BLOCK) + t.shape[2:]), 1, 0)

    def attend(blk):
        qn, qr = blk
        s = jnp.einsum('bqhd,bkhd->bhqk', qn, k_nope) + jnp.einsum('bqhr,bkr->bhqk', qr, k_rope)
        p = jax.nn.softmax(s.astype(F32) * scale, axis=-1).astype(v.dtype)
        return jnp.einsum('bhqk,bkhd->bqhd', p, v)

    o = lax.map(attend, (to_blocks(q_nope), to_blocks(q_rope)))
    o = jnp.moveaxis(o, 0, 1).reshape(bsz, seqlen, MLA_HEADS * V_DIM)
    return o @ w_o

def hyena_filters(seqlen, w1, b1, w2, b2, w3, freq):
    t = jnp.arange(seqlen, dtype=F32)
    t_norm = t / max(seqlen - 1, 1)
    bands = jnp.linspace(1e-4, HY_BANDS - 1, HY_BANDS, dtype=F32)
    ang = (2.0 * math.pi / seqlen) * t[:, None] * bands[None]
    z = jnp.concatenate([t_norm[:, None], jnp.cos(ang), -jnp.sin(ang)], axis=-1)
    fr = freq.astype(F32)
    h = jnp.sin(fr * (z @ w1.astype(F32) + b1.astype(F32)))
    h = jnp.sin(fr * (h @ w2.astype(F32) + b2.astype(F32)))
    filt = (h @ w3.astype(F32)).reshape(seqlen, HY_ORDER, 2, W_H)
    max_decay = math.log(HY_TARGET) / HY_FAST_DECAY
    min_decay = math.log(HY_TARGET) / HY_SLOW_DECAY
    deltas = jnp.abs(jnp.linspace(min_decay, max_decay, W_H, dtype=F32))
    filt = filt * jnp.exp(-t_norm[:, None, None, None] * deltas)
    fwd, bwd = filt[:, :, 0], filt[:, :, 1]
    k = jnp.concatenate([fwd, jnp.zeros_like(fwd[:1]), bwd[:0:-1]], axis=0)
    k = k * lax.rsqrt(jnp.sum(k * k, axis=0, keepdims=True) + EPS)
    return jnp.fft.rfft(k, axis=0)

def fft_conv(u, k_f, bias):
    seqlen = u.shape[1]
    u32 = u.astype(F32)
    u_f = jnp.fft.rfft(u32, n=2 * seqlen, axis=1)
    y = jnp.fft.irfft(u_f * k_f[None], n=2 * seqlen, axis=1)[:, :seqlen]
    return (y + u32 * bias.astype(F32)).astype(u.dtype)

def mixer_hyena(p_h, conv_w, f_w1, f_b1, f_w2, f_b2, f_w3, f_freq, bias, w_out):
    v, x1, x2 = jnp.split(short_conv(p_h, conv_w), 3, axis=-1)
    k_f = hyena_filters(p_h.shape[1], f_w1, f_b1, f_w2, f_b2, f_w3, f_freq)
    z = x1 * fft_conv(v, k_f[:, 0], bias[0])
    z = x2 * fft_conv(z, k_f[:, 1], bias[1])
    return z @ w_out

def cross_attention(h, mem_n, w_q, w_kv, w_o):
    bsz, seqlen, _ = h.shape
    q = (h @ w_q).reshape(bsz, seqlen, XA_HEADS, XA_DH)
    kv = (mem_n @ w_kv).reshape(bsz, mem_n.shape[1], XA_HEADS, 2 * XA_DH)
    k, v = jnp.split(kv, 2, axis=-1)
    s = jnp.einsum('bqhd,bkhd->bhqk', q, k).astype(F32) * (XA_DH ** -0.5)
    p = jax.nn.softmax(s, axis=-1).astype(v.dtype)
    o = jnp.einsum('bhqk,bkhd->bqhd', p, v).reshape(bsz, seqlen, XA_HEADS * XA_DH)
    return o @ w_o

def hier_moe(h, w_group, b_group, w_expert, b_expert, w_gate, w_up, w_down):
    bsz, seqlen, d = h.shape
    t = h.reshape(-1, d)
    g_logits = (t @ w_group).astype(F32) + b_group.astype(F32)
    g_prob = jax.nn.softmax(g_logits, axis=-1)
    g_idx = jnp.argmax(g_logits, axis=-1)
    g_w = jnp.take_along_axis(g_prob, g_idx[:, None], axis=-1)
    e_logits = ((t @ w_expert).astype(F32) + b_expert.astype(F32)).reshape(-1, N_GROUPS, EXP_PER_GROUP)
    e_logits = jnp.take_along_axis(e_logits, g_idx[:, None, None], axis=1)[:, 0]
    top_v, top_i = lax.top_k(e_logits, TOP_K)
    e_w = jax.nn.softmax(top_v, axis=-1) * g_w
    expert_id = g_idx[:, None] * EXP_PER_GROUP + top_i
    combine = jnp.sum(jax.nn.one_hot(expert_id, N_EXPERTS, dtype=F32) * e_w[..., None], axis=1).astype(h.dtype)
    out = jnp.zeros_like(t)
    for g in range(N_GROUPS):
        sl = slice(g * EXP_PER_GROUP, (g + 1) * EXP_PER_GROUP)
        hid = jax.nn.silu(jnp.einsum('td,edf->tef', t, w_gate[sl])) * jnp.einsum('td,edf->tef', t, w_up[sl])
        out = out + jnp.einsum('tef,efd->td', hid * combine[:, sl, None], w_down[sl])
    return out.reshape(bsz, seqlen, d)

def setup_inputs(seed: int = 0) -> dict:
    key = jax.random.key(seed)
    keys = jax.random.split(key, 80)
    counter = [0]

    def nxt():
        k = keys[counter[0]]
        counter[0] += 1
        return k

    def nrm(shape, scale):
        return jax.random.normal(nxt(), shape, F32) * scale

    def gain(shape):
        return 1.0 + nrm(shape, 0.02)

    L = DEPTH
    G, P = S5_GROUPS, S5_STATE
    inp = {}
    inp['x'] = nrm((BATCH, SEQ, D_MODEL), 1.0)
    inp['mem'] = nrm((BATCH, N_MEM, D_MODEL), 1.0)
    inp['positions'] = (jax.random.randint(nxt(), (BATCH, 1), 0, MAX_POS_OFFSET, dtype=jnp.int32)
                        + jnp.arange(SEQ, dtype=jnp.int32)[None])
    inp['mix_norm'] = gain((L, D_MODEL))
    inp['w_in'] = nrm((L, D_MODEL, N_IN), D_MODEL ** -0.5)
    inp['gate_bias'] = nrm((L, N_BRANCH, D_MODEL), 0.1)
    inp['conv_a'] = nrm((L, 3, W_A), 3 ** -0.5)
    inp['w_out_a'] = nrm((L, W_A, D_MODEL), W_A ** -0.5)
    inp['s5_lambda_re'] = -0.5 + nrm((L, 2, G, P), 0.01)
    inp['s5_lambda_im'] = math.pi * jnp.arange(P, dtype=F32) + nrm((L, 2, G, P), 0.01)
    inp['s5_log_step'] = jax.random.uniform(nxt(), (L, 2, G), F32, math.log(1e-3), math.log(1e-1))
    inp['s5_b_re'] = nrm((L, 2, G, P, S5_GROUP), (2 * S5_GROUP) ** -0.5)
    inp['s5_b_im'] = nrm((L, 2, G, P, S5_GROUP), (2 * S5_GROUP) ** -0.5)
    inp['s5_c_re'] = nrm((L, 2, G, S5_GROUP, P), (2 * P) ** -0.5)
    inp['s5_c_im'] = nrm((L, 2, G, S5_GROUP, P), (2 * P) ** -0.5)
    inp['s5_d'] = nrm((L, W_S), 1.0)
    inp['s5_w_glu'] = nrm((L, W_S, 2 * D_MODEL), W_S ** -0.5)
    inp['mla_q_norm'] = gain((L, Q_LORA))
    inp['mla_w_q_b'] = nrm((L, Q_LORA, MLA_HEADS * (QK_NOPE + QK_ROPE)), Q_LORA ** -0.5)
    inp['mla_kv_norm'] = gain((L, KV_LORA))
    inp['mla_w_kv_b'] = nrm((L, KV_LORA, MLA_HEADS * (QK_NOPE + V_DIM)), KV_LORA ** -0.5)
    inp['mla_w_o'] = nrm((L, MLA_HEADS * V_DIM, D_MODEL), (MLA_HEADS * V_DIM) ** -0.5)
    inp['hy_conv'] = nrm((L, 3, 3 * W_H), 3 ** -0.5)
    inp['hy_f_w1'] = nrm((L, HY_EMB, HY_FO), HY_EMB ** -0.5)
    inp['hy_f_b1'] = nrm((L, HY_FO), 0.1)
    inp['hy_f_w2'] = nrm((L, HY_FO, HY_FO), HY_FO ** -0.5)
    inp['hy_f_b2'] = nrm((L, HY_FO), 0.1)
    inp['hy_f_w3'] = nrm((L, HY_FO, HY_ORDER * 2 * W_H), HY_FO ** -0.5)
    inp['hy_f_freq'] = gain((L, HY_FO))
    inp['hy_bias'] = nrm((L, HY_ORDER, W_H), 0.5)
    inp['hy_w_out'] = nrm((L, W_H, D_MODEL), W_H ** -0.5)
    inp['w_mix_out'] = nrm((L, D_MODEL, D_MODEL), D_MODEL ** -0.5)
    inp['xa_norm'] = gain((L, D_MODEL))
    inp['mem_norm'] = gain((D_MODEL,))
    inp['xa_w_q'] = nrm((L, D_MODEL, XA_HEADS * XA_DH), D_MODEL ** -0.5)
    inp['xa_w_kv'] = nrm((L, D_MODEL, 2 * XA_HEADS * XA_DH), D_MODEL ** -0.5)
    inp['xa_w_o'] = nrm((L, XA_HEADS * XA_DH, D_MODEL), (XA_HEADS * XA_DH) ** -0.5)
    inp['moe_norm'] = gain((L, D_MODEL))
    inp['moe_w_group'] = nrm((L, D_MODEL, N_GROUPS), D_MODEL ** -0.5)
    inp['moe_b_group'] = nrm((L, N_GROUPS), 0.01)
    inp['moe_w_expert'] = nrm((L, D_MODEL, N_EXPERTS), D_MODEL ** -0.5)
    inp['moe_b_expert'] = nrm((L, N_EXPERTS), 0.01)
    inp['moe_w_gate'] = nrm((L, N_EXPERTS, D_MODEL, D_FF_E), D_MODEL ** -0.5)
    inp['moe_w_up'] = nrm((L, N_EXPERTS, D_MODEL, D_FF_E), D_MODEL ** -0.5)
    inp['moe_w_down'] = nrm((L, N_EXPERTS, D_FF_E, D_MODEL), D_FF_E ** -0.5)
    inp['final_norm'] = gain((D_MODEL,))
    return inp

def reference(x, mem, positions, mix_norm, w_in, gate_bias, conv_a, w_out_a,
              s5_lambda_re, s5_lambda_im, s5_log_step, s5_b_re, s5_b_im, s5_c_re, s5_c_im, s5_d, s5_w_glu,
              mla_q_norm, mla_w_q_b, mla_kv_norm, mla_w_kv_b, mla_w_o,
              hy_conv, hy_f_w1, hy_f_b1, hy_f_w2, hy_f_b2, hy_f_w3, hy_f_freq, hy_bias, hy_w_out,
              w_mix_out, xa_norm, mem_norm, xa_w_q, xa_w_kv, xa_w_o,
              moe_norm, moe_w_group, moe_b_group, moe_w_expert, moe_b_expert, moe_w_gate, moe_w_up, moe_w_down,
              final_norm):
    inv_freq = 1.0 / (ROPE_BASE ** (jnp.arange(0, QK_ROPE, 2, dtype=F32) / QK_ROPE))
    ang = positions.astype(F32)[..., None] * inv_freq
    cos = jnp.cos(ang).astype(x.dtype)
    sin = jnp.sin(ang).astype(x.dtype)
    mem_n = rmsnorm(mem, mem_norm)
    for l in range(DEPTH):
        h = rmsnorm(x, mix_norm[l])
        p_a, p_s, p_m, p_h, p_g = jnp.split(h @ w_in[l], IN_SPLITS, axis=-1)
        y_a = mixer_short_conv(p_a, conv_a[l], w_out_a[l])
        y_s = mixer_s5(p_s, s5_lambda_re[l], s5_lambda_im[l], s5_log_step[l], s5_b_re[l], s5_b_im[l],
                       s5_c_re[l], s5_c_im[l], s5_d[l], s5_w_glu[l])
        y_m = mixer_mla(p_m, cos, sin, mla_q_norm[l], mla_w_q_b[l], mla_kv_norm[l], mla_w_kv_b[l], mla_w_o[l])
        y_h = mixer_hyena(p_h, hy_conv[l], hy_f_w1[l], hy_f_b1[l], hy_f_w2[l], hy_f_b2[l], hy_f_w3[l],
                          hy_f_freq[l], hy_bias[l], hy_w_out[l])
        gates = jax.nn.sigmoid(p_g.reshape(p_g.shape[:-1] + (N_BRANCH, D_MODEL)) + gate_bias[l])
        merged = (gates[..., 0, :] * y_a + gates[..., 1, :] * y_s
                  + gates[..., 2, :] * y_m + gates[..., 3, :] * y_h)
        x = x + merged @ w_mix_out[l]
        x = x + cross_attention(rmsnorm(x, xa_norm[l]), mem_n, xa_w_q[l], xa_w_kv[l], xa_w_o[l])
        x = x + hier_moe(rmsnorm(x, moe_norm[l]), moe_w_group[l], moe_b_group[l], moe_w_expert[l],
                         moe_b_expert[l], moe_w_gate[l], moe_w_up[l], moe_w_down[l])
    return rmsnorm(x, final_norm)


_drawn_inputs = setup_inputs


def setup_inputs(seed=0):
    import zlib

    import numpy as np

    out = dict(_drawn_inputs(seed))
    spreads = {}
    factors = {'s5_lambda_re': 8.0,
     'mla_q_norm': 8.0,
     'mla_kv_norm': 4.461,
     'xa_norm': 8.0,
     'mem_norm': 8.0,
     'moe_b_group': 8.0,
     'moe_b_expert': 4.158,
     'final_norm': 2.837}
    for name, (base, spread) in spreads.items():
        noise = np.random.default_rng([zlib.crc32(name.encode()), seed]).standard_normal(out[name].shape)
        drawn = base * np.exp(spread * noise) if base else spread * noise
        out[name] = __import__('jax').numpy.asarray(drawn.astype(out[name].dtype))
    for name, factor in factors.items():
        out[name] = (out[name] * factor).astype(out[name].dtype)
    return out
```

```python
import math
from contextlib import ExitStack

import numpy as np
import concourse.bass as bass
from concourse import mybir

F32 = mybir.dt.float32
I32 = mybir.dt.int32
ALU = mybir.AluOpType
ACT = mybir.ActivationFunctionType
X_AXIS = mybir.AxisListType.X

P = 128
EPS = 1e-6
ROUND = 1.5 * 2.0 ** 23
INV_TWO_PI = 1.0 / (2.0 * math.pi)
SIN_SCALE = 6.2831845

DEPTH, D, T = 2, 1024, 256
KT = D // P
TT = T // P
W = 512
WT = W // P
STATE_TILES = 16
ALL_TILES = 2 * STATE_TILES
HEADS, NOPE, ROPE, VD = 8, 64, 32, 64
QK = NOPE + ROPE
LORA = 256
XH, XD = 4, 128
BRANCH = 4
GROUPS, PER_GROUP, FF = 4, 8, 256
EXPERTS = GROUPS * PER_GROUP
HY_EMB, HY_FO, HY_ORDER = 33, 64, 2
NFFT = 2 * T
MLA_SCALE = float(QK) ** -0.5
XA_SCALE = float(XD) ** -0.5

COL_A, COL_S = 0, 3 * W
COL_M = COL_S + W
COL_KR = COL_M + 2 * LORA
COL_H = COL_KR + ROPE
COL_G = COL_H + 3 * W

PAR, PAR_ROWS = {}, 0
for _name, _k in (("mix_norm", KT), ("gate_bias", BRANCH * KT), ("conv_a", 3 * WT), ("s5_d", WT),
                  ("mla_q_norm", 2), ("mla_kv_norm", 2), ("hy_conv", 9 * WT), ("hy_bias", HY_ORDER * WT),
                  ("xa_norm", KT), ("moe_norm", KT)):
    PAR[_name] = PAR_ROWS
    PAR_ROWS += _k
PAR["freq"], PAR["b1"], PAR["b2"] = PAR_ROWS, PAR_ROWS + 1, PAR_ROWS + 2
PAR_ROWS += 3
assert PAR_ROWS <= P

SLOT, RING = 2048, 6
IN_COLS = 256
IN_ORDER = ([("in_s", 0), ("in_a", 0), ("in_s", 1)] + [("in_h", i) for i in range(6)] + [("in_k", 0)]
            + [("in_a", i) for i in range(1, 6)] + [("in_m", i) for i in range(2)] + [("in_g", i) for i in range(16)])
CHUNKS = (IN_ORDER + [("out_a", 0), ("out_a", 1), ("mla_q", 0), ("mla_kv", 0), ("mla_o", 0), ("mla_o", 1),
                      ("filter", 0), ("hy_out", 0), ("hy_out", 1)]
          + [("glu", i) for i in range(4)] + [("mix", i) for i in range(4)]
          + [("xa_q", i) for i in range(2)] + [("xa_kv", i) for i in range(4)] + [("xa_o", i) for i in range(2)])
CHUNK_AT = {c: i for i, c in enumerate(CHUNKS)}
MOE_AT = -(-len(CHUNKS) // RING) * RING
TURN = 2
TURNS = EXPERTS // TURN
assert 3 * TURN == RING


def attention_jobs(name, heads):
    jobs = [(name + "_sc", 0), (name + "_sc", 1)]
    for h in range(heads):
        jobs.append((name + "_tr", h))
        if h + 2 < heads:
            jobs.append((name + "_sc", h + 2))
        jobs.append((name + "_pv", h))
    return jobs


def hyena_jobs(o):
    return ([(f"kf{o}", i) for i in range(4)] + [(f"kn{o}", 0)] + [(f"kd{o}", i) for i in range(5)]
            + [(f"vt{o}", i) for i in range(2)] + [(f"vd{o}", i) for i in range(4)] + [(f"vi{o}", i) for i in range(2)])


JOBS = ([("mix_sum", 0)] + IN_ORDER[:9]
        + [("s5_par", 0)] + [("s5_b", i) for i in range(4)] + [("s5_c", i) for i in range(4)] + IN_ORDER[9:]
        + [("out_a", i) for i in range(4)]
        + [("mla_sum", 0)] + [(n, i) for i in range(4) for n in ("mla_q", "mla_qs")]
        + [("mla_k", i) for i in range(4)] + [("mla_v", i) for i in range(2)]
        + attention_jobs("mla", HEADS) + [("mla_o", i) for i in range(4)]
        + [("filt", 0), ("filt", 1)] + hyena_jobs(0) + hyena_jobs(1) + [("hy_out", i) for i in range(4)]
        + [("glu", i) for i in range(8)] + [("mix", i) for i in range(4)]
        + [("xa_sum", 0), ("xa_q", 0), ("xa_q", 1), ("xa_k", 0), ("xa_k", 1), ("xa_v", 0), ("xa_v", 1)]
        + attention_jobs("xa", XH) + [("xa_o", i) for i in range(4)]
        + [("moe_sum", 0), ("route", 0), ("route_t", 0)] + [("route_b", i) for i in range(EXPERTS // 2)])
JOB_AT = {j: i for i, j in enumerate(JOBS)}
JOB_BANKS, FIRST_JOB_BANK = 4, 4
LAST_USE = {c: c for c in CHUNKS}
for _n in ("out_a", "mla_o", "hy_out", "xa_o"):
    for _i in range(2):
        LAST_USE[(_n, _i)] = (_n, 2 * _i + 1)
LAST_USE[("mla_q", 0)] = ("mla_qs", 3)
LAST_USE[("mla_kv", 0)] = ("mla_v", 1)
LAST_USE[("filter", 0)] = ("kf1", 3)
for _i in range(4):
    LAST_USE[("glu", _i)] = ("glu", 4 * (_i // 2) + 2 + _i % 2)
    LAST_USE[("xa_kv", _i)] = ("xa_v", 1)
TILE_SLOTS = {}
for _i in range(ALL_TILES):
    TILE_SLOTS.setdefault(IN_ORDER[9 + _i * 24 // ALL_TILES], []).append(_i)


class Signal:

    def __init__(self, sem, per_layer, unit=1, base=0):
        self.sem, self.per_layer, self.unit, self.base, self.count = sem, per_layer, unit, base, 0

    def __call__(self, l, n):
        return self.sem, l * (self.per_layer * self.unit) + (self.base + n * self.unit)

    def rise(self):
        self.count += 1
        return self.sem, self.unit

    def last(self, l):
        return self(l, self.count)


SCALAR = dict(root=4, s5_exp=2, s5_sin=2, s5_col=1, s5_bT=4, s5_cT=4, u=4, ph=6, kraw=1, pa=6, latent=2,
              gate_raw=32, gate=4, wave=32, qcopy=4, knope=4, v=4, exp=24, probT=12, o=12, filt=2, k_root=2,
              k_dft=8, seq=4, gelu=1, glu=4, xa_qk=4, rexp=2, comb=1, cw=16, silu=2 * EXPERTS)
VECTOR = dict(par=2, square=4, h=3 * KT, s5_arg=2, s5_rows=1, s5_b=1, s5_c=4, phase=32, bu_used=32, xs=32, y=8,
              merge=16, lat=4, rope_q=4, k=1, max=12, p=24, filt=2, k_fb=8, k_sq=2, k_sd=4,
              spec=8, z=4, x=12, rmax=1, r12=1, comb=1, spread=16, hid=2 * EXPERTS)
VECTOR_STEPS, POOL_STEPS = 520, 80
POOL = dict(a=1, hyena=1)


def encoder(nc, a, out):
    with ExitStack() as ctx:
        def sb(name, shape, dt=F32):
            return ctx.enter_context(nc.sbuf_tensor(name, shape, dt))

        def semaphore(name):
            return ctx.enter_context(nc.semaphore(name))

        def signal(name, per_layer, unit=1, base=0):
            return Signal(semaphore(name), per_layer, unit, base)

        ring = sb("ring", [P, RING, SLOT])
        xT = sb("xT", [P, KT, T])
        memT = sb("memT", [P, KT, T])
        hT = sb("hT", [P, KT, T])
        gates = sb("gates", [P, BRANCH * KT * T])
        phyena = sb("phyena", [P, 3 * WT, T + 2])
        pa = sb("pa", [P, 2 * WT * T + WT * (T + 2)])
        u_fwd = sb("u_fwd", [P, WT, T])
        u_bwd = sb("u_bwd", [P, WT, T])
        latent = sb("latent", [P, 4, T])
        krope_raw = sb("krope_raw", [P, 2, T])
        waves_r = sb("waves_r", [P, 2, T])
        rope_t = sb("rope_t", [P, 2, 2, T])
        arena = sb("arena", [P, 8192])
        rstd = sb("rstd", [P, 2, T])
        ident = sb("ident", [P, P])
        swap = sb("swap", [QK, ROPE])
        ones = sb("ones", [P, P])
        zeros = sb("zeros", [P, P])
        dft = sb("dft", [P, TT, NFFT])
        idft = sb("idft", [P, 4, T])
        decay = sb("decay", [P, TT, W])
        clock = sb("clock", [P, T])
        small = sb("small", [P, 20])
        par_all = sb("par_all", [P, DEPTH, P])
        par = sb("par", [P, P])
        ends = sb("ends", [P, 2 * KT])
        filter_w = sb("filter_w", [HY_FO, 3, HY_FO])
        s5_all = sb("s5_all", [ALL_TILES, DEPTH, 2 * P + 2])
        s5_col = sb("s5_col", [P, 4, ALL_TILES])
        route_w = sb("route_w", [P, KT, GROUPS + EXPERTS])
        bias = sb("bias", [1, GROUPS + EXPERTS])
        rt = sb("rt", [P, 400])
        stat = sb("stat", [P, 3, HEADS, 2])
        k_scale = sb("k_scale", [P, WT])
        psum = ctx.enter_context(nc.psum_tensor("psum", [P, 8, 512], F32))

        eps = small[:, 0:1]
        half = (small[:, 1:2], small[:, 2:3])
        inv_turns, sin_sign = small[64:96, 3:4], small[64:96, 4:5]
        rank4, rank8 = small[:, 5:9], small[:, 9:17]
        quarter = small[:, 17:18]

        def view(buf, at, *shape):
            v = buf[:, at:at + int(np.prod(shape))]
            names = "abcd"[:len(shape)]
            if len(shape) == 1:
                return v
            return v.rearrange(f"p ({' '.join(names)}) -> p {' '.join(names)}",
                               **{n: s for n, s in zip(names, shape)})

        gate = view(gates, 0, BRANCH * KT, T)
        p_b, p_c, xin = view(pa, 0, WT, T), view(pa, WT * T, WT, T), view(pa, 2 * WT * T, WT, T + 2)
        positions = krope_raw[64:96, 0, :].bitcast(I32)
        embed, combT = krope_raw[0:HY_EMB, 1, :], krope_raw[0:EXPERTS, 0, :]
        s5_rows = waves_r[0:ALL_TILES].rearrange("p a b -> p (a b)")[:, 0:2 * P + 2]
        s5_w = view(pa, 512, 12, P)[0:ALL_TILES]
        latent_flat = latent[:].rearrange("p a b -> p (a b)")
        par_rows = view(latent_flat, 0, DEPTH, P)
        ends_rows = latent_flat[0:2 * KT, 256:256 + P]
        filter_h = latent[0:HY_FO]
        conv_t = rope_t[:].rearrange("p a b t -> p (a b) t")
        ys = u_fwd
        b_raw = view(gates, 0, 2, ALL_TILES, 16)
        b_blk = view(gates, 1024, 2, ALL_TILES, 2, 16)
        c_raw = view(gates, 3072, 2, 2 * WT, 64)
        c_blk = view(gates, 4096, 2, 2 * WT, 2, 64)
        b_tmp = view(gates, 6144, 2, ALL_TILES, 16)
        bT = view(arena, 0, 4 * WT, P)
        cT = view(arena, 2048, 4 * WT, P)
        wave = view(arena, 4096, 2, 2, T)
        turn_t = view(arena, 5120, 2, T)
        prod = view(arena, 5632, 2, 2, T)
        zst = view(arena, 6656, 2, T)
        xs = view(arena, 7168, 2, 2, T)
        qT = view(arena, 0, HEADS, T)
        kT = view(arena, 2048, HEADS, T)
        v_tok = view(arena, 4096, TT, W)
        prob = view(arena, 5120, 2, TT, T)
        probT = view(arena, 6144, 2, TT, T)
        oT = view(arena, 7168, 4, T)
        k_cos = view(arena, 0, 2, W)
        k_sin = view(arena, 1024, 2, W)
        k_nyq = view(arena, 2048, W)
        k_sd = view(arena, 2560, 2, TT, W)
        seq_tok = view(arena, 4608, TT, W)
        spec = view(arena, 5632, 4, W)
        k_fb = view(pa, 0, 2, TT, W)
        k_sq = view(pa, 2048, TT, W)
        spec_t = view(pa, 2048, 2, W)
        z_hy = u_bwd
        glu_s = view(arena, 0, 2, T)
        mix_t = rope_t[:, 0]
        silu = view(arena, 0, 2, T)
        hid_t = view(arena, 512, 2, T)
        hid = view(arena, 1024, 2, T)
        spread = view(arena, 2048, 2, 2, T)
        merged = hT
        at, r = 0, {}
        for name, n in (("logits", 36), ("gmax", 1), ("gdiff", 4), ("key4", 4), ("m4", 1), ("oh4", 4), ("gsum", 1),
                        ("e4", 32), ("es", 8), ("v1", 1), ("key8", 8), ("m8", 1), ("oh1", 8), ("es2", 8), ("v2", 1),
                        ("oh2", 8), ("ex", 1), ("w1", 1), ("w2", 1), ("c8", 8), ("t8", 8), ("comb", 32)):
            r[name] = view(rt, at, TT, n)
            at += TT * n

        slot_dmas, dmas_upto = [0] * RING, {}
        for i, c in enumerate(CHUNKS):
            slot_dmas[i % RING] += 3 if c[0] == "in_k" else 1
            dmas_upto[c] = slot_dmas[i % RING]
        slot_loaded = [signal(f"slot{s}_loaded", slot_dmas[s] + TURNS, 16) for s in range(RING)]
        consts_loaded, x_loaded, small_loaded = (semaphore("consts_loaded"), semaphore("x_loaded"),
                                                 semaphore("small_loaded"))
        s5_loaded, route_loaded = signal("s5_matrices_loaded", 4, 16), signal("route_loaded", 7, 16)
        cleared = semaphore("cleared")
        start_pe, start_act, start_dve = semaphore("start_product"), semaphore("start_scalar"), semaphore("start_vector")
        end_pe, end_act, end_dve, stored = (semaphore("end_product"), semaphore("end_scalar"),
                                            semaphore("end_vector"), semaphore("stored"))
        product = signal("product", len(JOBS))
        act = {n: signal("scalar_" + n, k, base=2 * (n == "silu")) for n, k in SCALAR.items()}
        vec = {n: signal("vector_" + n, k, base=2 * (n == "hid")) for n, k in VECTOR.items()}
        gps = {n: signal("pool_" + n, k) for n, k in POOL.items()}
        vector_step = signal("vector_step", VECTOR_STEPS)
        pool_step = signal("pool_step", POOL_STEPS)
        s5_bu, s5_y = signal("s5_bu_product", ALL_TILES), signal("s5_y_product", ALL_TILES)
        moe_gate = signal("expert_gate_product", 2 * EXPERTS)
        hid_half = signal("expert_value", 2 * EXPERTS)
        moe_up = signal("expert_up_product", 2 * EXPERTS, base=2 * EXPERTS)
        moe_down = signal("expert_down_product", EXPERTS, base=EXPERTS)

        freed = {}

        def bank(job):
            return psum[:, FIRST_JOB_BANK + JOB_AT[job] % JOB_BANKS, :]

        def bank2(job):
            return bank(job).rearrange("p (a b) -> p a b", a=2)

        def done(l, job):
            return product(l, JOB_AT[job] + 1)

        def reads(job, sig):
            freed.setdefault(job, []).append((sig, sig.count))

        def col(name, i, rows=slice(0, P)):
            return par[rows, PAR[name] + i:PAR[name] + i + 1]

        block = ctx.enter_context(nc.Block())

        @block.sync
        def _(sp):
            def load(l, i):
                (name, n), s = CHUNKS[i], i % RING
                if name == "in_k":
                    w = a["w_in"][l].rearrange("(k p) c -> p k c", p=P)
                    dst = ring[:, s, 0:KT * 2 * ROPE].rearrange("p (k c) -> p k c", k=KT)
                    for d, c0, c in ((0, COL_KR, 32), (32, COL_KR + 16, 16), (48, COL_KR, 16)):
                        sp.dma_start(dst[:, :, d:d + c], w[:, :, c0:c0 + c]).then_inc(*slot_loaded[s].rise())
                    return
                if name[:3] == "in_":
                    first = {"s": COL_S, "h": COL_H, "a": COL_A, "m": COL_M, "g": COL_G}[name[3]]
                    w, c0, k, c = "w_in", first + n * IN_COLS, KT, IN_COLS
                elif name == "filter":
                    sp.dma_start(ring[0:HY_FO, s, :], a["hy_f_w3"][l]).then_inc(*slot_loaded[s].rise())
                    return
                elif name == "glu":
                    w, c0, k, c = "s5_w_glu", (n % 2) * D + (n // 2) * 512, WT, 512
                else:
                    w, k, c = {"out_a": ("w_out_a", WT, 512), "mla_q": ("mla_w_q_b", 2, HEADS * QK),
                               "mla_kv": ("mla_w_kv_b", 2, HEADS * (NOPE + VD)), "mla_o": ("mla_w_o", WT, 512),
                               "hy_out": ("hy_w_out", WT, 512), "mix": ("w_mix_out", KT, 256),
                               "xa_q": ("xa_w_q", KT, 256), "xa_kv": ("xa_w_kv", KT, 256),
                               "xa_o": ("xa_w_o", WT, 512)}[name]
                    c0 = n * c
                sp.dma_start(ring[:, s, 0:k * c].rearrange("p (k c) -> p k c", k=k),
                             a[w][l].rearrange("(k p) c -> p k c", p=P)[:, :, c0:c0 + c]).then_inc(*slot_loaded[s].rise())

            def expert(l, e, s):
                for j, w in enumerate(("moe_w_gate", "moe_w_up")):
                    sp.dma_start(ring[:, s + j, :].rearrange("p (k c) -> p k c", k=KT),
                                 a[w][l][e].rearrange("(k p) c -> p k c", p=P)).then_inc(*slot_loaded[s + j].rise())
                sp.dma_start(ring[:, s + 2, :].rearrange("p (k c) -> p k c", k=2),
                             a["moe_w_down"][l][e].rearrange("(k p) c -> p k c", p=P)).then_inc(*slot_loaded[s + 2].rise())

            with sp.Fori(0, DEPTH) as l:
                sp.wait_ge(moe_down.sem, l * EXPERTS + EXPERTS)
                for i, chunk in enumerate(CHUNKS):
                    if i >= RING:
                        sp.wait_ge(*done(l, LAST_USE[CHUNKS[i - RING]]))
                    load(l, i)
                sp.wait_ge(*done(l, ("xa_o", 3)))
                for j in range(TURN):
                    expert(l, j, 3 * j)
                with sp.Fori(1, TURNS) as t:
                    for j in range(TURN):
                        sp.wait_ge(moe_down.sem, l * EXPERTS + t * TURN + (EXPERTS - TURN + j + 1))
                        expert(l, t * TURN + j, 3 * j)

        @block.gpsimd
        def _(g):
            for t in (par_rows, phyena[:], xin):
                g.memset(t, 0.0).then_inc(cleared, 1)
            for dst, src in ((ident[:], a["c_ident"]), (view(arena, 0, TT, D), a["x"][0].rearrange("(k p) d -> p k d", p=P)),
                             (view(arena, 2048, TT, D), a["mem"][0].rearrange("(k p) d -> p k d", p=P))):
                g.dma_start(dst, src).then_inc(x_loaded, 16)
            for dst, src in ((small[:], a["c_small"]), (swap[:], a["c_swap"]), (clock[:], a["c_clock"]),
                             (dft[:], a["c_dft"]), (idft[:], a["c_idft"]), (decay[:], a["c_decay"]),
                             (embed, a["c_embed"]), (positions, a["positions"].partition_broadcast(ROPE)),
                             (ends_rows[0:KT], a["mem_norm"].rearrange("(k p) -> k p", p=P)),
                             (ends_rows[KT:2 * KT], a["final_norm"].rearrange("(k p) -> k p", p=P))):
                g.dma_start(dst, src).then_inc(consts_loaded, 16)
            g.wait_ge(cleared, 3)
            for l in range(DEPTH):
                for name in ("mix_norm", "gate_bias", "conv_a", "s5_d", "mla_q_norm", "mla_kv_norm", "hy_conv",
                             "hy_bias", "xa_norm", "moe_norm"):
                    w = a[name][l]
                    src = w.rearrange("(k p) -> k p", p=P) if len(w.shape) == 1 else w.rearrange("b (k p) -> (b k) p", p=P)
                    g.dma_start(par_rows[PAR[name]:PAR[name] + src.shape[0], l, :], src).then_inc(small_loaded, 16)
                for name, w in (("freq", "hy_f_freq"), ("b1", "hy_f_b1"), ("b2", "hy_f_b2")):
                    g.dma_start(par_rows[PAR[name]:PAR[name] + 1, l, 0:HY_FO], a[w][l:l + 1]).then_inc(small_loaded, 16)
                g.dma_start(s5_all[:, l, 0:P], a["s5_lambda_re"][l].rearrange("d (t g) p -> (d t) (g p)", g=2)).then_inc(small_loaded, 16)
                g.dma_start(s5_all[:, l, P:2 * P], a["s5_lambda_im"][l].rearrange("d (t g) p -> (d t) (g p)", g=2)).then_inc(small_loaded, 16)
                g.dma_start(s5_all[:, l, 2 * P:], a["s5_log_step"][l].rearrange("d (t g) -> (d t) g", g=2)).then_inc(small_loaded, 16)

            with g.Fori(0, DEPTH) as l:
                def step(ins):
                    ins.then_inc(*pool_step.rise())

                def link(ins):
                    ins.then_inc(*pool_step.rise())
                    g.wait_ge(*pool_step.last(l))

                g.wait_ge(*vec["h"](l, KT))
                for ri, w in enumerate(("s5_b_re", "s5_b_im")):
                    g.dma_start(b_raw[:, ri, :, :], a[w][l].rearrange("d (t g) p h -> (g p) (d t) h", g=2)).then_inc(*s5_loaded.rise())
                for ri, w in enumerate(("s5_c_re", "s5_c_im")):
                    g.dma_start(c_raw[:, ri, :, :], a[w][l].rearrange("d (j q) h p -> (q h) (d j) p", q=8)).then_inc(*s5_loaded.rise())

                for dst, src in ((filter_w[0:HY_EMB, 0, :], a["hy_f_w1"][l]), (filter_w[:, 1, :], a["hy_f_w2"][l]),
                                 (filter_w[:, 2, :], a["hy_f_w2"][l]),
                                 (route_w[:, :, 0:GROUPS], a["moe_w_group"][l].rearrange("(k p) c -> p k c", p=P)),
                                 (route_w[:, :, GROUPS:], a["moe_w_expert"][l].rearrange("(k p) c -> p k c", p=P)),
                                 (bias[:, 0:GROUPS], a["moe_b_group"][bass.ds(l, 1)]), (bias[:, GROUPS:], a["moe_b_expert"][bass.ds(l, 1)])):
                    g.dma_start(dst, src).then_inc(*route_loaded.rise())

                def conv(dst, padded, first, name, tiles, then=None):
                    for k in range(3):
                        step(g.tensor_tensor(conv_t[:, k, :], padded[:, first, k:k + T],
                                             col(name, k * tiles + first).to_broadcast([P, T]), ALU.mult))
                    g.wait_ge(*pool_step.last(l))
                    link(g.tensor_tensor(conv_t[:, 0], conv_t[:, 0], conv_t[:, 1], ALU.add))
                    return g.tensor_tensor(dst, conv_t[:, 0], conv_t[:, 2], ALU.add)

                g.wait_ge(*act["ph"](l, 6))
                for i in range(3 * WT):
                    ins = conv(phyena[:, i, 1:T + 1], phyena, i, "hy_conv", 3 * WT)
                    if i < 3 * WT - 1:
                        link(ins)
                    else:
                        ins.then_inc(*gps["hyena"].rise())
                g.wait_ge(*act["pa"](l, 6))
                link(g.tensor_tensor(xin[:, :, 1:T + 1], p_c, xin[:, :, 1:T + 1], ALU.mult))
                for i in range(WT):
                    link(conv(p_c[:, i, :], xin, i, "conv_a", WT))
                g.tensor_tensor(p_b, p_b, p_c, ALU.mult).then_inc(*gps["a"].rise())

        @block.scalar
        def _(sc):
            def evacuate(l, dst, src, job, sig, func=ACT.Identity, last=True, **kw):
                sc.wait_ge(*done(l, job))
                sc.activation(dst, src, func, **kw).then_inc(*sig.rise())
                if last:
                    reads(job, sig)

            for i in range(8):
                sc.wait_ge(start_pe, i + 1)
                t = (xT, memT)[i // 4]
                sc.activation(t[:, 4 * (i % 2):4 * (i % 2) + 4, (i % 4 // 2) * P:(i % 4 // 2 + 1) * P],
                              psum[:, i, :].rearrange("p (k t) -> p k t", k=4), ACT.Identity).then_inc(start_act, 1)
            sc.wait_ge(start_pe, 9)
            sc.activation(par_all[:].rearrange("p l c -> p (l c)"), psum[:, 0, 0:DEPTH * P], ACT.Identity).then_inc(start_act, 1)
            sc.wait_ge(start_pe, 10)
            sc.activation(ends[:], psum[:, 1, 0:2 * KT], ACT.Identity).then_inc(start_act, 1)
            sc.wait_ge(start_pe, 11)
            sc.activation(rstd[:, 0, :], psum[:, 2, 0:T], ACT.Sqrt, bias=eps, scale=1.0 / D).then_inc(start_act, 1)
            sc.wait_ge(start_dve, 3)
            sc.activation(waves_r[64:96], rope_t[64:96, 0], ACT.Sin, scale=SIN_SCALE).then_inc(start_act, 1)
            sc.sem_inc(act["silu"].sem, 2)

            def root(l, job, width, tiles=1):
                evacuate(l, rstd[:, 0:tiles, :], bank(job)[:, 0:tiles * T].rearrange("p (a t) -> p a t", a=tiles),
                         job, act["root"], ACT.Sqrt, bias=eps, scale=1.0 / width)

            def attention(l, name, heads, scale, first, o_of):
                def exps(h):
                    sc.wait_ge(*vec["max"](l, first + h + 1))
                    for q in range(TT):
                        if h >= 2:
                            sc.wait_ge(*done(l, (name + "_tr", h - 2)))
                        evacuate(l, prob[:, h % 2, q, :], bank2((name + "_sc", h))[:, q, :], (name + "_sc", h), act["exp"],
                                 ACT.Exp, last=q == TT - 1, bias=stat[:, 0, h, q:q + 1], scale=scale,
                                 accum_out=stat[:, 1, h, q:q + 1])
                exps(0)
                for h in range(heads):
                    if h + 1 < heads:
                        exps(h + 1)
                    if h >= 2:
                        sc.wait_ge(*done(l, (name + "_pv", h - 2)))
                    evacuate(l, probT[:, h % 2], bank2((name + "_tr", h)), (name + "_tr", h), act["probT"])
                    dst, src = o_of(h, bank((name + "_pv", h)))
                    evacuate(l, dst, src, (name + "_pv", h), act["o"])

            with sc.Fori(0, DEPTH) as l:
                def in_a(n):
                    dst = (p_b, p_c, xin[:, :, 1:T + 1])[n // 2][:, 2 * (n % 2):2 * (n % 2) + 2, :]
                    evacuate(l, dst, bank2(("in_a", n)), ("in_a", n), act["pa"])

                root(l, ("mix_sum", 0), D)
                sc.wait_ge(*vec["par"](l, 2))
                sc.activation(s5_w[:, 0, 0:2], s5_rows[:, 2 * P:], ACT.Exp).then_inc(*act["s5_exp"].rise())
                sc.wait_ge(*vec["s5_arg"](l, 1))
                sc.activation(s5_w[:, 3, :], s5_w[:, 1, :], ACT.Exp).then_inc(*act["s5_exp"].rise())
                sc.wait_ge(*vec["s5_arg"](l, 2))
                sc.activation(s5_w[:, 7, :], s5_w[:, 5, :], ACT.Sin, scale=SIN_SCALE).then_inc(*act["s5_sin"].rise())
                sc.activation(s5_w[:, 8, :], s5_w[:, 6, :], ACT.Sin, scale=SIN_SCALE).then_inc(*act["s5_sin"].rise())
                for i in range(2):
                    job = ("in_s", i)
                    if i:
                        in_a(0)
                    evacuate(l, u_fwd[:, 2 * i:2 * i + 2, :], bank2(job), job, act["u"], last=False)
                    evacuate(l, u_bwd[:, 2 * i:2 * i + 2, :], bank2(job)[:, :, ::-1], job, act["u"])
                for i in range(6):
                    evacuate(l, phyena[:, 2 * i:2 * i + 2, 1:T + 1], bank2(("in_h", i)), ("in_h", i), act["ph"])
                evacuate(l, s5_col[:], bank(("s5_par", 0))[:, 0:P].rearrange("p (a b) -> p a b", a=4), ("s5_par", 0), act["s5_col"])
                for i in range(4):
                    evacuate(l, bT[:, 4 * i:4 * i + 4, :], bank(("s5_b", i)).rearrange("p (a b) -> p a b", a=4), ("s5_b", i), act["s5_bT"])
                for i in range(4):
                    evacuate(l, cT[:, 4 * i:4 * i + 4, :], bank(("s5_c", i)).rearrange("p (a b) -> p a b", a=4), ("s5_c", i), act["s5_cT"])

                def waves(i):
                    sc.wait_ge(*vec["phase"](l, i + 1))
                    sc.activation(wave[:, i % 2], wave[:, i % 2], ACT.Sin, scale=SIN_SCALE).then_inc(*act["wave"].rise())

                waves(0)
                for job in IN_ORDER[9:]:
                    name, n = job
                    if name == "in_k":
                        evacuate(l, krope_raw[64:96], bank2(job)[64:96], job, act["kraw"])
                    elif name == "in_a":
                        in_a(n)
                    elif name == "in_m":
                        evacuate(l, latent[:, 2 * n:2 * n + 2, :], bank2(job), job, act["latent"])
                    else:
                        for j in range(2):
                            evacuate(l, gate[:, 2 * n + j, :], bank2(job)[:, j, :], job, act["gate_raw"], last=j == 1,
                                     bias=col("gate_bias", 2 * n + j))
                    for i in TILE_SLOTS.get(job, []):
                        if i + 1 < ALL_TILES:
                            waves(i + 1)
                sc.wait_ge(*act["gate_raw"].last(l))
                for b in range(BRANCH):
                    g = gate[:, b * KT:(b + 1) * KT, :]
                    sc.activation(g, g, ACT.Sigmoid).then_inc(*act["gate"].rise())

                root(l, ("mla_sum", 0), LORA, tiles=2)
                for i in range(4):
                    evacuate(l, qT[0:QK, 2 * i:2 * i + 2, :], bank2(("mla_q", i))[0:QK], ("mla_q", i), act["qcopy"])
                for i in range(4):
                    evacuate(l, kT[0:NOPE, 2 * i:2 * i + 2, :], bank2(("mla_k", i))[0:NOPE], ("mla_k", i), act["knope"])
                for i in range(TT):
                    evacuate(l, v_tok[:, i, :], bank(("mla_v", i)), ("mla_v", i), act["v"])

                def o_mla(h, b):
                    rows = slice(VD * (h % 2), VD * (h % 2) + VD)
                    return oT[rows, h // 2, :], b[rows, 0:T]

                attention(l, "mla", HEADS, MLA_SCALE, 0, o_mla)

                for i in range(2):
                    sc.wait_ge(*vec["filt"](l, i + 1))
                    sc.activation(filter_h[:, i, :], filter_h[:, 2, :], ACT.Sin, scale=SIN_SCALE).then_inc(*act["filt"].rise())
                for o in range(HY_ORDER):
                    evacuate(l, k_scale[:], bank((f"kn{o}", 0))[:, 0:WT], (f"kn{o}", 0), act["k_root"], ACT.Sqrt, bias=eps)
                    for i, dst in enumerate((k_cos[:, 0], k_cos[:, 1], k_sin[:, 0], k_sin[:, 1])):
                        evacuate(l, dst, bank((f"kd{o}", i)), (f"kd{o}", i), act["k_dft"])
                    for i in range(TT):
                        evacuate(l, seq_tok[:, i, :], bank((f"vt{o}", i)), (f"vt{o}", i), act["seq"])

                sc.wait_ge(*vec["y"](l, 8))
                sc.activation(ys[:], ys[:], ACT.Gelu_apprx_tanh).then_inc(*act["gelu"].rise())
                for i in range(4):
                    if i >= 1:
                        sc.wait_ge(*vec["merge"](l, 12 + i))
                    evacuate(l, glu_s[:], bank2(("glu", 2 * i + 1)), ("glu", 2 * i + 1), act["glu"], ACT.Sigmoid)

                root(l, ("xa_sum", 0), D)
                for n in range(2):
                    evacuate(l, qT[:, 2 * n:2 * n + 2, :], bank2(("xa_q", n)), ("xa_q", n), act["xa_qk"])
                for n in range(2):
                    evacuate(l, kT[:, 2 * n:2 * n + 2, :], bank2(("xa_k", n)), ("xa_k", n), act["xa_qk"])
                for i in range(TT):
                    evacuate(l, v_tok[:, i, :], bank(("xa_v", i)), ("xa_v", i), act["v"])
                attention(l, "xa", XH, XA_SCALE, HEADS, lambda h, b: (oT[:, h, :], b[:, 0:T]))

                root(l, ("moe_sum", 0), D)
                sc.wait_ge(*vec["rmax"](l, 1))
                sc.activation(r["gdiff"], r["gdiff"], ACT.Exp).then_inc(*act["rexp"].rise())
                sc.wait_ge(*vec["r12"](l, 1))
                sc.activation(r["ex"], r["ex"], ACT.Exp).then_inc(*act["rexp"].rise())
                evacuate(l, combT, bank(("route_t", 0))[0:EXPERTS, 0:T], ("route_t", 0), act["comb"])
                for i in range(EXPERTS // 2):
                    evacuate(l, gate[:, 2 * i:2 * i + 2, :], bank2(("route_b", i)), ("route_b", i), act["cw"])
                with sc.Fori(0, TURNS) as t:
                    for j in range(TURN):
                        for f in range(2):
                            n = 2 * j + f
                            sc.wait_ge(moe_gate.sem, l * (2 * EXPERTS) + t * (2 * TURN) + (n + 1))
                            sc.wait_ge(vec["hid"].sem, l * (2 * EXPERTS) + t * (2 * TURN) + (n + 1))
                            sc.activation(silu[:, f, :], psum[:, 2 * f, 0:T], ACT.Silu).then_inc(act["silu"].sem, 1)

            sc.wait_ge(end_pe, 1)
            sc.activation(rstd[:, 0, :], psum[:, 4, 0:T], ACT.Sqrt, bias=eps, scale=1.0 / D).then_inc(end_act, 1)
            o_tok = view(arena, 0, TT, D)
            for i in range(4):
                sc.wait_ge(end_pe, 2 + i)
                sc.activation(o_tok[:, i // 2, (i % 2) * 512:(i % 2 + 1) * 512], psum[:, i, :], ACT.Identity).then_inc(end_act, 1)
                if i % 2:
                    sc.wait_ge(end_act, 2 + i)
                    sc.dma_start(out[0].rearrange("(k p) d -> p k d", p=P)[:, i // 2, :], o_tok[:, i // 2, :]).then_inc(stored, 16)
            sc.wait_ge(stored, 32)

        @block.vector
        def _(v):
            chain = [0]

            def start(ins):
                chain[0] += 1
                ins.then_inc(start_dve, 1)
                v.wait_ge(start_dve, chain[0])

            start(v.memset(ones[:], 1.0))
            start(v.memset(zeros[:], 0.0))
            v.wait_ge(consts_loaded, 10 * 16)
            ang, whole = rope_t[64:96, 0], rope_t[64:96, 1]
            start(v.tensor_copy(ang[:, 1, :], positions))
            start(v.tensor_scalar(ang[:, 1, :], ang[:, 1, :], inv_turns, None, ALU.mult))
            start(v.tensor_scalar(ang[:, 0, :], ang[:, 1, :], 0.25, None, ALU.add))
            start(v.tensor_scalar(whole, ang, ROUND, ROUND, ALU.add, ALU.subtract))
            start(v.tensor_tensor(ang, ang, whole, ALU.subtract))
            v.wait_ge(start_act, 8)
            start(v.tensor_tensor(hT[:], memT[:], memT[:], ALU.mult))
            v.wait_ge(start_act, 11)
            start(v.reciprocal(rstd[:, 0, :], rstd[:, 0, :]))
            for k in range(KT):
                start(v.scalar_tensor_tensor(memT[:, k, :], memT[:, k, :], ends[:, k:k + 1], rstd[:, 0, :],
                                             ALU.mult, ALU.mult))
            v.wait_ge(start_act, 12)
            start(v.tensor_scalar(waves_r[64:96, 1, :], waves_r[64:96, 1, :], sin_sign, None, ALU.mult))
            v.sem_inc(vec["hid"].sem, 2)

            def tile2(ap, n=2):
                return ap.unsqueeze(1).to_broadcast([ap.shape[0], n, ap.shape[-1]])

            with v.Fori(0, DEPTH) as l:
                def step(ins, *jobs):
                    ins.then_inc(*vector_step.rise())
                    for job in jobs:
                        reads(job, vector_step)

                def link(ins, *jobs):
                    step(ins, *jobs)
                    v.wait_ge(*vector_step.last(l))

                def result(name, ins, *jobs, settle=True):
                    ins.then_inc(*vec[name].rise())
                    for job in jobs:
                        reads(job, vec[name])
                    if settle:
                        v.wait_ge(*vec[name].last(l))

                def square_x():
                    result("square", v.tensor_tensor(hT[:], xT[:], xT[:], ALU.mult))

                def norm_x(root_n, gain):
                    v.wait_ge(*act["root"](l, root_n))
                    link(v.reciprocal(rstd[:, 0, :], rstd[:, 0, :]))
                    for k in range(KT):
                        result("h", v.scalar_tensor_tensor(hT[:, k, :], xT[:, k, :], col(gain, k), rstd[:, 0, :],
                                                           ALU.mult, ALU.mult))

                def add_x(job, i):
                    v.wait_ge(*done(l, job))
                    result("x", v.tensor_tensor(xT[:, 2 * i:2 * i + 2, :], xT[:, 2 * i:2 * i + 2, :], bank2(job), ALU.add), job)

                for c in (0, T + 1):
                    step(v.memset(xin[:, :, c:c + 1], 0.0))
                result("par", v.tensor_copy(par[:], par_all[:, bass.ds(l, 1), :].rearrange("p o a -> p (o a)")))
                result("par", v.tensor_copy(s5_rows, s5_all[:, bass.ds(l, 1), :].rearrange("p o a -> p (o a)")))
                v.wait_ge(*vec["par"].last(l))
                square_x()
                norm_x(1, "mix_norm")

                lre, lim = s5_rows[:, 0:P], s5_rows[:, P:2 * P]

                def w(i):
                    return s5_w[:, i, :]

                v.wait_ge(*act["s5_exp"](l, 1))
                for g in range(2):
                    half_g = slice(64 * g, 64 * g + 64)
                    step(v.tensor_scalar(w(2)[:, half_g], lim[:, half_g], s5_w[:, 0, g:g + 1], INV_TWO_PI, ALU.mult, ALU.mult))
                step(v.tensor_scalar(w(1)[:, 0:64], lre[:, 0:64], s5_w[:, 0, 0:1], None, ALU.mult))
                v.wait_ge(*vector_step.last(l))
                result("s5_arg", v.tensor_scalar(w(1)[:, 64:P], lre[:, 64:P], s5_w[:, 0, 1:2], None, ALU.mult))
                link(v.tensor_scalar(w(4), w(2), ROUND, ROUND, ALU.add, ALU.subtract))
                link(v.tensor_tensor(w(5), w(2), w(4), ALU.subtract))
                link(v.tensor_scalar(w(6), w(5), 0.25, None, ALU.add))
                link(v.tensor_scalar(w(4), w(6), ROUND, ROUND, ALU.add, ALU.subtract))
                result("s5_arg", v.tensor_tensor(w(6), w(6), w(4), ALU.subtract))
                link(v.tensor_tensor(w(11), lre, lre, ALU.mult))
                link(v.tensor_tensor(w(2), lim, lim, ALU.mult))
                link(v.tensor_tensor(w(11), w(11), w(2), ALU.add))
                link(v.reciprocal(w(11), w(11)))
                v.wait_ge(*act["s5_sin"](l, 2))
                link(v.tensor_tensor(w(9), w(3), w(8), ALU.mult))
                link(v.tensor_scalar(w(9), w(9), -1.0, None, ALU.add))
                link(v.tensor_tensor(w(10), w(3), w(7), ALU.mult))
                link(v.tensor_tensor(w(2), w(9), lre, ALU.mult))
                link(v.tensor_tensor(w(4), w(10), lim, ALU.mult))
                link(v.tensor_tensor(w(2), w(2), w(4), ALU.add))
                link(v.tensor_tensor(w(2), w(2), w(11), ALU.mult))
                link(v.tensor_tensor(w(4), w(10), lre, ALU.mult))
                link(v.tensor_tensor(w(1), w(9), lim, ALU.mult))
                link(v.tensor_tensor(w(4), w(4), w(1), ALU.subtract))
                result("s5_rows", v.tensor_tensor(w(4), w(4), w(11), ALU.mult))

                link(v.memset(b_blk, 0.0))
                v.wait_ge(*s5_loaded(l, 4))
                v.wait_ge(*act["s5_col"](l, 1))
                cre, cim = (s5_col[:, i, :].unsqueeze(2).to_broadcast([P, ALL_TILES, 16]) for i in (2, 3))
                for ri in range(2):
                    step(v.tensor_tensor(b_tmp[:, 0], b_raw[:, 0], cre if ri == 0 else cim, ALU.mult))
                    link(v.tensor_tensor(b_tmp[:, 1], b_raw[:, 1], cim if ri == 0 else cre, ALU.mult))
                    for g in range(2):
                        rows = slice(64 * g, 64 * g + 64)
                        ins = v.tensor_tensor(b_blk[rows, ri, :, g, :], b_tmp[rows, 0], b_tmp[rows, 1],
                                              ALU.subtract if ri == 0 else ALU.add)
                        if ri == 1 and g == 1:
                            result("s5_b", ins)
                        else:
                            link(ins)
                for ri in range(2):
                    for g in range(2):
                        result("s5_c", v.tensor_scalar(c_blk[:, ri, :, g, :], c_raw[:, ri], half[g], 1.0 - 2.0 * ri, ALU.mult, ALU.mult))

                def phase(i):
                    wv, th = wave[:, i % 2], s5_col[:, 1, i:i + 1]
                    step(v.tensor_scalar(wv[:, 0, :], clock[:], th, None, ALU.mult))
                    link(v.tensor_scalar(wv[:, 1, :], clock[:], th, quarter, ALU.mult, ALU.add))
                    link(v.tensor_scalar(turn_t, wv, ROUND, ROUND, ALU.add, ALU.subtract))
                    result("phase", v.tensor_tensor(wv, wv, turn_t, ALU.subtract))

                def y_of(g):
                    v.wait_ge(*s5_y(l, 4 * g + 4))
                    y = psum[:, 2 + g % 2, 0:T]
                    if g < WT:
                        result("y", v.scalar_tensor_tensor(ys[:, g, :], u_fwd[:, g, :], col("s5_d", g), y, ALU.mult, ALU.add))
                    else:
                        v.wait_ge(*vec["y"](l, g - WT + 1))
                        result("y", v.tensor_tensor(ys[:, g - WT, :], ys[:, g - WT, :], y[:, ::-1], ALU.add))

                v.wait_ge(*act["s5_cT"](l, 4))
                phase(0)
                for i in range(ALL_TILES):
                    if i + 1 < ALL_TILES:
                        phase(i + 1)
                    v.wait_ge(*act["wave"](l, i + 1))
                    v.wait_ge(*s5_bu(l, i + 1))
                    sin, cos = wave[:, i % 2, 0, :], wave[:, i % 2, 1, :]
                    bu = psum[:, i % 2, :].rearrange("p (a b) -> p a b", a=2)
                    step(v.tensor_tensor(prod[:, 0], bu, tile2(cos), ALU.mult))
                    result("bu_used", v.tensor_tensor(prod[:, 1], bu[:, ::-1, :], tile2(sin), ALU.mult))
                    v.wait_ge(*vector_step.last(l))
                    v.wait_ge(*vec["bu_used"].last(l))
                    step(v.tensor_tensor(zst[:, 0], prod[:, 0, 0], prod[:, 1, 0], ALU.add))
                    link(v.tensor_tensor(zst[:, 1], prod[:, 0, 1], prod[:, 1, 1], ALU.subtract))
                    decays = s5_col[:, 0, i:i + 1].to_broadcast([P, T])
                    step(v.tensor_tensor_scan(prod[:, 0, 0], decays, zst[:, 0], 0.0, ALU.mult, ALU.add))
                    link(v.tensor_tensor_scan(prod[:, 0, 1], decays, zst[:, 1], 0.0, ALU.mult, ALU.add))
                    step(v.tensor_tensor(zst, prod[:, 0], tile2(cos), ALU.mult))
                    link(v.tensor_tensor(prod[:, 1], prod[:, 0, ::-1, :], tile2(sin), ALU.mult))
                    if i >= 2:
                        v.wait_ge(*s5_y(l, i - 1))
                    link(v.tensor_tensor(xs[:, i % 2, 0], zst[:, 0], prod[:, 1, 0], ALU.subtract))
                    result("xs", v.tensor_tensor(xs[:, i % 2, 1], zst[:, 1], prod[:, 1, 1], ALU.add))
                    if i % 4 == 1 and i > 4:
                        y_of(i // 4 - 1)
                y_of(7)

                def merge(job, b, i):
                    g = gate[:, b * KT + 2 * i:b * KT + 2 * i + 2, :]
                    m = merged[:, 2 * i:2 * i + 2, :]
                    v.wait_ge(*done(l, job))
                    if b == 0:
                        result("merge", v.tensor_tensor(m, g, bank2(job), ALU.mult), job)
                        return
                    if b == 1:
                        v.wait_ge(*act["glu"](l, i + 1))
                        link(v.tensor_tensor(mix_t, bank2(job), glu_s, ALU.mult), job)
                        link(v.tensor_tensor(mix_t, mix_t, g, ALU.mult))
                    else:
                        link(v.tensor_tensor(mix_t, g, bank2(job), ALU.mult), job)
                    result("merge", v.tensor_tensor(m, m, mix_t, ALU.add))

                v.wait_ge(*act["gate"](l, BRANCH))
                for i in range(4):
                    merge(("out_a", i), 0, i)
                v.wait_ge(*vec["merge"].last(l))

                v.wait_ge(*act["latent"](l, 2))
                result("square", v.tensor_tensor(oT, latent[:], latent[:], ALU.mult))
                v.wait_ge(*act["root"](l, 2))
                link(v.reciprocal(rstd[:], rstd[:]))
                for k in range(4):
                    result("lat", v.scalar_tensor_tensor(latent[:, k, :], latent[:, k, :],
                                                         col(("mla_q_norm", "mla_kv_norm")[k // 2], k % 2),
                                                         rstd[:, k // 2, :], ALU.mult, ALU.mult))
                cos, sin = waves_r[64:96, 0, :], waves_r[64:96, 1, :]
                one, two = rope_t[64:96, 0], rope_t[64:96, 1]
                step(v.tensor_tensor(one[:, 0, :], krope_raw[64:96, 0, :], cos, ALU.mult))
                link(v.tensor_tensor(two[:, 0, :], krope_raw[64:96, 1, :], sin, ALU.mult))
                result("k", v.tensor_tensor(kT[64:96], tile2(one[:, 0, :], HEADS), tile2(two[:, 0, :], HEADS), ALU.add))
                for i in range(4):
                    v.wait_ge(*act["qcopy"](l, i + 1))
                    link(v.tensor_tensor(one, qT[64:96, 2 * i:2 * i + 2, :], tile2(cos), ALU.mult))
                    v.wait_ge(*done(l, ("mla_qs", i)))
                    link(v.tensor_tensor(two, bank2(("mla_qs", i))[64:96], tile2(sin), ALU.mult), ("mla_qs", i))
                    result("rope_q", v.tensor_tensor(qT[64:96, 2 * i:2 * i + 2, :], one, two, ALU.add))

                def attention(name, heads, scale, first):
                    def maxima(h):
                        v.wait_ge(*done(l, (name + "_sc", h)))
                        link(v.tensor_reduce(stat[:, 2, h, :], bank2((name + "_sc", h)), X_AXIS, ALU.max))
                        result("max", v.tensor_scalar(stat[:, 0, h, :], stat[:, 2, h, :], -scale, None, ALU.mult))
                    maxima(0)
                    for h in range(heads):
                        if h + 1 < heads:
                            maxima(h + 1)
                        v.wait_ge(*act["exp"](l, 2 * (first + h) + 2))
                        link(v.reciprocal(stat[:, 1, h, :], stat[:, 1, h, :]))
                        for q in range(TT):
                            result("p", v.tensor_scalar(prob[:, h % 2, q, :], prob[:, h % 2, q, :], stat[:, 1, h, q:q + 1],
                                                        None, ALU.mult))

                attention("mla", HEADS, MLA_SCALE, 0)
                for i in range(4):
                    merge(("mla_o", i), 2, i)
                v.wait_ge(*vec["merge"].last(l))

                for i, b in enumerate(("b1", "b2")):
                    v.wait_ge(*done(l, ("filt", i)))
                    arg, whole = filter_h[:, 2, :], filter_h[:, 3, :]
                    rows = slice(0, HY_FO)
                    link(v.tensor_scalar(arg, bank(("filt", i))[rows, 0:T], col(b, 0, rows), col("freq", 0, rows),
                                         ALU.add, ALU.mult), ("filt", i))
                    link(v.tensor_scalar(arg, arg, INV_TWO_PI, None, ALU.mult))
                    link(v.tensor_scalar(whole, arg, ROUND, ROUND, ALU.add, ALU.subtract))
                    result("filt", v.tensor_tensor(arg, arg, whole, ALU.subtract))
                for o in range(HY_ORDER):
                    for i in range(4):
                        v.wait_ge(*done(l, (f"kf{o}", i)))
                        result("k_fb", v.tensor_tensor(k_fb[:, i // 2, i % 2, :], bank((f"kf{o}", i)), decay[:, i % 2, :],
                                                       ALU.mult), (f"kf{o}", i))
                    v.wait_ge(*vec["k_fb"].last(l))
                    link(v.memset(k_fb[0:1, 1, 0, :], 0.0))
                    step(v.tensor_tensor(k_sq, k_fb[:, 0], k_fb[:, 0], ALU.mult))
                    link(v.tensor_tensor(k_sd[:, 0], k_fb[:, 1], k_fb[:, 1], ALU.mult))
                    result("k_sq", v.tensor_tensor(k_sq, k_sq, k_sd[:, 0], ALU.add))
                    result("k_sd", v.tensor_tensor(k_sd[:, 0], k_fb[:, 0], k_fb[:, 1], ALU.add))
                    result("k_sd", v.tensor_tensor(k_sd[:, 1], k_fb[:, 0], k_fb[:, 1], ALU.subtract))
                    v.wait_ge(*act["k_root"](l, o + 1))
                    link(v.reciprocal(k_scale[:], k_scale[:]))
                    v.wait_ge(*act["k_dft"](l, 4 * o + 4))
                    link(v.tensor_copy(k_nyq, k_cos[:, 0]))
                    v.wait_ge(*done(l, (f"kd{o}", 4)))
                    step(v.tensor_copy(k_nyq[0:1], bank((f"kd{o}", 4))[0:1]), (f"kd{o}", 4))
                    link(v.memset(k_sin[0:1, 0, :], 0.0))
                    for i in range(2):
                        c, s = (f"vd{o}", 2 * i), (f"vd{o}", 2 * i + 1)
                        v.wait_ge(*done(l, s))
                        step(v.tensor_tensor(spec[:, i], bank(c), k_cos[:, i], ALU.mult))
                        step(v.tensor_tensor(spec[:, 2 + i], bank(c), k_sin[:, i], ALU.mult), c)
                        step(v.tensor_tensor(spec_t[:, 0], bank(s), k_sin[:, i], ALU.mult))
                        link(v.tensor_tensor(spec_t[:, 1], bank(s), k_nyq if i == 0 else k_cos[:, 1], ALU.mult), s)
                        result("spec", v.tensor_tensor(spec[:, i], spec[:, i], spec_t[:, 0], ALU.subtract))
                        result("spec", v.tensor_tensor(spec[:, 2 + i], spec[:, 2 + i], spec_t[:, 1], ALU.add))
                    if o == 0:
                        v.wait_ge(*gps["hyena"](l, 1))
                    for i in range(2):
                        job = (f"vi{o}", i)
                        v.wait_ge(*done(l, job))
                        for j in range(2):
                            ch = 2 * i + j
                            u = phyena[:, ch, 1:T + 1] if o == 0 else z_hy[:, ch, :]
                            link(v.tensor_scalar(mix_t[:, j, :], u, col("hy_bias", o * WT + ch), None, ALU.mult))
                            link(v.scalar_tensor_tensor(mix_t[:, j, :], bank2(job)[:, j, :], k_scale[:, ch:ch + 1],
                                                        mix_t[:, j, :], ALU.mult, ALU.add), *([job] * j))
                        xg = phyena[:, WT * (o + 1) + 2 * i:WT * (o + 1) + 2 * i + 2, 1:T + 1]
                        result("z", v.tensor_tensor(z_hy[:, 2 * i:2 * i + 2, :], xg, mix_t, ALU.mult))
                    v.wait_ge(*vec["z"].last(l))
                for i in range(4):
                    merge(("hy_out", i), 3, i)
                v.wait_ge(*vec["merge"].last(l))
                for i in range(4):
                    merge(("glu", 2 * i), 1, i)
                for i in range(4):
                    add_x(("mix", i), i)

                v.wait_ge(*vec["x"].last(l))
                square_x()
                norm_x(3, "xa_norm")
                attention("xa", XH, XA_SCALE, HEADS)
                for i in range(4):
                    add_x(("xa_o", i), i)

                v.wait_ge(*vec["x"].last(l))
                square_x()
                norm_x(4, "moe_norm")

                def spread_over(ap, n):
                    return ap.to_broadcast([P, TT, n])

                def first_best(best, of, key, m, oh, rank, n):
                    link(v.tensor_reduce(best, of, X_AXIS, ALU.max))
                    link(v.tensor_tensor(key, of, spread_over(best, n), ALU.is_equal))
                    link(v.tensor_tensor(key, key, rank.unsqueeze(1).to_broadcast([P, TT, n]), ALU.mult))
                    link(v.tensor_reduce(m, key, X_AXIS, ALU.max))
                    link(v.tensor_tensor(oh, key, spread_over(m, n), ALU.is_equal))

                v.wait_ge(*done(l, ("route", 0)))
                link(v.tensor_copy(r["logits"], bank(("route", 0))[:, 0:P].rearrange("p (t c) -> p t c", t=TT)[:, :, 0:GROUPS + EXPERTS]),
                     ("route", 0))
                gl = r["logits"][:, :, 0:GROUPS]
                el = r["logits"][:, :, GROUPS:]
                first_best(r["gmax"], gl, r["key4"], r["m4"], r["oh4"], rank4, GROUPS)
                result("rmax", v.tensor_tensor(r["gdiff"], gl, spread_over(r["gmax"], GROUPS), ALU.subtract))
                for t in range(TT):
                    e4 = r["e4"][:, t, :].rearrange("p (g e) -> p g e", g=GROUPS)
                    link(v.tensor_tensor(e4, el[:, t, :].rearrange("p (g e) -> p g e", g=GROUPS),
                                         r["oh4"][:, t, :].unsqueeze(2).to_broadcast([P, GROUPS, PER_GROUP]), ALU.mult))
                    link(v.tensor_reduce(r["es"][:, t, :], e4.rearrange("p g e -> p e g"), X_AXIS, ALU.add))
                first_best(r["v1"], r["es"], r["key8"], r["m8"], r["oh1"], rank8, PER_GROUP)
                link(v.scalar_tensor_tensor(r["es2"], r["oh1"], -1e30, r["es"], ALU.mult, ALU.add))
                first_best(r["v2"], r["es2"], r["key8"], r["m8"], r["oh2"], rank8, PER_GROUP)
                result("r12", v.tensor_tensor(r["ex"], r["v2"], r["v1"], ALU.subtract))
                v.wait_ge(*act["rexp"](l, 2))
                link(v.tensor_reduce(r["gsum"], r["gdiff"], X_AXIS, ALU.add))
                link(v.reciprocal(r["gsum"], r["gsum"]))
                link(v.tensor_scalar(r["w1"], r["ex"], 1.0, None, ALU.add))
                link(v.reciprocal(r["w1"], r["w1"]))
                link(v.tensor_tensor(r["w1"], r["w1"], r["gsum"], ALU.mult))
                link(v.tensor_tensor(r["w2"], r["w1"], r["ex"], ALU.mult))
                link(v.tensor_tensor(r["c8"], r["oh1"], spread_over(r["w1"], PER_GROUP), ALU.mult))
                link(v.tensor_tensor(r["t8"], r["oh2"], spread_over(r["w2"], PER_GROUP), ALU.mult))
                link(v.tensor_tensor(r["c8"], r["c8"], r["t8"], ALU.add))
                for t in range(TT):
                    ins = v.tensor_tensor(r["comb"][:, t, :].rearrange("p (g e) -> p g e", g=GROUPS),
                                          r["oh4"][:, t, :].unsqueeze(2).to_broadcast([P, GROUPS, PER_GROUP]),
                                          r["c8"][:, t, :].unsqueeze(1).to_broadcast([P, GROUPS, PER_GROUP]), ALU.mult)
                    if t == 0:
                        link(ins)
                    else:
                        result("comb", ins)
                v.wait_ge(*act["comb"](l, 1))
                for i in range(EXPERTS // 2):
                    if i >= 2:
                        v.wait_ge(*done(l, ("route_b", i - 2)))
                    result("spread", v.tensor_tensor(spread[0:EXPERTS, i % 2], tile2(combT),
                                                     ident[0:EXPERTS, 2 * i:2 * i + 2].unsqueeze(2).to_broadcast([EXPERTS, 2, T]), ALU.mult), settle=False)

                with v.Fori(0, TURNS) as t:
                    for j in range(TURN):
                        for f in range(2):
                            n = 2 * j + f
                            base = l * (2 * EXPERTS) + t * (2 * TURN)
                            v.wait_ge(*act["cw"](l, EXPERTS // 2))
                            v.wait_ge(act["silu"].sem, base + (2 + n + 1))
                            v.wait_ge(moe_up.sem, base + (2 * EXPERTS + n + 1))
                            v.tensor_tensor(hid_t[:, f, :], silu[:, f, :], psum[:, 2 * f + 1, 0:T], ALU.mult).then_inc(hid_half.sem, 1)
                            v.wait_ge(hid_half.sem, base + (n + 1))
                            v.wait_ge(moe_down.sem, l * EXPERTS + t * TURN + (EXPERTS + j))
                            v.tensor_tensor(hid[:, f, :], hid_t[:, f, :],
                                            gate[:, bass.ds(t * TURN + j, 1), :].rearrange("p o t -> p (o t)"), ALU.mult).then_inc(vec["hid"].sem, 1)
                v.wait_ge(moe_down.sem, l * EXPERTS + 2 * EXPERTS)
                for i in range(4):
                    acc = psum[:, 4 + i, :].rearrange("p (a b) -> p a b", a=2)
                    result("x", v.tensor_tensor(xT[:, 2 * i:2 * i + 2, :], xT[:, 2 * i:2 * i + 2, :], acc, ALU.add))
                v.wait_ge(*vec["x"].last(l))

            v.tensor_tensor(hT[:], xT[:], xT[:], ALU.mult).then_inc(end_dve, 1)
            v.wait_ge(end_act, 1)
            v.reciprocal(rstd[:, 0, :], rstd[:, 0, :]).then_inc(end_dve, 1)
            v.wait_ge(end_dve, 2)
            for k in range(KT):
                v.scalar_tensor_tensor(hT[:, k, :], xT[:, k, :], ends[:, KT + k:KT + k + 1], rstd[:, 0, :],
                                       ALU.mult, ALU.mult).then_inc(end_dve, 1)

        @block.tensor
        def _(pe):
            pe.wait_ge(x_loaded, 3 * 16)
            for i in range(8):
                src = view(arena, 2048 * (i // 4), TT, D)
                for k in range(4):
                    c = (4 * (i % 2) + k) * P
                    ins = pe.transpose(psum[:, i, k * P:(k + 1) * P], src[:, i % 4 // 2, c:c + P], ident[:])
                ins.then_inc(start_pe, 1)
            pe.wait_ge(small_loaded, DEPTH * 16 * 16)
            pe.wait_ge(start_act, 1)
            for l in range(DEPTH):
                ins = pe.transpose(psum[:, 0, l * P:(l + 1) * P], par_rows[:, l, :], ident[:])
            ins.then_inc(start_pe, 1)
            pe.wait_ge(consts_loaded, 10 * 16)
            pe.wait_ge(start_act, 2)
            pe.transpose(psum[:, 1, 0:2 * KT], ends_rows, ident[0:2 * KT, 0:2 * KT]).then_inc(start_pe, 1)
            pe.wait_ge(start_act, 3)
            pe.wait_ge(start_dve, 8)
            for k in range(KT):
                ins = pe.matmul(psum[:, 2, 0:T], ones[:], hT[:, k, :], start=k == 0, stop=k == KT - 1)
            ins.then_inc(start_pe, 1)
            pe.sem_inc(moe_up.sem, 2 * EXPERTS)
            pe.sem_inc(moe_down.sem, EXPERTS)

            with pe.Fori(0, DEPTH) as l:
                def begin(job):
                    i = JOB_AT[job]
                    if i >= JOB_BANKS:
                        for sig, n in freed[JOBS[i - JOB_BANKS]]:
                            pe.wait_ge(*sig(l, n))
                    return bank(job)

                def finish(ins):
                    ins.then_inc(*product.rise())

                def chunk(name, n=0):
                    i = CHUNK_AT[(name, n)]
                    pe.wait_ge(*slot_loaded[i % RING](l, dmas_upto[(name, n)]))
                    return ring[:, i % RING, :]

                def split(slot, k, c):
                    return slot[:, 0:k * c].rearrange("p (k c) -> p k c", k=k)

                def project(out, w, rhs, nk, c0, m=P):
                    for k in range(nk):
                        ins = pe.matmul(out, w[:, k, c0:c0 + m], rhs[:, k, :], start=k == 0, stop=k == nk - 1)
                    return ins

                def pair(job, w, rhs, nk, c0):
                    b = begin(job)
                    for j in range(2):
                        ins = project(b[:, j * T:(j + 1) * T], w, rhs, nk, c0 + j * P)
                    finish(ins)

                def total(job, src, groups=1):
                    b = begin(job)
                    nk = src.shape[1] // groups
                    for g in range(groups):
                        for k in range(nk):
                            ins = pe.matmul(b[:, g * T:(g + 1) * T], ones[:], src[:, g * nk + k, :], start=k == 0, stop=k == nk - 1)
                    finish(ins)

                def turn(job, tiles):
                    b = begin(job)
                    for j, t in enumerate(tiles):
                        ins = pe.transpose(b[:, j * P:(j + 1) * P], t, ident[:])
                    finish(ins)

                def s5_in(i):
                    d, j, q = i // STATE_TILES, i % STATE_TILES // 4, i % 4
                    rows = slice(32 * q, 32 * q + 32)
                    if i >= 2:
                        pe.wait_ge(*vec["bu_used"](l, i - 1))
                    u = (u_fwd, u_bwd)[d][rows, j, :]
                    for ri in range(2):
                        ins = pe.matmul(psum[:, i % 2, ri * T:(ri + 1) * T], bT[rows, ri * 2 * WT + d * WT + j, :], u,
                                        start=True, stop=True)
                    ins.then_inc(*s5_bu.rise())

                def s5_out(i):
                    d, j, q = i // STATE_TILES, i % STATE_TILES // 4, i % 4
                    rows = slice(32 * q, 32 * q + 32)
                    if i % 4 == 0 and i >= 8:
                        pe.wait_ge(*vec["y"](l, i // 4 - 1))
                    pe.wait_ge(*vec["xs"](l, i + 1))
                    for ri in range(2):
                        ins = pe.matmul(psum[rows, 2 + i // 4 % 2, 0:T], cT[:, ri * 2 * WT + d * WT + j, rows], xs[:, i % 2, ri, :],
                                        start=ri == 0, stop=ri == 1)
                    ins.then_inc(*s5_y.rise())

                def attention(name, heads, rows, first, vd):
                    def scores(h):
                        b = begin((name + "_sc", h))
                        for q in range(TT):
                            ins = pe.matmul(b[:, q * T:(q + 1) * T], qT[0:rows, h, q * P:(q + 1) * P], kT[0:rows, h, :],
                                            start=True, stop=True)
                        finish(ins)
                    scores(0)
                    scores(1)
                    for h in range(heads):
                        b = begin((name + "_tr", h))
                        pe.wait_ge(*vec["p"](l, 2 * (first + h) + 2))
                        for kt in range(TT):
                            for q in range(TT):
                                ins = pe.transpose(b[:, kt * T + q * P:kt * T + (q + 1) * P],
                                                   prob[:, h % 2, q, kt * P:(kt + 1) * P], ident[:])
                        finish(ins)
                        if h + 2 < heads:
                            scores(h + 2)
                        b = begin((name + "_pv", h))
                        pe.wait_ge(*act["probT"](l, first + h + 1))
                        o = b[vd * h % P:vd * h % P + vd, 0:T]
                        for kt in range(TT):
                            ins = pe.matmul(o, v_tok[:, kt, h * vd:(h + 1) * vd], probT[:, h % 2, kt, :],
                                            start=kt == 0, stop=kt == TT - 1)
                        finish(ins)

                pe.wait_ge(*vec["square"](l, 1))
                total(("mix_sum", 0), hT)
                pe.wait_ge(*vec["h"](l, KT))
                for job in IN_ORDER[:9]:
                    pair(job, split(chunk(*job), KT, IN_COLS), hT, KT, 0)
                b = begin(("s5_par", 0))
                pe.wait_ge(*vec["s5_rows"](l, 1))
                for n, i in enumerate((3, 5, 2, 4)):
                    ins = pe.matmul(b[:, n * ALL_TILES:(n + 1) * ALL_TILES], s5_w[:, i, :], ident[0:ALL_TILES, 0:ALL_TILES],
                                    start=True, stop=True)
                finish(ins)
                pe.wait_ge(*vec["s5_b"](l, 1))
                flat = view(gates, 1024, 4 * WT, P)
                for i in range(4):
                    turn(("s5_b", i), [flat[:, 4 * i + j, :] for j in range(4)])
                pe.wait_ge(*vec["s5_c"](l, 4))
                flat = view(gates, 4096, 4 * WT, P)
                for i in range(4):
                    turn(("s5_c", i), [flat[:, 4 * i + j, :] for j in range(4)])
                pe.wait_ge(*act["u"](l, 4))
                for job in IN_ORDER[9:]:
                    slot = chunk(*job)
                    if job[0] == "in_k":
                        b = begin(job)
                        for j in range(2):
                            ins = project(b[64:96, j * T:(j + 1) * T], split(slot, KT, 2 * ROPE), hT, KT, j * ROPE, ROPE)
                        finish(ins)
                    else:
                        pair(job, split(slot, KT, IN_COLS), hT, KT, 0)
                    for i in TILE_SLOTS.get(job, []):
                        if i == 0:
                            pe.wait_ge(*act["s5_bT"](l, 4))
                            pe.wait_ge(*act["s5_cT"](l, 4))
                        s5_in(i)
                        if i:
                            s5_out(i - 1)
                s5_out(ALL_TILES - 1)

                pe.wait_ge(*gps["a"](l, 1))
                for i in range(4):
                    pair(("out_a", i), split(chunk("out_a", i // 2), WT, 512), p_b, WT, (i % 2) * 256)

                pe.wait_ge(*vec["square"](l, 2))
                total(("mla_sum", 0), oT, groups=2)
                pe.wait_ge(*vec["lat"](l, 4))
                wq, wkv = split(chunk("mla_q"), 2, HEADS * QK), split(chunk("mla_kv"), 2, HEADS * (NOPE + VD))
                c_q, c_kv = latent[:, 0:2, :], latent[:, 2:4, :]
                for i in range(4):
                    b = begin(("mla_q", i))
                    for j in range(2):
                        ins = project(b[0:QK, j * T:(j + 1) * T], wq, c_q, 2, (2 * i + j) * QK, QK)
                    finish(ins)
                    b = begin(("mla_qs", i))
                    pe.wait_ge(*act["qcopy"](l, i + 1))
                    finish(pe.matmul(b[64:96, :], swap[:], qT[0:QK, 2 * i:2 * i + 2, :], start=True, stop=True))
                for i in range(4):
                    b = begin(("mla_k", i))
                    for j in range(2):
                        ins = project(b[0:NOPE, j * T:(j + 1) * T], wkv, c_kv, 2, (2 * i + j) * (NOPE + VD), NOPE)
                    finish(ins)
                for i in range(TT):
                    b = begin(("mla_v", i))
                    for k in range(2):
                        wv = wkv[:, k, :].rearrange("p (h c) -> p h c", h=HEADS)[:, :, NOPE:]
                        ins = pe.matmul(b, c_kv[:, k, i * P:(i + 1) * P], wv, start=k == 0, stop=k == 1)
                    finish(ins)
                pe.wait_ge(*act["knope"](l, 4))
                pe.wait_ge(*act["v"](l, 2))
                pe.wait_ge(*act["qcopy"](l, 4))
                pe.wait_ge(*vec["rope_q"](l, 4))
                attention("mla", HEADS, QK, 0, VD)
                pe.wait_ge(*act["o"](l, HEADS))
                for i in range(4):
                    pair(("mla_o", i), split(chunk("mla_o", i // 2), WT, 512), oT, WT, (i % 2) * 256)

                pe.wait_ge(*route_loaded(l, 7))
                for i in range(2):
                    b = begin(("filt", i))
                    if i == 0:
                        ins = pe.matmul(b[:, 0:T], filter_w[0:HY_EMB, 0:2, :].rearrange("p a b -> p (a b)"), embed, start=True, stop=True)
                    else:
                        pe.wait_ge(*act["filt"](l, 1))
                        ins = pe.matmul(b[:, 0:T], filter_w[:, 1:3, :].rearrange("p a b -> p (a b)"), filter_h[:, 0, :], start=True, stop=True)
                    finish(ins)
                pe.wait_ge(*act["filt"](l, 2))
                w3 = chunk("filter")
                for o in range(HY_ORDER):
                    for i in range(4):
                        b = begin((f"kf{o}", i))
                        c = (2 * o + i // 2) * W
                        finish(pe.matmul(b, filter_h[:, 1, (i % 2) * P:(i % 2 + 1) * P], w3[0:HY_FO, c:c + W], start=True, stop=True))
                    b = begin((f"kn{o}", 0))
                    pe.wait_ge(*vec["k_sq"](l, o + 1))
                    for ch in range(WT):
                        for t in range(TT):
                            ins = pe.matmul(b[:, ch:ch + 1], k_sq[:, t, ch * P:(ch + 1) * P], ones[:, 0:1], start=t == 0, stop=t == TT - 1)
                    finish(ins)
                    pe.wait_ge(*vec["k_sd"](l, 2 * o + 2))
                    for i, (f, sd) in enumerate(((0, 0), (1, 0), (2, 1), (3, 1))):
                        b = begin((f"kd{o}", i))
                        for t in range(TT):
                            ins = pe.matmul(b, dft[:, t, f * P:(f + 1) * P], k_sd[:, sd, t, :], start=t == 0, stop=t == TT - 1)
                        finish(ins)
                    b = begin((f"kd{o}", 4))
                    for t in range(TT):
                        ins = pe.matmul(b[0:1, :], dft[:, t, T:T + 1], k_sd[:, 0, t, :], start=t == 0, stop=t == TT - 1)
                    finish(ins)
                    if o == 0:
                        pe.wait_ge(*gps["hyena"](l, 1))
                    else:
                        pe.wait_ge(*vec["z"](l, 2))
                    for t in range(TT):
                        src = phyena[:, 0:WT, 1:T + 1] if o == 0 else z_hy[:]
                        turn((f"vt{o}", t), [src[:, j, t * P:(t + 1) * P] for j in range(WT)])
                    pe.wait_ge(*act["seq"](l, 2 * o + 2))
                    for i, f in enumerate((0, 2, 1, 3)):
                        b = begin((f"vd{o}", i))
                        for t in range(TT):
                            ins = pe.matmul(b, dft[:, t, f * P:(f + 1) * P], seq_tok[:, t, :], start=t == 0, stop=t == TT - 1)
                        finish(ins)
                    pe.wait_ge(*vec["spec"](l, 4 * o + 4))
                    for i in range(2):
                        b = begin((f"vi{o}", i))
                        for j in range(2):
                            for f in range(4):
                                c = (2 * i + j) * P
                                ins = pe.matmul(b[:, j * T:(j + 1) * T], spec[:, f, c:c + P], idft[:, f, :], start=f == 0, stop=f == 3)
                        finish(ins)
                pe.wait_ge(*vec["z"](l, 4))
                for i in range(4):
                    pair(("hy_out", i), split(chunk("hy_out", i // 2), WT, 512), z_hy, WT, (i % 2) * 256)

                pe.wait_ge(*act["gelu"](l, 1))
                for i in range(4):
                    for g in range(2):
                        pair(("glu", 2 * i + g), split(chunk("glu", 2 * (i // 2) + g), WT, 512), ys, WT, (i % 2) * 256)
                pe.wait_ge(*vec["merge"](l, 16))
                for i in range(4):
                    pair(("mix", i), split(chunk("mix", i), KT, 256), merged, KT, 0)

                pe.wait_ge(*vec["square"](l, 3))
                total(("xa_sum", 0), hT)
                pe.wait_ge(*vec["h"](l, 2 * KT))
                for n in range(2):
                    pair(("xa_q", n), split(chunk("xa_q", n), KT, 256), hT, KT, 0)
                for n in range(2):
                    b = begin(("xa_k", n))
                    for j in range(2):
                        ins = project(b[:, j * T:(j + 1) * T], split(chunk("xa_kv", 2 * n + j), KT, 256), memT, KT, 0)
                    finish(ins)
                for t in range(TT):
                    b = begin(("xa_v", t))
                    for h in range(XH):
                        w = split(chunk("xa_kv", h), KT, 256)
                        for k in range(KT):
                            ins = pe.matmul(b[:, h * XD:(h + 1) * XD], memT[:, k, t * P:(t + 1) * P], w[:, k, XD:], start=k == 0, stop=k == KT - 1)
                    finish(ins)
                pe.wait_ge(*act["xa_qk"](l, 4))
                pe.wait_ge(*act["v"](l, 4))
                attention("xa", XH, XD, HEADS, XD)
                pe.wait_ge(*act["o"](l, HEADS + XH))
                for i in range(4):
                    pair(("xa_o", i), split(chunk("xa_o", i // 2), WT, 512), oT, WT, (i % 2) * 256)

                pe.wait_ge(*vec["square"](l, 4))
                total(("moe_sum", 0), hT)
                pe.wait_ge(*vec["h"](l, 3 * KT))
                b = begin(("route", 0))
                for t in range(TT):
                    o = b[:, 64 * t:64 * t + GROUPS + EXPERTS]
                    for k in range(KT):
                        pe.matmul(o, hT[:, k, t * P:(t + 1) * P], route_w[:, k, :], start=k == 0, stop=False)
                    ins = pe.matmul(o, ones[0:1, :], bias[:], start=False, stop=True)
                finish(ins)
                b = begin(("route_t", 0))
                pe.wait_ge(*vec["comb"](l, 1))
                for t in range(TT):
                    ins = pe.transpose(b[0:EXPERTS, t * P:(t + 1) * P], r["comb"][:, t, :], ident[:])
                finish(ins)
                for i in range(EXPERTS // 2):
                    b = begin(("route_b", i))
                    pe.wait_ge(*vec["spread"](l, i + 1))
                    finish(pe.matmul(b, ones[0:EXPERTS, :], spread[0:EXPERTS, i % 2], start=True, stop=True))

                pe.wait_ge(*act["cw"](l, EXPERTS // 2))
                for i in range(4):
                    pe.matmul(psum[:, 4 + i, :], zeros[:], dft[:, 0, :], start=True, stop=True, skip_group_check=True)
                with pe.Fori(0, TURNS) as t:
                    for j in range(TURN):
                        w = []
                        for s in range(3 * j, 3 * j + 3):
                            pe.wait_ge(slot_loaded[s].sem, l * (16 * slot_loaded[s].per_layer) + t * 16 + 16 * (slot_dmas[s] + 1))
                            w.append(split(ring[:, s, :], (KT, KT, 2)[s % 3], (FF, FF, D)[s % 3]))
                        base = l * (2 * EXPERTS) + t * (2 * TURN)
                        for f in range(2):
                            n = 2 * j + f
                            pe.wait_ge(act["silu"].sem, base + (n + 1))
                            pe.wait_ge(vec["hid"].sem, base + (n + 1))
                            project(psum[:, 2 * f, 0:T], w[0], hT, KT, f * P).then_inc(moe_gate.sem, 1)
                            project(psum[:, 2 * f + 1, 0:T], w[1], hT, KT, f * P).then_inc(moe_up.sem, 1)
                        for f in range(2):
                            pe.wait_ge(vec["hid"].sem, base + (2 + 2 * j + f + 1))
                            for m in range(KT):
                                ins = pe.matmul(psum[:, 4 + m // 2, (m % 2) * T:(m % 2 + 1) * T], w[2][:, f, m * P:(m + 1) * P],
                                                hid[:, f, :], start=False, stop=True, skip_group_check=True)
                        ins.then_inc(moe_down.sem, 1)

            pe.wait_ge(end_dve, 1)
            for k in range(KT):
                ins = pe.matmul(psum[:, 4, 0:T], ones[:], hT[:, k, :], start=k == 0, stop=k == KT - 1)
            ins.then_inc(end_pe, 1)
            pe.wait_ge(end_dve, 2 + KT)
            for i in range(4):
                for k in range(4):
                    ins = pe.transpose(psum[:, i, k * P:(k + 1) * P], hT[:, 4 * (i % 2) + k, (i // 2) * P:(i // 2 + 1) * P], ident[:])
                ins.then_inc(end_pe, 1)

        for sig in [product, vector_step, pool_step, route_loaded, s5_bu, s5_y, s5_loaded, *act.values(), *vec.values(), *gps.values()]:
            if sig.count != sig.per_layer and sig not in (act["silu"], vec["hid"]):
                raise AssertionError(f"{sig.sem} rises {sig.count} times in a layer, not {sig.per_layer}")


_CONSTS = ("c_ident", "c_small", "c_swap", "c_clock", "c_dft", "c_idft", "c_decay", "c_embed")


def constants():
    f8 = np.float64
    t = np.arange(T)
    small = np.zeros((P, 20), np.float32)
    small[:, 0] = EPS
    small[:, 1] = (np.arange(P) // 16) % 2 == 0
    small[:, 2] = (np.arange(P) // 16) % 2 == 1
    inv = 1.0 / (10000.0 ** (np.arange(0, ROPE, 2, dtype=f8) / ROPE))
    small[64:96, 3] = np.tile(inv / (2 * np.pi), 2)
    small[64:80, 4], small[80:96, 4] = -1.0, 1.0
    small[:, 5:9] = np.arange(4, 0, -1)
    small[:, 9:17] = np.arange(8, 0, -1)
    small[:, 17] = 0.25
    f = np.arange(T)
    ang = 2 * np.pi * ((t[:, None] * f[None]) % NFFT) / NFFT
    cos, sin = np.cos(ang), np.sin(ang)
    sin[:, 0] = (-1.0) ** t
    dft = np.concatenate([cos, sin], axis=1)
    weight = np.full(2 * T, 2.0 / NFFT)
    weight[0] = weight[T] = 1.0 / NFFT
    idft = dft.T * weight[:, None]
    t_norm = np.arange(T, dtype=np.float32) / np.float32(T - 1)
    bands = np.linspace(1e-4, (HY_EMB - 1) // 2 - 1, (HY_EMB - 1) // 2)
    a = (2 * np.pi / T) * t[:, None] * bands[None]
    embed = np.concatenate([t_norm[:, None], np.cos(a), -np.sin(a)], axis=-1).T
    deltas = np.abs(np.linspace(math.log(1e-2) / 1.5, math.log(1e-2) / 0.3, W))
    decay = np.exp(-t_norm.astype(f8)[:, None] * deltas)
    out = {"c_ident": np.eye(P), "c_swap": np.roll(np.eye(QK)[:, NOPE:], 0, axis=0)[:, (np.arange(ROPE) + ROPE // 2) % ROPE], "c_small": small, "c_clock": np.tile(t, (P, 1)),
           "c_dft": dft.reshape(TT, P, NFFT).transpose(1, 0, 2), "c_idft": idft.reshape(4, P, T).transpose(1, 0, 2),
           "c_decay": decay.reshape(TT, P, W).transpose(1, 0, 2), "c_embed": embed}
    return {k: np.ascontiguousarray(v.astype(np.float32)) for k, v in out.items()}


def kernel(**inputs):
    import concourse.bacc as _bacc
    from concourse.bass_utils import run_bass_kernel_spmd as _run

    nc = _bacc.Bacc("TRN2", target_bir_lowering=False, num_devices=1)
    arrays, aps = {}, {}
    for name, value in {**inputs, **constants()}.items():
        v = np.ascontiguousarray(value)
        arrays[f"in_{name}"] = v
        aps[name] = nc.dram_tensor(f"in_{name}", v.shape, mybir.dt.from_np(v.dtype), kind="ExternalInput").ap()
    out = nc.dram_tensor("out_0", (1, T, D), F32, kind="ExternalOutput").ap()
    encoder(nc, aps, out)
    r = _run(nc, [arrays], core_ids=[0])
    return r.results[0]["out_0"]
```

```python
import math
from contextlib import ExitStack

import numpy as np
import concourse.bass as bass
from concourse import mybir

F32 = mybir.dt.float32
I32 = mybir.dt.int32
ALU = mybir.AluOpType
ACT = mybir.ActivationFunctionType
X_AXIS = mybir.AxisListType.X

P = 128
EPS = 1e-6
ROUND = 1.5 * 2.0 ** 23
INV_TWO_PI = 1.0 / (2.0 * math.pi)
SIN_SCALE = 6.2831845

DEPTH, D, T = 2, 1024, 256
KT = D // P
TT = T // P
W = 512
WT = W // P
STATE_TILES = 16
ALL_TILES = 2 * STATE_TILES
HEADS, NOPE, ROPE, VD = 8, 64, 32, 64
QK = NOPE + ROPE
LORA = 256
XH, XD = 4, 128
BRANCH = 4
GROUPS, PER_GROUP, FF = 4, 8, 256
EXPERTS = GROUPS * PER_GROUP
HY_EMB, HY_FO, HY_ORDER = 33, 64, 2
NFFT = 2 * T
MLA_SCALE = float(QK) ** -0.5
XA_SCALE = float(XD) ** -0.5

COL_A, COL_S = 0, 3 * W
COL_M = COL_S + W
COL_KR = COL_M + 2 * LORA
COL_H = COL_KR + ROPE
COL_G = COL_H + 3 * W

PAR, PAR_ROWS = {}, 0
for _name, _k in (("mix_norm", KT), ("gate_bias", BRANCH * KT), ("conv_a", 3 * WT), ("s5_d", WT),
                  ("mla_q_norm", 2), ("mla_kv_norm", 2), ("hy_conv", 9 * WT), ("hy_bias", HY_ORDER * WT),
                  ("xa_norm", KT), ("moe_norm", KT)):
    PAR[_name] = PAR_ROWS
    PAR_ROWS += _k
PAR["freq"], PAR["b1"], PAR["b2"] = PAR_ROWS, PAR_ROWS + 1, PAR_ROWS + 2
PAR_ROWS += 3
assert PAR_ROWS <= P

SLOT, RING = 2048, 6
IN_COLS = 256
IN_ORDER = ([("in_s", 0), ("in_a", 0), ("in_s", 1)] + [("in_h", i) for i in range(6)] + [("in_k", 0)]
            + [("in_a", i) for i in range(1, 6)] + [("in_m", i) for i in range(2)] + [("in_g", i) for i in range(16)])
CHUNKS = (IN_ORDER + [("out_a", 0), ("out_a", 1), ("mla_q", 0), ("mla_kv", 0), ("mla_o", 0), ("mla_o", 1),
                      ("filter", 0), ("hy_out", 0), ("hy_out", 1)]
          + [("glu", i) for i in range(4)] + [("mix", i) for i in range(4)]
          + [("xa_q", i) for i in range(2)] + [("xa_kv", i) for i in range(4)] + [("xa_o", i) for i in range(2)])
CHUNK_AT = {c: i for i, c in enumerate(CHUNKS)}
MOE_AT = -(-len(CHUNKS) // RING) * RING
TURN = 2
TURNS = EXPERTS // TURN
CAP = 112
GROUP_TURNS = PER_GROUP // TURN
assert 3 * TURN == RING


def attention_jobs(name, heads):
    jobs = [(name + "_sc", 0), (name + "_sc", 1), (name + "_v", 0), (name + "_v", 1)]
    for h in range(heads):
        jobs.append((name + "_tr", h))
        if h + 2 < heads:
            jobs.append((name + "_sc", h + 2))
        if h:
            jobs.append((name + "_pv", h - 1))
    return jobs + [(name + "_pv", heads - 1)]


def hyena_jobs(o):
    return ([(f"kf{o}", i) for i in range(4)] + [(f"kn{o}", 0)] + [(f"kd{o}", i) for i in range(5)]
            + [(f"vt{o}", i) for i in range(2)] + [(f"vd{o}", i) for i in range(4)] + [(f"vi{o}", i) for i in range(2)])


MLA_QK = [("mla_q", 0), ("mla_q", 1), ("mla_qs", 0), ("mla_q", 2), ("mla_qs", 1), ("mla_q", 3), ("mla_qs", 2),
          ("mla_k", 0), ("mla_qs", 3), ("mla_k", 1), ("mla_k", 2), ("mla_k", 3)]
TILE_HALVES = 44
JOBS = ([("mix_sum", 0)] + IN_ORDER[:6]
        + [("s5_par", 0)] + IN_ORDER[6:9] + [("s5_b", i) for i in range(4)] + [("s5_c", i) for i in range(4)] + IN_ORDER[9:]
        + [("out_a", i) for i in range(4)]
        + [("mla_sum", 0)] + MLA_QK
        + attention_jobs("mla", HEADS) + [("mla_o", i) for i in range(4)]
        + [("filt", 0), ("filt", 1)] + hyena_jobs(0) + hyena_jobs(1) + [("hy_out", i) for i in range(4)]
        + [("glu", i) for i in range(8)] + [("mix", i) for i in range(4)]
        + [("xa_k", 0), ("xa_sum", 0), ("xa_k", 1), ("xa_q", 0), ("xa_q", 1)]
        + attention_jobs("xa", XH) + [("xa_o", i) for i in range(4)]
        + [("moe_sum", 0), ("route", 0)] + [("h_tok", i) for i in range(4)] + [("rank", 0)]
        + [("gather", i) for i in range(KT)] + [("back", i) for i in range(2)] + [("cw", i) for i in range(EXPERTS // 4)])
JOB_AT = {j: i for i, j in enumerate(JOBS)}
JOB_BANKS, FIRST_JOB_BANK = 4, 4
LAST_USE = {c: c for c in CHUNKS}
for _n in ("out_a", "mla_o", "hy_out", "xa_o"):
    for _i in range(2):
        LAST_USE[(_n, _i)] = (_n, 2 * _i + 1)
LAST_USE[("mla_q", 0)] = ("mla_qs", 3)
LAST_USE[("mla_kv", 0)] = ("mla_v", 1)
LAST_USE[("filter", 0)] = ("kf1", 3)
for _i in range(4):
    LAST_USE[("glu", _i)] = ("glu", 4 * (_i // 2) + 2 + _i % 2)
    LAST_USE[("xa_kv", _i)] = ("xa_v", 1)
TILE_SLOTS = {}
for _i in range(ALL_TILES):
    _h = 3 + _i * TILE_HALVES // ALL_TILES
    TILE_SLOTS.setdefault((IN_ORDER[9 + _h // 2], _h % 2), []).append(_i)


class Signal:

    def __init__(self, sem, per_layer, unit=1, base=0):
        self.sem, self.per_layer, self.unit, self.base, self.count = sem, per_layer, unit, base, 0

    def __call__(self, l, n):
        return self.sem, l * (self.per_layer * self.unit) + (self.base + n * self.unit)

    def rise(self):
        self.count += 1
        return self.sem, self.unit

    def last(self, l):
        return self(l, self.count)


SCALAR = dict(root=4, s5_exp=2, s5_sin=2, s5_col=1, s5_bT=4, s5_cT=4, u=4, ph=6, kraw=1, pa=6, latent=2,
              gate_raw=32, gate=4, wave=32, turns=64, qcopy=4, knope=4, v=4, exp=24, probT=12, o=12, filt=2, k_root=2,
              k_dft=8, seq=4, gelu=1, glu=4, xa_qk=4, rexp=2, h_tok=4, gather=KT, back=2, cw=EXPERTS // 4, y_slot=2 * GROUPS, silu=2 * EXPERTS)
VECTOR = dict(par=2, square=13, h=3 * KT, s5_arg=2, s5_rows=1, s5_b=1, s5_c=4, phase=32, bu_used=32, xs=32, y=8,
              merge=16, lat=4, rope_q=4, k=1, max=12, p=24, filt=2, k_fb=8, k_sq=2, k_sd=4,
              spec=8, z=4, x=12, oh=1, pick=8, flag=1, rmax=1, r12=1, comb=1, hid=2 * EXPERTS)
VECTOR_STEPS, POOL_STEPS = 459, 80
POOL = dict(a=1, hyena=1)


def encoder(nc, a, out):
    with ExitStack() as ctx:
        def sb(name, shape, dt=F32):
            return ctx.enter_context(nc.sbuf_tensor(name, shape, dt))

        def semaphore(name):
            return ctx.enter_context(nc.semaphore(name))

        def signal(name, per_layer, unit=1, base=0):
            return Signal(semaphore(name), per_layer, unit, base)

        ring = sb("ring", [P, RING, SLOT])
        xT = sb("xT", [P, KT, T])
        memT = sb("memT", [P, KT, T])
        hT = sb("hT", [P, KT, T])
        gates = sb("gates", [P, BRANCH * KT * T])
        phyena = sb("phyena", [P, 3 * WT, T + 2])
        pa = sb("pa", [P, 2 * WT * T + WT * (T + 2)])
        u_fwd = sb("u_fwd", [P, WT, T])
        u_bwd = sb("u_bwd", [P, WT, T])
        latent = sb("latent", [P, 4, T])
        krope_raw = sb("krope_raw", [P, 2, T])
        waves_r = sb("waves_r", [P, 2, T])
        rope_t = sb("rope_t", [P, 2, 2, T])
        arena = sb("arena", [P, 8192])
        rstd = sb("rstd", [P, 2, T])
        ident = sb("ident", [P, P])
        swap = sb("swap", [QK, ROPE])
        ones = sb("ones", [P, P])
        zeros = sb("zeros", [P, P])
        dft = sb("dft", [P, TT, NFFT])
        idft = sb("idft", [P, 4, T])
        decay = sb("decay", [P, TT, W])
        clock = sb("clock", [P, T])
        small = sb("small", [P, 20])
        par_all = sb("par_all", [P, DEPTH, P])
        par = sb("par", [P, P])
        ends = sb("ends", [P, 2 * KT])
        filter_w = sb("filter_w", [HY_FO, 3, HY_FO])
        s5_all = sb("s5_all", [ALL_TILES, DEPTH, 2 * P + 2])
        s5_col = sb("s5_col", [P, 4, ALL_TILES])
        route_w = sb("route_w", [P, KT, GROUPS + EXPERTS])
        bias = sb("bias", [1, GROUPS + EXPERTS])
        rt = sb("rt", [P, 400])
        stat = sb("stat", [P, 3, HEADS, 2])
        k_scale = sb("k_scale", [P, WT])
        upto = sb("upto", [P, P])
        crowded = sb("crowded", [1, 1], I32)
        psum = ctx.enter_context(nc.psum_tensor("psum", [P, 8, 512], F32))

        eps = small[:, 0:1]
        half = (small[:, 1:2], small[:, 2:3])
        inv_turns, sin_sign = small[64:96, 3:4], small[64:96, 4:5]
        rank4, rank8 = small[:, 5:9], small[:, 9:17]
        quarter = small[:, 17:18]

        def view(buf, at, *shape):
            v = buf[:, at:at + int(np.prod(shape))]
            names = "abcd"[:len(shape)]
            if len(shape) == 1:
                return v
            return v.rearrange(f"p ({' '.join(names)}) -> p {' '.join(names)}",
                               **{n: s for n, s in zip(names, shape)})

        gate = view(gates, 0, BRANCH * KT, T)
        p_b, p_c, xin = view(pa, 0, WT, T), view(pa, WT * T, WT, T), view(pa, 2 * WT * T, WT, T + 2)
        positions = krope_raw[64:96, 0, :].bitcast(I32)
        embed = krope_raw[0:HY_EMB, 1, :]
        s5_rows = waves_r[0:ALL_TILES].rearrange("p a b -> p (a b)")[:, 0:2 * P + 2]
        s5_w = view(pa, 512, 12, P)[0:ALL_TILES]
        latent_flat = latent[:].rearrange("p a b -> p (a b)")
        par_rows = view(latent_flat, 0, DEPTH, P)
        ends_rows = latent_flat[0:2 * KT, 256:256 + P]
        filter_h = latent[0:HY_FO]
        conv_t = rope_t[:].rearrange("p a b t -> p (a b) t")
        ys = u_fwd
        b_raw = view(gates, 0, 2, ALL_TILES, 16)
        b_blk = view(gates, 1024, 2, ALL_TILES, 2, 16)
        c_raw = view(gates, 3072, 2, 2 * WT, 64)
        c_blk = view(gates, 4096, 2, 2 * WT, 2, 64)
        b_tmp = view(gates, 6144, 2, ALL_TILES, 16)
        bT = view(arena, 0, 4 * WT, P)
        cT = view(arena, 2048, 4 * WT, P)
        wave = view(arena, 4096, 2, 2, T)
        turn_t = view(arena, 5120, 2, T)
        prod = view(arena, 5632, 2, 2, T)
        zst = view(arena, 6656, 2, T)
        xs = view(arena, 7168, 2, 2, T)
        qT = view(arena, 0, HEADS, T)
        kT = view(arena, 2048, HEADS, T)
        v_tok = view(arena, 4096, TT, W)
        prob = view(arena, 5120, 2, TT, T)
        probT = view(arena, 6144, 2, TT, T)
        oT = view(arena, 7168, 4, T)
        k_cos = view(arena, 0, 2, W)
        k_sin = view(arena, 1024, 2, W)
        k_nyq = view(arena, 2048, W)
        k_sd = view(arena, 2560, 2, TT, W)
        seq_tok = view(arena, 4608, TT, W)
        spec = view(arena, 5632, 4, W)
        k_fb = view(pa, 0, 2, TT, W)
        k_sq = view(pa, 2048, TT, W)
        spec_t = view(pa, 2048, 2, W)
        z_hy = u_bwd
        glu_s = view(arena, 0, 2, T)
        mix_t = rope_t[:, 0]
        silu = view(arena, 0, 2, T)
        hid_t = view(arena, 512, 2, T)
        hid = view(arena, 1024, 2, T)
        h_tok = view(arena, 0, TT, D)
        pick = view(arena, 2048, TT, GROUPS, CAP)
        hg = view(arena, 3072, KT, GROUPS * CAP)
        back = view(arena, 6656, GROUPS, T)
        y_slot = view(gates, 4096, GROUPS, D)
        cw_slot = view(gates, 0, EXPERTS, CAP)
        merged = hT
        x_sq = view(arena, 5120, KT, T)
        at, r = 0, {}
        for name, n in (("logits", 36), ("gmax", 1), ("gdiff", 4), ("key4", 4), ("m4", 1), ("oh4", 4), ("gsum", 1),
                        ("e4", 32), ("es", 8), ("v1", 1), ("key8", 8), ("m8", 1), ("oh1", 8), ("es2", 8), ("v2", 1),
                        ("oh2", 8), ("ex", 1), ("w1", 1), ("w2", 1), ("c8", 8), ("t8", 8), ("comb", 32), ("rank", 4), ("count", 4)):
            r[name] = view(rt, at, TT, n)
            at += TT * n

        slot_dmas, dmas_upto = [0] * RING, {}
        for i, c in enumerate(CHUNKS):
            slot_dmas[i % RING] += 3 if c[0] == "in_k" else 1
            dmas_upto[c] = slot_dmas[i % RING]
        slot_loaded = [signal(f"slot{s}_loaded", slot_dmas[s] + TURNS, 16) for s in range(RING)]
        consts_loaded, x_loaded, small_loaded = (semaphore("consts_loaded"), semaphore("x_loaded"),
                                                 semaphore("small_loaded"))
        s5_loaded, route_loaded = signal("s5_matrices_loaded", 4, 16), signal("route_loaded", 7, 16)
        cleared = semaphore("cleared")
        start_pe, start_act, start_dve = semaphore("start_product"), semaphore("start_scalar"), semaphore("start_vector")
        end_pe, end_act, end_dve, stored = (semaphore("end_product"), semaphore("end_scalar"),
                                            semaphore("end_vector"), semaphore("stored"))
        product = signal("product", len(JOBS))
        act = {n: signal("scalar_" + n, k, base=2 * (n == "silu")) for n, k in SCALAR.items()}
        vec = {n: signal("vector_" + n, k, base=2 * (n == "hid")) for n, k in VECTOR.items()}
        gps = {n: signal("pool_" + n, k) for n, k in POOL.items()}
        vector_step = signal("vector_step", VECTOR_STEPS)
        pool_step = signal("pool_step", POOL_STEPS)
        s5_bu, s5_y = signal("s5_bu_product", ALL_TILES), signal("s5_y_product", ALL_TILES)
        moe_gate = signal("expert_gate_product", 2 * EXPERTS)
        hid_half = signal("expert_value", 2 * EXPERTS)
        moe_up = signal("expert_up_product", 2 * EXPERTS, base=2 * EXPERTS)
        moe_down = signal("expert_down_product", EXPERTS, base=EXPERTS)
        moe_out = signal("scattered_product", 1)
        dense_cw, dense_cw_out = signal("dense_weight_product", EXPERTS // 2), signal("dense_weight_scalar", EXPERTS // 2)

        freed = {}

        def bank(job):
            return psum[:, FIRST_JOB_BANK + JOB_AT[job] % JOB_BANKS, :]

        def bank2(job):
            return bank(job).rearrange("p (a b) -> p a b", a=2)

        def done(l, job):
            return product(l, JOB_AT[job] + 1)

        def reads(job, sig):
            freed.setdefault(job, []).append((sig, sig.count))

        def col(name, i, rows=slice(0, P)):
            return par[rows, PAR[name] + i:PAR[name] + i + 1]

        block = ctx.enter_context(nc.Block())

        def load_small(eng, l):
            for name in ("mix_norm", "gate_bias", "conv_a", "s5_d", "mla_q_norm", "mla_kv_norm", "hy_conv",
                         "hy_bias", "xa_norm", "moe_norm"):
                w = a[name][l]
                src = w.rearrange("(k p) -> k p", p=P) if len(w.shape) == 1 else w.rearrange("b (k p) -> (b k) p", p=P)
                eng.dma_start(par_rows[PAR[name]:PAR[name] + src.shape[0], l, :], src).then_inc(small_loaded, 16)
            for name, w in (("freq", "hy_f_freq"), ("b1", "hy_f_b1"), ("b2", "hy_f_b2")):
                eng.dma_start(par_rows[PAR[name]:PAR[name] + 1, l, 0:HY_FO], a[w][l:l + 1]).then_inc(small_loaded, 16)
            for c, n, w in ((0, P, a["s5_lambda_re"][l].rearrange("d (t g) p -> (d t) (g p)", g=2)),
                            (P, P, a["s5_lambda_im"][l].rearrange("d (t g) p -> (d t) (g p)", g=2)),
                            (2 * P, 2, a["s5_log_step"][l].rearrange("d (t g) -> (d t) g", g=2))):
                eng.dma_start(s5_all[:, l, c:c + n], w).then_inc(small_loaded, 16)

        @block.sync
        def _(sp):
            def load(l, i):
                (name, n), s = CHUNKS[i], i % RING
                if name == "in_k":
                    w = a["w_in"][l].rearrange("(k p) c -> p k c", p=P)
                    dst = ring[:, s, 0:KT * 2 * ROPE].rearrange("p (k c) -> p k c", k=KT)
                    for d, c0, c in ((0, COL_KR, 32), (32, COL_KR + 16, 16), (48, COL_KR, 16)):
                        sp.dma_start(dst[:, :, d:d + c], w[:, :, c0:c0 + c]).then_inc(*slot_loaded[s].rise())
                    return
                if name[:3] == "in_":
                    first = {"s": COL_S, "h": COL_H, "a": COL_A, "m": COL_M, "g": COL_G}[name[3]]
                    w, c0, k, c = "w_in", first + n * IN_COLS, KT, IN_COLS
                elif name == "filter":
                    sp.dma_start(ring[0:HY_FO, s, :], a["hy_f_w3"][l]).then_inc(*slot_loaded[s].rise())
                    return
                elif name == "glu":
                    w, c0, k, c = "s5_w_glu", (n % 2) * D + (n // 2) * 512, WT, 512
                else:
                    w, k, c = {"out_a": ("w_out_a", WT, 512), "mla_q": ("mla_w_q_b", 2, HEADS * QK),
                               "mla_kv": ("mla_w_kv_b", 2, HEADS * (NOPE + VD)), "mla_o": ("mla_w_o", WT, 512),
                               "hy_out": ("hy_w_out", WT, 512), "mix": ("w_mix_out", KT, 256),
                               "xa_q": ("xa_w_q", KT, 256), "xa_kv": ("xa_w_kv", KT, 256),
                               "xa_o": ("xa_w_o", WT, 512)}[name]
                    c0 = n * c
                sp.dma_start(ring[:, s, 0:k * c].rearrange("p (k c) -> p k c", k=k),
                             a[w][l].rearrange("(k p) c -> p k c", p=P)[:, :, c0:c0 + c]).then_inc(*slot_loaded[s].rise())

            def expert(l, e, s):
                for j, w in enumerate(("moe_w_gate", "moe_w_up")):
                    sp.dma_start(ring[:, s + j, :].rearrange("p (k c) -> p k c", k=KT),
                                 a[w][l][e].rearrange("(k p) c -> p k c", p=P)).then_inc(*slot_loaded[s + j].rise())
                sp.dma_start(ring[:, s + 2, :].rearrange("p (k c) -> p k c", k=2),
                             a["moe_w_down"][l][e].rearrange("(k p) c -> p k c", p=P)).then_inc(*slot_loaded[s + 2].rise())

            for dst, src in ((ident[:], a["c_ident"]), (view(arena, 0, TT, D), a["x"][0].rearrange("(k p) d -> p k d", p=P)),
                             (view(arena, 2048, TT, D), a["mem"][0].rearrange("(k p) d -> p k d", p=P))):
                sp.dma_start(dst, src).then_inc(x_loaded, 16)
            sp.wait_ge(cleared, 3)
            load_small(sp, 1)

            with sp.Fori(0, DEPTH) as l:
                sp.wait_ge(moe_down.sem, l * EXPERTS + EXPERTS)
                for i, chunk in enumerate(CHUNKS):
                    if i >= RING:
                        sp.wait_ge(*done(l, LAST_USE[CHUNKS[i - RING]]))
                    load(l, i)
                sp.wait_ge(*done(l, ("xa_o", 3)))
                for j in range(TURN):
                    expert(l, j, 3 * j)
                with sp.Fori(1, TURNS) as t:
                    for j in range(TURN):
                        sp.wait_ge(moe_down.sem, l * EXPERTS + t * TURN + (EXPERTS - TURN + j + 1))
                        expert(l, t * TURN + j, 3 * j)

        @block.gpsimd
        def _(g):
            for t in (par_rows, phyena[:], xin):
                g.memset(t, 0.0).then_inc(cleared, 1)
            for dst, src in ((small[:], a["c_small"]), (swap[:], a["c_swap"]), (upto[:], a["c_upto"]), (clock[:], a["c_clock"]),
                             (dft[:], a["c_dft"]), (idft[:], a["c_idft"]), (decay[:], a["c_decay"]),
                             (embed, a["c_embed"]), (positions, a["positions"].partition_broadcast(ROPE)),
                             (ends_rows[0:KT], a["mem_norm"].rearrange("(k p) -> k p", p=P)),
                             (ends_rows[KT:2 * KT], a["final_norm"].rearrange("(k p) -> k p", p=P))):
                g.dma_start(dst, src).then_inc(consts_loaded, 16)
            with g.Fori(0, DEPTH) as l:
                def step(ins):
                    ins.then_inc(*pool_step.rise())

                def link(ins):
                    ins.then_inc(*pool_step.rise())
                    g.wait_ge(*pool_step.last(l))

                g.wait_ge(*vec["h"](l, KT))
                for ri, w in enumerate(("s5_b_re", "s5_b_im")):
                    g.dma_start(b_raw[:, ri, :, :], a[w][l].rearrange("d (t g) p h -> (g p) (d t) h", g=2)).then_inc(*s5_loaded.rise())
                for ri, w in enumerate(("s5_c_re", "s5_c_im")):
                    g.dma_start(c_raw[:, ri, :, :], a[w][l].rearrange("d (j q) h p -> (q h) (d j) p", q=8)).then_inc(*s5_loaded.rise())

                for dst, src in ((filter_w[0:HY_EMB, 0, :], a["hy_f_w1"][l]), (filter_w[:, 1, :], a["hy_f_w2"][l]),
                                 (filter_w[:, 2, :], a["hy_f_w2"][l]),
                                 (route_w[:, :, 0:GROUPS], a["moe_w_group"][l].rearrange("(k p) c -> p k c", p=P)),
                                 (route_w[:, :, GROUPS:], a["moe_w_expert"][l].rearrange("(k p) c -> p k c", p=P)),
                                 (bias[:, 0:GROUPS], a["moe_b_group"][bass.ds(l, 1)]), (bias[:, GROUPS:], a["moe_b_expert"][bass.ds(l, 1)])):
                    g.dma_start(dst, src).then_inc(*route_loaded.rise())

                def conv(dst, padded, first, name, tiles, then=None):
                    for k in range(3):
                        step(g.tensor_tensor(conv_t[:, k, :], padded[:, first, k:k + T],
                                             col(name, k * tiles + first).to_broadcast([P, T]), ALU.mult))
                    g.wait_ge(*pool_step.last(l))
                    link(g.tensor_tensor(conv_t[:, 0], conv_t[:, 0], conv_t[:, 1], ALU.add))
                    return g.tensor_tensor(dst, conv_t[:, 0], conv_t[:, 2], ALU.add)

                g.wait_ge(*act["ph"](l, 6))
                for i in range(3 * WT):
                    ins = conv(phyena[:, i, 1:T + 1], phyena, i, "hy_conv", 3 * WT)
                    if i < 3 * WT - 1:
                        link(ins)
                    else:
                        ins.then_inc(*gps["hyena"].rise())
                g.wait_ge(*act["pa"](l, 6))
                link(g.tensor_tensor(xin[:, :, 1:T + 1], p_c, xin[:, :, 1:T + 1], ALU.mult))
                for i in range(WT):
                    link(conv(p_c[:, i, :], xin, i, "conv_a", WT))
                g.tensor_tensor(p_b, p_b, p_c, ALU.mult).then_inc(*gps["a"].rise())

        @block.scalar
        def _(sc):
            def evacuate(l, dst, src, job, sig, func=ACT.Identity, last=True, **kw):
                sc.wait_ge(*done(l, job))
                sc.activation(dst, src, func, **kw).then_inc(*sig.rise())
                if last:
                    reads(job, sig)

            sc.wait_ge(cleared, 3)
            load_small(sc, 0)
            for i in range(8):
                sc.wait_ge(start_pe, i + 1)
                t = (xT, memT)[i // 4]
                sc.activation(t[:, 4 * (i % 2):4 * (i % 2) + 4, (i % 4 // 2) * P:(i % 4 // 2 + 1) * P],
                              psum[:, i, :].rearrange("p (k t) -> p k t", k=4), ACT.Identity).then_inc(start_act, 1)
            sc.wait_ge(start_pe, 9)
            sc.activation(par_all[:].rearrange("p l c -> p (l c)"), psum[:, 0, 0:DEPTH * P], ACT.Identity).then_inc(start_act, 1)
            sc.wait_ge(start_pe, 10)
            sc.activation(ends[:], psum[:, 1, 0:2 * KT], ACT.Identity).then_inc(start_act, 1)
            sc.wait_ge(start_pe, 11)
            sc.activation(rstd[:, 0, :], psum[:, 2, 0:T], ACT.Sqrt, bias=eps, scale=1.0 / D).then_inc(start_act, 1)
            sc.wait_ge(start_dve, 3)
            sc.activation(waves_r[64:96], rope_t[64:96, 0], ACT.Sin, scale=SIN_SCALE).then_inc(start_act, 1)
            sc.sem_inc(act["silu"].sem, 2)

            def root(l, job, width, tiles=1):
                evacuate(l, rstd[:, 0:tiles, :], bank(job)[:, 0:tiles * T].rearrange("p (a t) -> p a t", a=tiles),
                         job, act["root"], ACT.Sqrt, bias=eps, scale=1.0 / width)

            def attention(l, name, heads, scale, first, o_of):
                def exps(h):
                    sc.wait_ge(*vec["max"](l, first + h + 1))
                    for q in range(TT):
                        if h >= 2:
                            sc.wait_ge(*done(l, (name + "_tr", h - 2)))
                        evacuate(l, prob[:, h % 2, q, :], bank2((name + "_sc", h))[:, q, :], (name + "_sc", h), act["exp"],
                                 ACT.Exp, last=q == TT - 1, bias=stat[:, 0, h, q:q + 1], scale=scale,
                                 accum_out=stat[:, 1, h, q:q + 1])
                def output(h):
                    dst, src = o_of(h, bank((name + "_pv", h)))
                    evacuate(l, dst, src, (name + "_pv", h), act["o"])

                exps(0)
                exps(1)
                for i in range(TT):
                    evacuate(l, v_tok[:, i, :], bank((name + "_v", i)), (name + "_v", i), act["v"])
                for h in range(heads):
                    if h >= 2:
                        sc.wait_ge(*done(l, (name + "_pv", h - 2)))
                    evacuate(l, probT[:, h % 2], bank2((name + "_tr", h)), (name + "_tr", h), act["probT"])
                    if h + 2 < heads:
                        exps(h + 2)
                    if h:
                        output(h - 1)
                output(heads - 1)

            with sc.Fori(0, DEPTH) as l:
                def in_a(n):
                    dst = (p_b, p_c, xin[:, :, 1:T + 1])[n // 2][:, 2 * (n % 2):2 * (n % 2) + 2, :]
                    evacuate(l, dst, bank2(("in_a", n)), ("in_a", n), act["pa"])

                root(l, ("mix_sum", 0), D)
                sc.wait_ge(*vec["par"](l, 2))
                sc.activation(s5_w[:, 0, 0:2], s5_rows[:, 2 * P:], ACT.Exp).then_inc(*act["s5_exp"].rise())
                sc.wait_ge(*vec["s5_arg"](l, 1))
                sc.activation(s5_w[:, 3, :], s5_w[:, 1, :], ACT.Exp).then_inc(*act["s5_exp"].rise())
                sc.wait_ge(*vec["s5_arg"](l, 2))
                sc.activation(s5_w[:, 7, :], s5_w[:, 5, :], ACT.Sin, scale=SIN_SCALE).then_inc(*act["s5_sin"].rise())
                sc.activation(s5_w[:, 8, :], s5_w[:, 6, :], ACT.Sin, scale=SIN_SCALE).then_inc(*act["s5_sin"].rise())
                for i in range(2):
                    job = ("in_s", i)
                    if i:
                        in_a(0)
                    evacuate(l, u_fwd[:, 2 * i:2 * i + 2, :], bank2(job), job, act["u"], last=False)
                    evacuate(l, u_bwd[:, 2 * i:2 * i + 2, :], bank2(job)[:, :, ::-1], job, act["u"])
                for i in range(6):
                    if i == 3:
                        evacuate(l, s5_col[:], bank(("s5_par", 0))[:, 0:P].rearrange("p (a b) -> p a b", a=4), ("s5_par", 0), act["s5_col"])
                    evacuate(l, phyena[:, 2 * i:2 * i + 2, 1:T + 1], bank2(("in_h", i)), ("in_h", i), act["ph"])
                for i in range(4):
                    evacuate(l, bT[:, 4 * i:4 * i + 4, :], bank(("s5_b", i)).rearrange("p (a b) -> p a b", a=4), ("s5_b", i), act["s5_bT"])
                for i in range(4):
                    evacuate(l, cT[:, 4 * i:4 * i + 4, :], bank(("s5_c", i)).rearrange("p (a b) -> p a b", a=4), ("s5_c", i), act["s5_cT"])

                def waves(i):
                    if i >= 2:
                        sc.wait_ge(*vec["xs"](l, i - 1))
                    th = s5_col[:, 1, i:i + 1]
                    sc.activation(wave[:, i % 2, 0, :], clock[:], ACT.Identity, scale=th).then_inc(*act["turns"].rise())
                    sc.activation(wave[:, i % 2, 1, :], clock[:], ACT.Identity, bias=quarter, scale=th).then_inc(*act["turns"].rise())
                    sc.wait_ge(*vec["phase"](l, i + 1))
                    sc.activation(wave[:, i % 2], wave[:, i % 2], ACT.Sin, scale=-SIN_SCALE).then_inc(*act["wave"].rise())

                sc.wait_ge(*act["s5_cT"](l, 4))
                waves(0)
                for job in IN_ORDER[9:]:
                    name, n = job
                    for i in TILE_SLOTS.get((job, 0), []) + TILE_SLOTS.get((job, 1), []):
                        if i + 1 < ALL_TILES:
                            waves(i + 1)
                    if name == "in_k":
                        evacuate(l, krope_raw[64:96], bank2(job)[64:96], job, act["kraw"])
                    elif name == "in_a":
                        in_a(n)
                    elif name == "in_m":
                        evacuate(l, latent[:, 2 * n:2 * n + 2, :], bank2(job), job, act["latent"])
                    else:
                        for j in range(2):
                            evacuate(l, gate[:, 2 * n + j, :], bank2(job)[:, j, :], job, act["gate_raw"], last=j == 1,
                                     bias=col("gate_bias", 2 * n + j))
                sc.wait_ge(*act["gate_raw"].last(l))
                for b in range(BRANCH):
                    g = gate[:, b * KT:(b + 1) * KT, :]
                    sc.activation(g, g, ACT.Sigmoid).then_inc(*act["gate"].rise())

                root(l, ("mla_sum", 0), LORA, tiles=2)
                for i in range(4):
                    evacuate(l, qT[0:QK, 2 * i:2 * i + 2, :], bank2(("mla_q", i))[0:QK], ("mla_q", i), act["qcopy"])
                for i in range(4):
                    evacuate(l, kT[0:NOPE, 2 * i:2 * i + 2, :], bank2(("mla_k", i))[0:NOPE], ("mla_k", i), act["knope"])

                def o_mla(h, b):
                    rows = slice(VD * (h % 2), VD * (h % 2) + VD)
                    return oT[rows, h // 2, :], b[rows, 0:T]

                attention(l, "mla", HEADS, MLA_SCALE, 0, o_mla)

                for i in range(2):
                    sc.wait_ge(*vec["filt"](l, i + 1))
                    sc.activation(filter_h[:, i, :], filter_h[:, 2, :], ACT.Sin, scale=SIN_SCALE).then_inc(*act["filt"].rise())
                for o in range(HY_ORDER):
                    evacuate(l, k_scale[:], bank((f"kn{o}", 0))[:, 0:WT], (f"kn{o}", 0), act["k_root"], ACT.Sqrt, bias=eps)
                    for i, dst in enumerate((k_cos[:, 0], k_cos[:, 1], k_sin[:, 0], k_sin[:, 1])):
                        evacuate(l, dst, bank((f"kd{o}", i)), (f"kd{o}", i), act["k_dft"])
                    for i in range(TT):
                        evacuate(l, seq_tok[:, i, :], bank((f"vt{o}", i)), (f"vt{o}", i), act["seq"])

                sc.wait_ge(*vec["y"](l, 8))
                sc.activation(ys[:], ys[:], ACT.Gelu_apprx_tanh).then_inc(*act["gelu"].rise())
                for i in range(4):
                    if i >= 1:
                        sc.wait_ge(*vec["merge"](l, 12 + i))
                    evacuate(l, glu_s[:], bank2(("glu", 2 * i + 1)), ("glu", 2 * i + 1), act["glu"], ACT.Sigmoid)

                def xa_key(n):
                    evacuate(l, kT[:, 2 * n:2 * n + 2, :], bank2(("xa_k", n)), ("xa_k", n), act["xa_qk"])

                xa_key(0)
                root(l, ("xa_sum", 0), D)
                xa_key(1)
                for n in range(2):
                    evacuate(l, qT[:, 2 * n:2 * n + 2, :], bank2(("xa_q", n)), ("xa_q", n), act["xa_qk"])
                attention(l, "xa", XH, XA_SCALE, HEADS, lambda h, b: (oT[:, h, :], b[:, 0:T]))

                root(l, ("moe_sum", 0), D)
                for i in range(4):
                    evacuate(l, h_tok[:, i // 2, (i % 2) * 512:(i % 2 + 1) * 512], bank(("h_tok", i)), ("h_tok", i), act["h_tok"])
                sc.wait_ge(*vec["rmax"](l, 1))
                sc.activation(r["gdiff"], r["gdiff"], ACT.Exp).then_inc(*act["rexp"].rise())
                sc.wait_ge(*vec["r12"](l, 1))
                sc.activation(r["ex"], r["ex"], ACT.Exp).then_inc(*act["rexp"].rise())
                for k in range(KT):
                    evacuate(l, hg[:, k, :], bank(("gather", k))[:, 0:GROUPS * CAP], ("gather", k), act["gather"])
                for i in range(2):
                    evacuate(l, back[0:CAP, 2 * i:2 * i + 2, :], bank2(("back", i))[0:CAP], ("back", i), act["back"])
                for i in range(EXPERTS // 4):
                    evacuate(l, cw_slot[:, 4 * i:4 * i + 4, :], bank(("cw", i))[:, 0:4 * CAP].rearrange("p (a b) -> p a b", a=4),
                             ("cw", i), act["cw"])

                def expert_gates(base, t, width):
                    for j in range(TURN):
                        for f in range(2):
                            n = 2 * j + f
                            sc.wait_ge(moe_gate.sem, l * (2 * EXPERTS) + t * (2 * TURN) + (base + n + 1))
                            sc.wait_ge(vec["hid"].sem, l * (2 * EXPERTS) + t * (2 * TURN) + (base + n + 1))
                            sc.activation(silu[:, f, 0:width], psum[:, 2 * f, 0:width], ACT.Silu).then_inc(act["silu"].sem, 1)

                flag = sc.value_load(crowded[0:1, 0:1], min_val=0, max_val=1)
                with sc.If(flag < 1):
                    sc.sem_inc(dense_cw_out.sem, EXPERTS // 2)
                    for g in range(GROUPS):
                        with sc.Fori(0, GROUP_TURNS) as t:
                            expert_gates(2 * PER_GROUP * g, t, CAP)
                        sc.wait_ge(moe_down.sem, l * EXPERTS + (EXPERTS + PER_GROUP * (g + 1)))
                        for i in range(2):
                            sc.activation(y_slot[0:CAP, g, i * 512:(i + 1) * 512], psum[0:CAP, 4 + i, :],
                                          ACT.Identity).then_inc(*act["y_slot"].rise())
                with sc.Else():
                    sc.sem_inc(act["y_slot"].sem, 2 * GROUPS)
                    for i in range(EXPERTS // 2):
                        sc.wait_ge(*dense_cw(l, i + 1))
                        sc.activation(gate[:, 2 * i:2 * i + 2, :], psum[:, 4 + i % 4, :].rearrange("p (a b) -> p a b", a=2),
                                      ACT.Identity).then_inc(*dense_cw_out.rise())
                    with sc.Fori(0, TURNS) as t:
                        expert_gates(0, t, T)

            sc.wait_ge(end_pe, 1)
            sc.activation(rstd[:, 0, :], psum[:, 4, 0:T], ACT.Sqrt, bias=eps, scale=1.0 / D).then_inc(end_act, 1)
            o_tok = view(arena, 0, TT, D)
            for i in range(4):
                sc.wait_ge(end_pe, 2 + i)
                sc.activation(o_tok[:, i // 2, (i % 2) * 512:(i % 2 + 1) * 512], psum[:, i, :], ACT.Identity).then_inc(end_act, 1)
                if i % 2:
                    sc.wait_ge(end_act, 2 + i)
                    sc.dma_start(out[0].rearrange("(k p) d -> p k d", p=P)[:, i // 2, :], o_tok[:, i // 2, :]).then_inc(stored, 16)
            sc.wait_ge(stored, 32)

        @block.vector
        def _(v):
            chain = [0]

            def start(ins):
                chain[0] += 1
                ins.then_inc(start_dve, 1)
                v.wait_ge(start_dve, chain[0])

            start(v.memset(ones[:], 1.0))
            start(v.memset(zeros[:], 0.0))
            v.wait_ge(consts_loaded, 11 * 16)
            ang, whole = rope_t[64:96, 0], rope_t[64:96, 1]
            start(v.tensor_copy(ang[:, 1, :], positions))
            start(v.tensor_scalar(ang[:, 1, :], ang[:, 1, :], inv_turns, None, ALU.mult))
            start(v.tensor_scalar(ang[:, 0, :], ang[:, 1, :], 0.25, None, ALU.add))
            start(v.tensor_scalar(whole, ang, ROUND, ROUND, ALU.add, ALU.subtract))
            start(v.tensor_tensor(ang, ang, whole, ALU.subtract))
            v.wait_ge(start_act, 8)
            start(v.tensor_tensor(hT[:], memT[:], memT[:], ALU.mult))
            v.wait_ge(start_act, 11)
            start(v.reciprocal(rstd[:, 0, :], rstd[:, 0, :]))
            for k in range(KT):
                start(v.scalar_tensor_tensor(memT[:, k, :], memT[:, k, :], ends[:, k:k + 1], rstd[:, 0, :],
                                             ALU.mult, ALU.mult))
            v.wait_ge(start_act, 12)
            start(v.tensor_scalar(waves_r[64:96, 1, :], waves_r[64:96, 1, :], sin_sign, None, ALU.mult))
            v.sem_inc(vec["hid"].sem, 2)

            def tile2(ap, n=2):
                return ap.unsqueeze(1).to_broadcast([ap.shape[0], n, ap.shape[-1]])

            with v.Fori(0, DEPTH) as l:
                def step(ins, *jobs):
                    ins.then_inc(*vector_step.rise())
                    for job in jobs:
                        reads(job, vector_step)

                def link(ins, *jobs):
                    step(ins, *jobs)
                    v.wait_ge(*vector_step.last(l))

                def result(name, ins, *jobs, settle=True):
                    ins.then_inc(*vec[name].rise())
                    for job in jobs:
                        reads(job, vec[name])
                    if settle:
                        v.wait_ge(*vec[name].last(l))

                def square_x(i):
                    x = xT[:, 2 * i:2 * i + 2, :]
                    result("square", v.tensor_tensor(x_sq[:, 2 * i:2 * i + 2, :], x, x, ALU.mult))

                def norm_x(root_n, gain):
                    v.wait_ge(*act["root"](l, root_n))
                    link(v.reciprocal(rstd[:, 0, :], rstd[:, 0, :]))
                    for k in range(KT):
                        result("h", v.scalar_tensor_tensor(hT[:, k, :], xT[:, k, :], col(gain, k), rstd[:, 0, :],
                                                           ALU.mult, ALU.mult))

                def add_x(job, i):
                    v.wait_ge(*done(l, job))
                    result("x", v.tensor_tensor(xT[:, 2 * i:2 * i + 2, :], xT[:, 2 * i:2 * i + 2, :], bank2(job), ALU.add), job)
                    square_x(i)

                for c in (0, T + 1):
                    step(v.memset(xin[:, :, c:c + 1], 0.0))
                result("par", v.tensor_copy(par[:], par_all[:, bass.ds(l, 1), :].rearrange("p o a -> p (o a)")))
                result("par", v.tensor_copy(s5_rows, s5_all[:, bass.ds(l, 1), :].rearrange("p o a -> p (o a)")))
                for i in range(4):
                    square_x(i)
                norm_x(1, "mix_norm")

                lre, lim = s5_rows[:, 0:P], s5_rows[:, P:2 * P]

                def w(i):
                    return s5_w[:, i, :]

                v.wait_ge(*act["s5_exp"](l, 1))
                for g in range(2):
                    half_g = slice(64 * g, 64 * g + 64)
                    step(v.tensor_scalar(w(2)[:, half_g], lim[:, half_g], s5_w[:, 0, g:g + 1], INV_TWO_PI, ALU.mult, ALU.mult))
                step(v.tensor_scalar(w(1)[:, 0:64], lre[:, 0:64], s5_w[:, 0, 0:1], None, ALU.mult))
                v.wait_ge(*vector_step.last(l))
                result("s5_arg", v.tensor_scalar(w(1)[:, 64:P], lre[:, 64:P], s5_w[:, 0, 1:2], None, ALU.mult))
                link(v.tensor_scalar(w(4), w(2), ROUND, ROUND, ALU.add, ALU.subtract))
                link(v.tensor_tensor(w(5), w(2), w(4), ALU.subtract))
                link(v.tensor_scalar(w(6), w(5), 0.25, None, ALU.add))
                link(v.tensor_scalar(w(4), w(6), ROUND, ROUND, ALU.add, ALU.subtract))
                result("s5_arg", v.tensor_tensor(w(6), w(6), w(4), ALU.subtract))
                link(v.tensor_tensor(w(11), lre, lre, ALU.mult))
                link(v.tensor_tensor(w(2), lim, lim, ALU.mult))
                link(v.tensor_tensor(w(11), w(11), w(2), ALU.add))
                link(v.reciprocal(w(11), w(11)))
                v.wait_ge(*act["s5_sin"](l, 2))
                link(v.tensor_tensor(w(9), w(3), w(8), ALU.mult))
                link(v.tensor_scalar(w(9), w(9), -1.0, None, ALU.add))
                link(v.tensor_tensor(w(10), w(3), w(7), ALU.mult))
                link(v.tensor_tensor(w(2), w(9), lre, ALU.mult))
                link(v.tensor_tensor(w(4), w(10), lim, ALU.mult))
                link(v.tensor_tensor(w(2), w(2), w(4), ALU.add))
                link(v.tensor_tensor(w(2), w(2), w(11), ALU.mult))
                link(v.tensor_tensor(w(4), w(10), lre, ALU.mult))
                link(v.tensor_tensor(w(1), w(9), lim, ALU.mult))
                link(v.tensor_tensor(w(4), w(4), w(1), ALU.subtract))
                result("s5_rows", v.tensor_tensor(w(4), w(4), w(11), ALU.mult))

                link(v.memset(b_blk, 0.0))
                v.wait_ge(*s5_loaded(l, 4))
                v.wait_ge(*act["s5_col"](l, 1))
                cre, cim = (s5_col[:, i, :].unsqueeze(2).to_broadcast([P, ALL_TILES, 16]) for i in (2, 3))
                for ri in range(2):
                    step(v.tensor_tensor(b_tmp[:, 0], b_raw[:, 0], cre if ri == 0 else cim, ALU.mult))
                    link(v.tensor_tensor(b_tmp[:, 1], b_raw[:, 1], cim if ri == 0 else cre, ALU.mult))
                    for g in range(2):
                        rows = slice(64 * g, 64 * g + 64)
                        ins = v.tensor_tensor(b_blk[rows, ri, :, g, :], b_tmp[rows, 0], b_tmp[rows, 1],
                                              ALU.subtract if ri == 0 else ALU.add)
                        if ri == 1 and g == 1:
                            result("s5_b", ins)
                        else:
                            link(ins)
                for ri in range(2):
                    for g in range(2):
                        result("s5_c", v.tensor_scalar(c_blk[:, ri, :, g, :], c_raw[:, ri], half[g], 1.0 - 2.0 * ri, ALU.mult, ALU.mult))

                def near(i):
                    v.wait_ge(*act["turns"](l, 2 * i + 2))
                    step(v.tensor_scalar(turn_t, wave[:, i % 2], ROUND, ROUND, ALU.add, ALU.subtract))

                def phase(i):
                    result("phase", v.tensor_tensor(wave[:, i % 2], turn_t, wave[:, i % 2], ALU.subtract), settle=False)

                def y_of(g):
                    v.wait_ge(*s5_y(l, 4 * g + 4))
                    y = psum[:, 2 + g % 2, 0:T]
                    if g < WT:
                        result("y", v.scalar_tensor_tensor(ys[:, g, :], u_fwd[:, g, :], col("s5_d", g), y, ALU.mult, ALU.add))
                    else:
                        v.wait_ge(*vec["y"](l, g - WT + 1))
                        result("y", v.tensor_tensor(ys[:, g - WT, :], ys[:, g - WT, :], y[:, ::-1], ALU.add))

                near(0)
                v.wait_ge(*vector_step.last(l))
                phase(0)
                for i in range(ALL_TILES):
                    v.wait_ge(*act["wave"](l, i + 1))
                    v.wait_ge(*s5_bu(l, i + 1))
                    sin, cos = wave[:, i % 2, 0, :], wave[:, i % 2, 1, :]
                    bu = psum[:, i % 2, :].rearrange("p (a b) -> p a b", a=2)
                    step(v.tensor_tensor(prod[:, 0], bu, tile2(cos), ALU.mult))
                    result("bu_used", v.tensor_tensor(prod[:, 1], bu[:, ::-1, :], tile2(sin), ALU.mult), settle=False)
                    if i + 1 < ALL_TILES:
                        near(i + 1)
                    v.wait_ge(*vector_step.last(l))
                    v.wait_ge(*vec["bu_used"].last(l))
                    step(v.tensor_tensor(zst[:, 0], prod[:, 0, 0], prod[:, 1, 0], ALU.add))
                    step(v.tensor_tensor(zst[:, 1], prod[:, 0, 1], prod[:, 1, 1], ALU.subtract))
                    if i + 1 < ALL_TILES:
                        phase(i + 1)
                    v.wait_ge(*vector_step.last(l))
                    decays = s5_col[:, 0, i:i + 1].to_broadcast([P, T])
                    step(v.tensor_tensor_scan(prod[:, 0, 0], decays, zst[:, 0], 0.0, ALU.mult, ALU.add))
                    link(v.tensor_tensor_scan(prod[:, 0, 1], decays, zst[:, 1], 0.0, ALU.mult, ALU.add))
                    step(v.tensor_tensor(zst, prod[:, 0], tile2(cos), ALU.mult))
                    link(v.tensor_tensor(prod[:, 1], prod[:, 0, ::-1, :], tile2(sin), ALU.mult))
                    if i >= 2:
                        v.wait_ge(*s5_y(l, i - 1))
                    link(v.tensor_tensor(xs[:, i % 2, 0], zst[:, 0], prod[:, 1, 0], ALU.subtract))
                    result("xs", v.tensor_tensor(xs[:, i % 2, 1], zst[:, 1], prod[:, 1, 1], ALU.add))
                    if i % 4 == 2 and i > 5:
                        y_of(i // 4 - 1)
                y_of(7)

                def merge(job, b, i):
                    g = gate[:, b * KT + 2 * i:b * KT + 2 * i + 2, :]
                    m = merged[:, 2 * i:2 * i + 2, :]
                    v.wait_ge(*done(l, job))
                    if b == 0:
                        result("merge", v.tensor_tensor(m, g, bank2(job), ALU.mult), job)
                        return
                    if b == 1:
                        v.wait_ge(*act["glu"](l, i + 1))
                        link(v.tensor_tensor(mix_t, bank2(job), glu_s, ALU.mult), job)
                        link(v.tensor_tensor(mix_t, mix_t, g, ALU.mult))
                    else:
                        link(v.tensor_tensor(mix_t, g, bank2(job), ALU.mult), job)
                    result("merge", v.tensor_tensor(m, m, mix_t, ALU.add))

                v.wait_ge(*act["gate"](l, BRANCH))
                for i in range(4):
                    merge(("out_a", i), 0, i)
                v.wait_ge(*vec["merge"].last(l))

                v.wait_ge(*act["latent"](l, 2))
                result("square", v.tensor_tensor(oT, latent[:], latent[:], ALU.mult))
                v.wait_ge(*act["root"](l, 2))
                link(v.reciprocal(rstd[:], rstd[:]))
                for k in range(4):
                    result("lat", v.scalar_tensor_tensor(latent[:, k, :], latent[:, k, :],
                                                         col(("mla_q_norm", "mla_kv_norm")[k // 2], k % 2),
                                                         rstd[:, k // 2, :], ALU.mult, ALU.mult))
                cos, sin = waves_r[64:96, 0, :], waves_r[64:96, 1, :]
                one, two = rope_t[64:96, 0], rope_t[64:96, 1]
                step(v.tensor_tensor(one[:, 0, :], krope_raw[64:96, 0, :], cos, ALU.mult))
                link(v.tensor_tensor(two[:, 0, :], krope_raw[64:96, 1, :], sin, ALU.mult))
                result("k", v.tensor_tensor(kT[64:96], tile2(one[:, 0, :], HEADS), tile2(two[:, 0, :], HEADS), ALU.add))
                for i in range(4):
                    v.wait_ge(*act["qcopy"](l, i + 1))
                    link(v.tensor_tensor(one, qT[64:96, 2 * i:2 * i + 2, :], tile2(cos), ALU.mult))
                    v.wait_ge(*done(l, ("mla_qs", i)))
                    link(v.tensor_tensor(two, bank2(("mla_qs", i))[64:96], tile2(sin), ALU.mult), ("mla_qs", i))
                    result("rope_q", v.tensor_tensor(qT[64:96, 2 * i:2 * i + 2, :], one, two, ALU.add))

                def attention(name, heads, scale, first):
                    def maxima(h):
                        v.wait_ge(*done(l, (name + "_sc", h)))
                        link(v.tensor_reduce(stat[:, 2, h, :], bank2((name + "_sc", h)), X_AXIS, ALU.max))
                        result("max", v.tensor_scalar(stat[:, 0, h, :], stat[:, 2, h, :], -scale, None, ALU.mult))
                    maxima(0)
                    for h in range(heads):
                        if h + 1 < heads:
                            maxima(h + 1)
                        v.wait_ge(*act["exp"](l, 2 * (first + h) + 2))
                        link(v.reciprocal(stat[:, 1, h, :], stat[:, 1, h, :]))
                        for q in range(TT):
                            result("p", v.tensor_scalar(prob[:, h % 2, q, :], prob[:, h % 2, q, :], stat[:, 1, h, q:q + 1],
                                                        None, ALU.mult))

                attention("mla", HEADS, MLA_SCALE, 0)
                for i in range(4):
                    merge(("mla_o", i), 2, i)
                v.wait_ge(*vec["merge"].last(l))

                for i, b in enumerate(("b1", "b2")):
                    v.wait_ge(*done(l, ("filt", i)))
                    arg, whole = filter_h[:, 2, :], filter_h[:, 3, :]
                    rows = slice(0, HY_FO)
                    link(v.tensor_scalar(arg, bank(("filt", i))[rows, 0:T], col(b, 0, rows), col("freq", 0, rows),
                                         ALU.add, ALU.mult), ("filt", i))
                    link(v.tensor_scalar(arg, arg, INV_TWO_PI, None, ALU.mult))
                    link(v.tensor_scalar(whole, arg, ROUND, ROUND, ALU.add, ALU.subtract))
                    result("filt", v.tensor_tensor(arg, arg, whole, ALU.subtract))
                for o in range(HY_ORDER):
                    for i in range(4):
                        v.wait_ge(*done(l, (f"kf{o}", i)))
                        result("k_fb", v.tensor_tensor(k_fb[:, i // 2, i % 2, :], bank((f"kf{o}", i)), decay[:, i % 2, :],
                                                       ALU.mult), (f"kf{o}", i))
                    v.wait_ge(*vec["k_fb"].last(l))
                    link(v.memset(k_fb[0:1, 1, 0, :], 0.0))
                    step(v.tensor_tensor(k_sq, k_fb[:, 0], k_fb[:, 0], ALU.mult))
                    link(v.tensor_tensor(k_sd[:, 0], k_fb[:, 1], k_fb[:, 1], ALU.mult))
                    result("k_sq", v.tensor_tensor(k_sq, k_sq, k_sd[:, 0], ALU.add))
                    result("k_sd", v.tensor_tensor(k_sd[:, 0], k_fb[:, 0], k_fb[:, 1], ALU.add))
                    result("k_sd", v.tensor_tensor(k_sd[:, 1], k_fb[:, 0], k_fb[:, 1], ALU.subtract))
                    v.wait_ge(*act["k_root"](l, o + 1))
                    link(v.reciprocal(k_scale[:], k_scale[:]))
                    v.wait_ge(*act["k_dft"](l, 4 * o + 4))
                    link(v.tensor_copy(k_nyq, k_cos[:, 0]))
                    v.wait_ge(*done(l, (f"kd{o}", 4)))
                    step(v.tensor_copy(k_nyq[0:1], bank((f"kd{o}", 4))[0:1]), (f"kd{o}", 4))
                    link(v.memset(k_sin[0:1, 0, :], 0.0))
                    for i in range(2):
                        c, s = (f"vd{o}", 2 * i), (f"vd{o}", 2 * i + 1)
                        v.wait_ge(*done(l, s))
                        step(v.tensor_tensor(spec[:, i], bank(c), k_cos[:, i], ALU.mult))
                        step(v.tensor_tensor(spec[:, 2 + i], bank(c), k_sin[:, i], ALU.mult), c)
                        step(v.tensor_tensor(spec_t[:, 0], bank(s), k_sin[:, i], ALU.mult))
                        link(v.tensor_tensor(spec_t[:, 1], bank(s), k_nyq if i == 0 else k_cos[:, 1], ALU.mult), s)
                        result("spec", v.tensor_tensor(spec[:, i], spec[:, i], spec_t[:, 0], ALU.subtract))
                        result("spec", v.tensor_tensor(spec[:, 2 + i], spec[:, 2 + i], spec_t[:, 1], ALU.add))
                    if o == 0:
                        v.wait_ge(*gps["hyena"](l, 1))
                    for i in range(2):
                        job = (f"vi{o}", i)
                        v.wait_ge(*done(l, job))
                        for j in range(2):
                            ch = 2 * i + j
                            u = phyena[:, ch, 1:T + 1] if o == 0 else z_hy[:, ch, :]
                            link(v.tensor_scalar(mix_t[:, j, :], u, col("hy_bias", o * WT + ch), None, ALU.mult))
                            link(v.scalar_tensor_tensor(mix_t[:, j, :], bank2(job)[:, j, :], k_scale[:, ch:ch + 1],
                                                        mix_t[:, j, :], ALU.mult, ALU.add), *([job] * j))
                        xg = phyena[:, WT * (o + 1) + 2 * i:WT * (o + 1) + 2 * i + 2, 1:T + 1]
                        result("z", v.tensor_tensor(z_hy[:, 2 * i:2 * i + 2, :], xg, mix_t, ALU.mult))
                    v.wait_ge(*vec["z"].last(l))
                for i in range(4):
                    merge(("hy_out", i), 3, i)
                v.wait_ge(*vec["merge"].last(l))
                for i in range(4):
                    merge(("glu", 2 * i), 1, i)
                for i in range(4):
                    add_x(("mix", i), i)

                norm_x(3, "xa_norm")
                attention("xa", XH, XA_SCALE, HEADS)
                for i in range(4):
                    add_x(("xa_o", i), i)

                norm_x(4, "moe_norm")

                def spread_over(ap, n):
                    return ap.to_broadcast([P, TT, n])

                def first_best(best, of, key, m, oh, rank, n):
                    link(v.tensor_reduce(best, of, X_AXIS, ALU.max))
                    link(v.tensor_tensor(key, of, spread_over(best, n), ALU.is_equal))
                    link(v.tensor_tensor(key, key, rank.unsqueeze(1).to_broadcast([P, TT, n]), ALU.mult))
                    link(v.tensor_reduce(m, key, X_AXIS, ALU.max))
                    link(v.tensor_tensor(oh, key, spread_over(m, n), ALU.is_equal))

                v.wait_ge(*done(l, ("route", 0)))
                link(v.tensor_copy(r["logits"], bank(("route", 0))[:, 0:P].rearrange("p (t c) -> p t c", t=TT)[:, :, 0:GROUPS + EXPERTS]),
                     ("route", 0))
                gl = r["logits"][:, :, 0:GROUPS]
                el = r["logits"][:, :, GROUPS:]
                first_best(r["gmax"], gl, r["key4"], r["m4"], r["oh4"], rank4, GROUPS)
                result("oh", v.tensor_scalar(r["oh4"], r["oh4"], 1.0, None, ALU.mult))
                result("rmax", v.tensor_tensor(r["gdiff"], gl, spread_over(r["gmax"], GROUPS), ALU.subtract))
                v.wait_ge(*done(l, ("rank", 0)))
                step(v.tensor_scalar(r["rank"], bank(("rank", 0))[:, 0:TT * GROUPS].rearrange("p (t g) -> p t g", t=TT),
                                     -1.0, None, ALU.add))
                link(v.tensor_copy(r["count"][:, 0, :], bank(("rank", 0))[:, TT * GROUPS:(TT + 1) * GROUPS]), ("rank", 0))
                for t in range(TT):
                    for g in range(GROUPS):
                        result("pick", v.tensor_scalar(pick[:, t, g, :], clock[:, 0:CAP], r["rank"][:, t, g:g + 1],
                                                       r["oh4"][:, t, g:g + 1], ALU.is_equal, ALU.mult), settle=False)
                link(v.tensor_reduce(r["m4"][:, 0, :], r["count"][:, 0, :], X_AXIS, ALU.max))
                result("flag", v.tensor_scalar(crowded[:], r["m4"][0:1, 0, :], float(CAP), None, ALU.is_gt))
                for t in range(TT):
                    e4 = r["e4"][:, t, :].rearrange("p (g e) -> p g e", g=GROUPS)
                    link(v.tensor_tensor(e4, el[:, t, :].rearrange("p (g e) -> p g e", g=GROUPS),
                                         r["oh4"][:, t, :].unsqueeze(2).to_broadcast([P, GROUPS, PER_GROUP]), ALU.mult))
                    link(v.tensor_reduce(r["es"][:, t, :], e4.rearrange("p g e -> p e g"), X_AXIS, ALU.add))
                first_best(r["v1"], r["es"], r["key8"], r["m8"], r["oh1"], rank8, PER_GROUP)
                link(v.scalar_tensor_tensor(r["es2"], r["oh1"], -1e30, r["es"], ALU.mult, ALU.add))
                first_best(r["v2"], r["es2"], r["key8"], r["m8"], r["oh2"], rank8, PER_GROUP)
                result("r12", v.tensor_tensor(r["ex"], r["v2"], r["v1"], ALU.subtract))
                v.wait_ge(*act["rexp"](l, 2))
                link(v.tensor_reduce(r["gsum"], r["gdiff"], X_AXIS, ALU.add))
                link(v.reciprocal(r["gsum"], r["gsum"]))
                link(v.tensor_scalar(r["w1"], r["ex"], 1.0, None, ALU.add))
                link(v.reciprocal(r["w1"], r["w1"]))
                link(v.tensor_tensor(r["w1"], r["w1"], r["gsum"], ALU.mult))
                link(v.tensor_tensor(r["w2"], r["w1"], r["ex"], ALU.mult))
                link(v.tensor_tensor(r["c8"], r["oh1"], spread_over(r["w1"], PER_GROUP), ALU.mult))
                link(v.tensor_tensor(r["t8"], r["oh2"], spread_over(r["w2"], PER_GROUP), ALU.mult))
                link(v.tensor_tensor(r["c8"], r["c8"], r["t8"], ALU.add))
                for t in range(TT):
                    ins = v.tensor_tensor(r["comb"][:, t, :].rearrange("p (g e) -> p g e", g=GROUPS),
                                          r["oh4"][:, t, :].unsqueeze(2).to_broadcast([P, GROUPS, PER_GROUP]),
                                          r["c8"][:, t, :].unsqueeze(1).to_broadcast([P, GROUPS, PER_GROUP]), ALU.mult)
                    if t == 0:
                        link(ins)
                    else:
                        result("comb", ins, settle=False)

                def expert_values(first, t, weights, width, ready):
                    for j in range(TURN):
                        for f in range(2):
                            n = 2 * (first + j) + f
                            base = l * (2 * EXPERTS) + t * (2 * TURN)
                            v.wait_ge(*ready)
                            v.wait_ge(act["silu"].sem, base + (2 + n + 1))
                            v.wait_ge(moe_up.sem, base + (2 * EXPERTS + n + 1))
                            v.tensor_tensor(hid_t[:, f, 0:width], silu[:, f, 0:width], psum[:, 2 * f + 1, 0:width],
                                            ALU.mult).then_inc(hid_half.sem, 1)
                            v.wait_ge(hid_half.sem, base + (n + 1))
                            v.wait_ge(moe_down.sem, l * EXPERTS + t * TURN + (EXPERTS + first + j))
                            w = weights[:, bass.ds(t * TURN + (first + j), 1), :].rearrange("p o t -> p (o t)")
                            v.tensor_tensor(hid[:, f, 0:width], hid_t[:, f, 0:width], w, ALU.mult).then_inc(vec["hid"].sem, 1)

                flag = v.value_load(crowded[0:1, 0:1], min_val=0, max_val=1)
                with v.If(flag < 1):
                    for g in range(GROUPS):
                        with v.Fori(0, GROUP_TURNS) as t:
                            expert_values(PER_GROUP * g, t, cw_slot, CAP, act["cw"](l, EXPERTS // 4))
                with v.Else():
                    with v.Fori(0, TURNS) as t:
                        expert_values(0, t, gate, T, dense_cw_out(l, EXPERTS // 2))
                v.wait_ge(*moe_out(l, 1))
                v.wait_ge(*moe_down(l, EXPERTS))
                for i in range(4):
                    acc = psum[:, 4 + i, :].rearrange("p (a b) -> p a b", a=2)
                    result("x", v.tensor_tensor(xT[:, 2 * i:2 * i + 2, :], xT[:, 2 * i:2 * i + 2, :], acc, ALU.add))

            v.tensor_tensor(hT[:], xT[:], xT[:], ALU.mult).then_inc(end_dve, 1)
            v.wait_ge(end_act, 1)
            v.reciprocal(rstd[:, 0, :], rstd[:, 0, :]).then_inc(end_dve, 1)
            v.wait_ge(end_dve, 2)
            for k in range(KT):
                v.scalar_tensor_tensor(hT[:, k, :], xT[:, k, :], ends[:, KT + k:KT + k + 1], rstd[:, 0, :],
                                       ALU.mult, ALU.mult).then_inc(end_dve, 1)

        @block.tensor
        def _(pe):
            pe.sem_inc(moe_up.sem, 2 * EXPERTS)
            pe.sem_inc(moe_down.sem, EXPERTS)
            pe.wait_ge(x_loaded, 3 * 16)
            for i in range(8):
                src = view(arena, 2048 * (i // 4), TT, D)
                for k in range(4):
                    c = (4 * (i % 2) + k) * P
                    ins = pe.transpose(psum[:, i, k * P:(k + 1) * P], src[:, i % 4 // 2, c:c + P], ident[:])
                ins.then_inc(start_pe, 1)
            pe.wait_ge(small_loaded, DEPTH * 16 * 16)
            pe.wait_ge(start_act, 1)
            for l in range(DEPTH):
                ins = pe.transpose(psum[:, 0, l * P:(l + 1) * P], par_rows[:, l, :], ident[:])
            ins.then_inc(start_pe, 1)
            pe.wait_ge(consts_loaded, 11 * 16)
            pe.wait_ge(start_act, 2)
            pe.transpose(psum[:, 1, 0:2 * KT], ends_rows, ident[0:2 * KT, 0:2 * KT]).then_inc(start_pe, 1)
            pe.wait_ge(start_act, 3)
            pe.wait_ge(start_dve, 8)
            for k in range(KT):
                ins = pe.matmul(psum[:, 2, 0:T], ones[:], hT[:, k, :], start=k == 0, stop=k == KT - 1)
            ins.then_inc(start_pe, 1)

            with pe.Fori(0, DEPTH) as l:
                def begin(job):
                    i = JOB_AT[job]
                    if i >= JOB_BANKS:
                        for sig, n in freed[JOBS[i - JOB_BANKS]]:
                            pe.wait_ge(*sig(l, n))
                    return bank(job)

                def finish(ins):
                    ins.then_inc(*product.rise())

                def chunk(name, n=0):
                    i = CHUNK_AT[(name, n)]
                    pe.wait_ge(*slot_loaded[i % RING](l, dmas_upto[(name, n)]))
                    return ring[:, i % RING, :]

                def split(slot, k, c):
                    return slot[:, 0:k * c].rearrange("p (k c) -> p k c", k=k)

                def project(out, w, rhs, nk, c0, m=P, h_from=None):
                    for k in range(nk):
                        if h_from is not None:
                            pe.wait_ge(*vec["h"](l, h_from + k + 1))
                        ins = pe.matmul(out, w[:, k, c0:c0 + m], rhs[:, k, :], start=k == 0, stop=k == nk - 1)
                    return ins

                def pair(job, w, rhs, nk, c0, h_from=None, between=None):
                    b = begin(job)
                    for j in range(2):
                        if between:
                            between(j)
                        ins = project(b[:, j * T:(j + 1) * T], w, rhs, nk, c0 + j * P, h_from=None if j else h_from)
                    finish(ins)

                def total_x(job, squares):
                    b = begin(job)
                    for k in range(KT):
                        if k % 2 == 0:
                            pe.wait_ge(*vec["square"](l, squares + k // 2 + 1))
                        ins = pe.matmul(b[:, 0:T], ones[:], x_sq[:, k, :], start=k == 0, stop=k == KT - 1)
                    finish(ins)

                def turn(job, tiles):
                    b = begin(job)
                    for j, t in enumerate(tiles):
                        ins = pe.transpose(b[:, j * P:(j + 1) * P], t, ident[:])
                    finish(ins)

                def s5_in(i):
                    d, j, q = i // STATE_TILES, i % STATE_TILES // 4, i % 4
                    rows = slice(32 * q, 32 * q + 32)
                    if i >= 2:
                        pe.wait_ge(*vec["bu_used"](l, i - 1))
                    u = (u_fwd, u_bwd)[d][rows, j, :]
                    for ri in range(2):
                        ins = pe.matmul(psum[:, i % 2, ri * T:(ri + 1) * T], bT[rows, ri * 2 * WT + d * WT + j, :], u,
                                        start=True, stop=True)
                    ins.then_inc(*s5_bu.rise())

                def s5_out(i):
                    d, j, q = i // STATE_TILES, i % STATE_TILES // 4, i % 4
                    rows = slice(32 * q, 32 * q + 32)
                    if i % 4 == 0 and i >= 8:
                        pe.wait_ge(*vec["y"](l, i // 4 - 1))
                    pe.wait_ge(*vec["xs"](l, i + 1))
                    for ri in range(2):
                        ins = pe.matmul(psum[rows, 2 + i // 4 % 2, 0:T], cT[:, ri * 2 * WT + d * WT + j, rows], xs[:, i % 2, ri, :],
                                        start=ri == 0, stop=ri == 1)
                    ins.then_inc(*s5_y.rise())

                def attention(name, heads, rows, first, vd, v_done, values):
                    def scores(h):
                        b = begin((name + "_sc", h))
                        for q in range(TT):
                            ins = pe.matmul(b[:, q * T:(q + 1) * T], qT[0:rows, h, q * P:(q + 1) * P], kT[0:rows, h, :],
                                            start=True, stop=True)
                        finish(ins)
                    def output(h):
                        b = begin((name + "_pv", h))
                        pe.wait_ge(*act["probT"](l, first + h + 1))
                        if h == 0:
                            pe.wait_ge(*act["v"](l, v_done))
                        o = b[vd * h % P:vd * h % P + vd, 0:T]
                        for kt in range(TT):
                            ins = pe.matmul(o, v_tok[:, kt, h * vd:(h + 1) * vd], probT[:, h % 2, kt, :],
                                            start=kt == 0, stop=kt == TT - 1)
                        finish(ins)

                    scores(0)
                    scores(1)
                    values()
                    for h in range(heads):
                        b = begin((name + "_tr", h))
                        pe.wait_ge(*vec["p"](l, 2 * (first + h) + 2))
                        for kt in range(TT):
                            for q in range(TT):
                                ins = pe.transpose(b[:, kt * T + q * P:kt * T + (q + 1) * P],
                                                   prob[:, h % 2, q, kt * P:(kt + 1) * P], ident[:])
                        finish(ins)
                        if h + 2 < heads:
                            scores(h + 2)
                        if h:
                            output(h - 1)
                    output(heads - 1)

                total_x(("mix_sum", 0), 0)
                for job in IN_ORDER[:6]:
                    pair(job, split(chunk(*job), KT, IN_COLS), hT, KT, 0, h_from=0 if job == IN_ORDER[0] else None)
                b = begin(("s5_par", 0))
                pe.wait_ge(*vec["s5_rows"](l, 1))
                for n, i in enumerate((3, 5, 2, 4)):
                    ins = pe.matmul(b[:, n * ALL_TILES:(n + 1) * ALL_TILES], s5_w[:, i, :], ident[0:ALL_TILES, 0:ALL_TILES],
                                    start=True, stop=True)
                finish(ins)
                for job in IN_ORDER[6:9]:
                    pair(job, split(chunk(*job), KT, IN_COLS), hT, KT, 0)
                pe.wait_ge(*vec["s5_b"](l, 1))
                flat = view(gates, 1024, 4 * WT, P)
                for i in range(4):
                    turn(("s5_b", i), [flat[:, 4 * i + j, :] for j in range(4)])
                pe.wait_ge(*vec["s5_c"](l, 4))
                flat = view(gates, 4096, 4 * WT, P)
                for i in range(4):
                    turn(("s5_c", i), [flat[:, 4 * i + j, :] for j in range(4)])
                pe.wait_ge(*act["u"](l, 4))
                for job in IN_ORDER[9:]:
                    slot = chunk(*job)
                    if job[0] == "in_k":
                        b = begin(job)
                        for j in range(2):
                            ins = project(b[64:96, j * T:(j + 1) * T], split(slot, KT, 2 * ROPE), hT, KT, j * ROPE, ROPE)
                        finish(ins)
                    else:
                        def tiles(j):
                            for i in TILE_SLOTS.get((job, j), []):
                                if i == 0:
                                    pe.wait_ge(*act["s5_bT"](l, 4))
                                    pe.wait_ge(*act["s5_cT"](l, 4))
                                s5_in(i)
                                if i >= 2:
                                    s5_out(i - 2)

                        pair(job, split(slot, KT, IN_COLS), hT, KT, 0, between=tiles)
                s5_out(ALL_TILES - 2)
                s5_out(ALL_TILES - 1)

                pe.wait_ge(*gps["a"](l, 1))
                for i in range(4):
                    pair(("out_a", i), split(chunk("out_a", i // 2), WT, 512), p_b, WT, (i % 2) * 256)

                b = begin(("mla_sum", 0))
                pe.wait_ge(*vec["square"](l, 5))
                for k in range(4):
                    ins = pe.matmul(b[:, k // 2 * T:(k // 2 + 1) * T], ones[:], oT[:, k, :], start=k % 2 == 0, stop=k % 2 == 1)
                finish(ins)
                pe.wait_ge(*vec["lat"](l, 4))
                wq, wkv = split(chunk("mla_q"), 2, HEADS * QK), split(chunk("mla_kv"), 2, HEADS * (NOPE + VD))
                c_q, c_kv = latent[:, 0:2, :], latent[:, 2:4, :]
                for name, i in MLA_QK:
                    b = begin((name, i))
                    if name == "mla_qs":
                        pe.wait_ge(*act["qcopy"](l, i + 1))
                        ins = pe.matmul(b[64:96, :], swap[:], qT[0:QK, 2 * i:2 * i + 2, :], start=True, stop=True)
                    for j in range(2):
                        if name == "mla_q":
                            ins = project(b[0:QK, j * T:(j + 1) * T], wq, c_q, 2, (2 * i + j) * QK, QK)
                        elif name == "mla_k":
                            ins = project(b[0:NOPE, j * T:(j + 1) * T], wkv, c_kv, 2, (2 * i + j) * (NOPE + VD), NOPE)
                    finish(ins)
                def mla_values():
                    for i in range(TT):
                        b = begin(("mla_v", i))
                        for k in range(2):
                            wv = wkv[:, k, :].rearrange("p (h c) -> p h c", h=HEADS)[:, :, NOPE:]
                            ins = pe.matmul(b, c_kv[:, k, i * P:(i + 1) * P], wv, start=k == 0, stop=k == 1)
                        finish(ins)

                pe.wait_ge(*act["knope"](l, 4))
                pe.wait_ge(*act["qcopy"](l, 4))
                pe.wait_ge(*vec["rope_q"](l, 4))
                attention("mla", HEADS, QK, 0, VD, 2, mla_values)
                pe.wait_ge(*act["o"](l, HEADS))
                for i in range(4):
                    pair(("mla_o", i), split(chunk("mla_o", i // 2), WT, 512), oT, WT, (i % 2) * 256)

                pe.wait_ge(*route_loaded(l, 7))
                for i in range(2):
                    b = begin(("filt", i))
                    if i == 0:
                        ins = pe.matmul(b[:, 0:T], filter_w[0:HY_EMB, 0:2, :].rearrange("p a b -> p (a b)"), embed, start=True, stop=True)
                    else:
                        pe.wait_ge(*act["filt"](l, 1))
                        ins = pe.matmul(b[:, 0:T], filter_w[:, 1:3, :].rearrange("p a b -> p (a b)"), filter_h[:, 0, :], start=True, stop=True)
                    finish(ins)
                pe.wait_ge(*act["filt"](l, 2))
                w3 = chunk("filter")
                for o in range(HY_ORDER):
                    for i in range(4):
                        b = begin((f"kf{o}", i))
                        c = (2 * o + i // 2) * W
                        finish(pe.matmul(b, filter_h[:, 1, (i % 2) * P:(i % 2 + 1) * P], w3[0:HY_FO, c:c + W], start=True, stop=True))
                    b = begin((f"kn{o}", 0))
                    pe.wait_ge(*vec["k_sq"](l, o + 1))
                    for ch in range(WT):
                        for t in range(TT):
                            ins = pe.matmul(b[:, ch:ch + 1], k_sq[:, t, ch * P:(ch + 1) * P], ones[:, 0:1], start=t == 0, stop=t == TT - 1)
                    finish(ins)
                    pe.wait_ge(*vec["k_sd"](l, 2 * o + 2))
                    for i, (f, sd) in enumerate(((0, 0), (1, 0), (2, 1), (3, 1))):
                        b = begin((f"kd{o}", i))
                        for t in range(TT):
                            ins = pe.matmul(b, dft[:, t, f * P:(f + 1) * P], k_sd[:, sd, t, :], start=t == 0, stop=t == TT - 1)
                        finish(ins)
                    b = begin((f"kd{o}", 4))
                    for t in range(TT):
                        ins = pe.matmul(b[0:1, :], dft[:, t, T:T + 1], k_sd[:, 0, t, :], start=t == 0, stop=t == TT - 1)
                    finish(ins)
                    if o == 0:
                        pe.wait_ge(*gps["hyena"](l, 1))
                    else:
                        pe.wait_ge(*vec["z"](l, 2))
                    for t in range(TT):
                        src = phyena[:, 0:WT, 1:T + 1] if o == 0 else z_hy[:]
                        turn((f"vt{o}", t), [src[:, j, t * P:(t + 1) * P] for j in range(WT)])
                    pe.wait_ge(*act["seq"](l, 2 * o + 2))
                    for i, f in enumerate((0, 2, 1, 3)):
                        b = begin((f"vd{o}", i))
                        for t in range(TT):
                            ins = pe.matmul(b, dft[:, t, f * P:(f + 1) * P], seq_tok[:, t, :], start=t == 0, stop=t == TT - 1)
                        finish(ins)
                    pe.wait_ge(*vec["spec"](l, 4 * o + 4))
                    for i in range(2):
                        b = begin((f"vi{o}", i))
                        for j in range(2):
                            for f in range(4):
                                c = (2 * i + j) * P
                                ins = pe.matmul(b[:, j * T:(j + 1) * T], spec[:, f, c:c + P], idft[:, f, :], start=f == 0, stop=f == 3)
                        finish(ins)
                pe.wait_ge(*vec["z"](l, 4))
                for i in range(4):
                    pair(("hy_out", i), split(chunk("hy_out", i // 2), WT, 512), z_hy, WT, (i % 2) * 256)

                pe.wait_ge(*act["gelu"](l, 1))
                for i in range(4):
                    for g in range(2):
                        pair(("glu", 2 * i + g), split(chunk("glu", 2 * (i // 2) + g), WT, 512), ys, WT, (i % 2) * 256)
                pe.wait_ge(*vec["merge"](l, 16))
                for i in range(4):
                    pair(("mix", i), split(chunk("mix", i), KT, 256), merged, KT, 0)

                def xa_keys(n):
                    b = begin(("xa_k", n))
                    for j in range(2):
                        ins = project(b[:, j * T:(j + 1) * T], split(chunk("xa_kv", 2 * n + j), KT, 256), memT, KT, 0)
                    finish(ins)

                xa_keys(0)
                total_x(("xa_sum", 0), 5)
                xa_keys(1)
                for n in range(2):
                    pair(("xa_q", n), split(chunk("xa_q", n), KT, 256), hT, KT, 0, h_from=None if n else KT)

                def xa_values():
                    for t in range(TT):
                        b = begin(("xa_v", t))
                        for h in range(XH):
                            w = split(chunk("xa_kv", h), KT, 256)
                            for k in range(KT):
                                ins = pe.matmul(b[:, h * XD:(h + 1) * XD], memT[:, k, t * P:(t + 1) * P], w[:, k, XD:], start=k == 0, stop=k == KT - 1)
                        finish(ins)

                pe.wait_ge(*act["xa_qk"](l, 4))
                attention("xa", XH, XD, HEADS, XD, 4, xa_values)
                pe.wait_ge(*act["o"](l, HEADS + XH))
                for i in range(4):
                    pair(("xa_o", i), split(chunk("xa_o", i // 2), WT, 512), oT, WT, (i % 2) * 256)

                total_x(("moe_sum", 0), 9)
                b = begin(("route", 0))
                for t in range(TT):
                    o = b[:, 64 * t:64 * t + GROUPS + EXPERTS]
                    for k in range(KT):
                        if t == 0:
                            pe.wait_ge(*vec["h"](l, 2 * KT + k + 1))
                        pe.matmul(o, hT[:, k, t * P:(t + 1) * P], route_w[:, k, :], start=k == 0, stop=False)
                    ins = pe.matmul(o, ones[0:1, :], bias[:], start=False, stop=True)
                finish(ins)
                for i in range(4):
                    turn(("h_tok", i), [hT[:, 4 * (i % 2) + k, (i // 2) * P:(i // 2 + 1) * P] for k in range(4)])
                b = begin(("rank", 0))
                pe.wait_ge(*vec["oh"](l, 1))
                oh = r["oh4"]
                for c, terms in enumerate((((upto, 0),), ((ones, 0), (upto, 1)), ((ones, 0), (ones, 1)))):
                    for n, (m, t) in enumerate(terms):
                        ins = pe.matmul(b[:, c * GROUPS:(c + 1) * GROUPS], m[:], oh[:, t, :], start=n == 0, stop=n == len(terms) - 1)
                finish(ins)
                pe.wait_ge(*act["h_tok"](l, 4))
                for k in range(KT):
                    b = begin(("gather", k))
                    if k == 0:
                        pe.wait_ge(*vec["pick"](l, 2 * GROUPS))
                    for t in range(TT):
                        ins = pe.matmul(b[:, 0:GROUPS * CAP], h_tok[:, t, k * P:(k + 1) * P], pick[:, t].rearrange("p g s -> p (g s)"),
                                        start=t == 0, stop=t == TT - 1)
                    finish(ins)
                for i in range(2):
                    b = begin(("back", i))
                    for g in range(2):
                        for t in range(TT):
                            ins = pe.transpose(b[0:CAP, g * T + t * P:g * T + (t + 1) * P], pick[:, t, 2 * i + g, :], ident[:])
                    finish(ins)
                for i in range(EXPERTS // 4):
                    b = begin(("cw", i))
                    if i == 0:
                        pe.wait_ge(*vec["comb"](l, 1))
                    for j in range(4):
                        e = 4 * i + j
                        for t in range(TT):
                            ins = pe.matmul(b[:, j * CAP:(j + 1) * CAP], r["comb"][:, t, e:e + 1].to_broadcast([P, P]),
                                            pick[:, t, e // PER_GROUP, :], start=t == 0, stop=t == TT - 1)
                    finish(ins)

                def expert_products(first, t, h_in, width, down):
                    for j in range(TURN):
                        w = []
                        for s in range(3 * j, 3 * j + 3):
                            pe.wait_ge(slot_loaded[s].sem, l * (16 * slot_loaded[s].per_layer) + t * 16
                                       + 16 * (slot_dmas[s] + first // TURN + 1))
                            w.append(split(ring[:, s, :], (KT, KT, 2)[s % 3], (FF, FF, D)[s % 3]))
                        base = l * (2 * EXPERTS) + t * (2 * TURN)
                        for f in range(2):
                            n = 2 * (first + j) + f
                            pe.wait_ge(act["silu"].sem, base + (n + 1))
                            pe.wait_ge(vec["hid"].sem, base + (n + 1))
                            project(psum[:, 2 * f, 0:width], w[0], h_in, KT, f * P).then_inc(moe_gate.sem, 1)
                            project(psum[:, 2 * f + 1, 0:width], w[1], h_in, KT, f * P).then_inc(moe_up.sem, 1)
                        for f in range(2):
                            pe.wait_ge(vec["hid"].sem, base + (2 + 2 * (first + j) + f + 1))
                            ins = down(w[2], f)
                        ins.then_inc(moe_down.sem, 1)

                flag = pe.value_load(crowded[0:1, 0:1], min_val=0, max_val=1)
                with pe.If(flag < 1):
                    pe.sem_inc(dense_cw.sem, EXPERTS // 2)
                    pe.wait_ge(*act["cw"](l, EXPERTS // 4))
                    pe.wait_ge(*act["gather"](l, KT))
                    for g in range(GROUPS):
                        if g:
                            pe.wait_ge(*act["y_slot"](l, 2 * g))
                        for i in range(2):
                            pe.matmul(psum[0:CAP, 4 + i, :], zeros[:, 0:CAP], dft[:, 0, :], start=True, stop=True, skip_group_check=True)

                        def down(w, f):
                            for i in range(2):
                                ins = pe.matmul(psum[0:CAP, 4 + i, :], hid[:, f, 0:CAP], w[:, f, i * 512:(i + 1) * 512],
                                                start=False, stop=True, skip_group_check=True)
                            return ins

                        with pe.Fori(0, GROUP_TURNS) as t:
                            expert_products(PER_GROUP * g, t, hg[:, :, g * CAP:(g + 1) * CAP], CAP, down)
                    pe.wait_ge(*act["back"](l, 2))
                    pe.wait_ge(*act["y_slot"](l, 2 * GROUPS))
                    for m in range(KT):
                        for g in range(GROUPS):
                            ins = pe.matmul(psum[:, 4 + m // 2, (m % 2) * T:(m % 2 + 1) * T], y_slot[0:CAP, g, m * P:(m + 1) * P],
                                            back[0:CAP, g, :], start=g == 0, stop=g == GROUPS - 1)
                    ins.then_inc(*moe_out.rise())
                with pe.Else():
                    pe.sem_inc(moe_out.sem, 1)
                    pe.wait_ge(*act["cw"](l, EXPERTS // 4))
                    for i in range(EXPERTS // 2):
                        if i >= 4:
                            pe.wait_ge(*dense_cw_out(l, i - 3))
                        for j in range(4):
                            ins = pe.matmul(psum[:, 4 + i % 4, j * P:(j + 1) * P],
                                            r["comb"][:, j % 2, 2 * i + j // 2:2 * i + j // 2 + 1].to_broadcast([P, P]), ident[:],
                                            start=True, stop=True)
                        ins.then_inc(*dense_cw.rise())
                    pe.wait_ge(*dense_cw_out(l, EXPERTS // 2))
                    for i in range(4):
                        pe.matmul(psum[:, 4 + i, :], zeros[:], dft[:, 0, :], start=True, stop=True, skip_group_check=True)

                    def down(w, f):
                        for m in range(KT):
                            ins = pe.matmul(psum[:, 4 + m // 2, (m % 2) * T:(m % 2 + 1) * T], w[:, f, m * P:(m + 1) * P],
                                            hid[:, f, :], start=False, stop=True, skip_group_check=True)
                        return ins

                    with pe.Fori(0, TURNS) as t:
                        expert_products(0, t, hT, T, down)

            pe.wait_ge(end_dve, 1)
            for k in range(KT):
                ins = pe.matmul(psum[:, 4, 0:T], ones[:], hT[:, k, :], start=k == 0, stop=k == KT - 1)
            ins.then_inc(end_pe, 1)
            pe.wait_ge(end_dve, 2 + KT)
            for i in range(4):
                for k in range(4):
                    ins = pe.transpose(psum[:, i, k * P:(k + 1) * P], hT[:, 4 * (i % 2) + k, (i // 2) * P:(i // 2 + 1) * P], ident[:])
                ins.then_inc(end_pe, 1)

        for sig in [product, vector_step, pool_step, route_loaded, moe_out, dense_cw, dense_cw_out, s5_bu, s5_y, s5_loaded, *act.values(), *vec.values(), *gps.values()]:
            if sig.count != sig.per_layer and sig not in (act["silu"], vec["hid"]):
                raise AssertionError(f"{sig.sem} rises {sig.count} times in a layer, not {sig.per_layer}")


_CONSTS = ("c_ident", "c_small", "c_swap", "c_upto", "c_clock", "c_dft", "c_idft", "c_decay", "c_embed")


def constants():
    f8 = np.float64
    t = np.arange(T)
    small = np.zeros((P, 20), np.float32)
    small[:, 0] = EPS
    small[:, 1] = (np.arange(P) // 16) % 2 == 0
    small[:, 2] = (np.arange(P) // 16) % 2 == 1
    inv = 1.0 / (10000.0 ** (np.arange(0, ROPE, 2, dtype=f8) / ROPE))
    small[64:96, 3] = np.tile(inv / (2 * np.pi), 2)
    small[64:80, 4], small[80:96, 4] = -1.0, 1.0
    small[:, 5:9] = np.arange(4, 0, -1)
    small[:, 9:17] = np.arange(8, 0, -1)
    small[:, 17] = 0.25
    f = np.arange(T)
    ang = 2 * np.pi * ((t[:, None] * f[None]) % NFFT) / NFFT
    cos, sin = np.cos(ang), np.sin(ang)
    sin[:, 0] = (-1.0) ** t
    dft = np.concatenate([cos, sin], axis=1)
    weight = np.full(2 * T, 2.0 / NFFT)
    weight[0] = weight[T] = 1.0 / NFFT
    idft = dft.T * weight[:, None]
    t_norm = np.arange(T, dtype=np.float32) / np.float32(T - 1)
    bands = np.linspace(1e-4, (HY_EMB - 1) // 2 - 1, (HY_EMB - 1) // 2)
    a = (2 * np.pi / T) * t[:, None] * bands[None]
    embed = np.concatenate([t_norm[:, None], np.cos(a), -np.sin(a)], axis=-1).T
    deltas = np.abs(np.linspace(math.log(1e-2) / 1.5, math.log(1e-2) / 0.3, W))
    decay = np.exp(-t_norm.astype(f8)[:, None] * deltas)
    out = {"c_ident": np.eye(P), "c_upto": np.triu(np.ones((P, P))), "c_swap": np.roll(np.eye(QK)[:, NOPE:], 0, axis=0)[:, (np.arange(ROPE) + ROPE // 2) % ROPE], "c_small": small, "c_clock": np.tile(t, (P, 1)),
           "c_dft": dft.reshape(TT, P, NFFT).transpose(1, 0, 2), "c_idft": idft.reshape(4, P, T).transpose(1, 0, 2),
           "c_decay": decay.reshape(TT, P, W).transpose(1, 0, 2), "c_embed": embed}
    return {k: np.ascontiguousarray(v.astype(np.float32)) for k, v in out.items()}


def kernel(**inputs):
    import concourse.bacc as _bacc
    from concourse.bass_utils import run_bass_kernel_spmd as _run

    nc = _bacc.Bacc("TRN2", target_bir_lowering=False, num_devices=1)
    arrays, aps = {}, {}
    for name, value in {**inputs, **constants()}.items():
        v = np.ascontiguousarray(value)
        arrays[f"in_{name}"] = v
        aps[name] = nc.dram_tensor(f"in_{name}", v.shape, mybir.dt.from_np(v.dtype), kind="ExternalInput").ap()
    out = nc.dram_tensor("out_0", (1, T, D), F32, kind="ExternalOutput").ap()
    encoder(nc, aps, out)
    r = _run(nc, [arrays], core_ids=[0])
    return r.results[0]["out_0"]
```

```python
import math
from contextlib import ExitStack

import numpy as np
import concourse.bass as bass
from concourse import mybir

F32 = mybir.dt.float32
I32 = mybir.dt.int32
ALU = mybir.AluOpType
ACT = mybir.ActivationFunctionType
X_AXIS = mybir.AxisListType.X

P = 128
EPS = 1e-6
ROUND = 1.5 * 2.0 ** 23
INV_TWO_PI = 1.0 / (2.0 * math.pi)
SIN_SCALE = 6.2831845

DEPTH, D, T = 2, 1024, 256
KT = D // P
TT = T // P
W = 512
WT = W // P
STATE_TILES = 16
ALL_TILES = 2 * STATE_TILES
HEADS, NOPE, ROPE, VD = 8, 64, 32, 64
QK = NOPE + ROPE
LORA = 256
XH, XD = 4, 128
BRANCH = 4
GROUPS, PER_GROUP, FF = 4, 8, 256
EXPERTS = GROUPS * PER_GROUP
HY_EMB, HY_FO, HY_ORDER = 33, 64, 2
NFFT = 2 * T
MLA_SCALE = float(QK) ** -0.5
XA_SCALE = float(XD) ** -0.5

COL_A, COL_S = 0, 3 * W
COL_M = COL_S + W
COL_KR = COL_M + 2 * LORA
COL_H = COL_KR + ROPE
COL_G = COL_H + 3 * W

PAR, PAR_ROWS = {}, 0
for _name, _k in (("mix_norm", KT), ("gate_bias", BRANCH * KT), ("conv_a", 3 * WT), ("s5_d", WT),
                  ("mla_q_norm", 2), ("mla_kv_norm", 2), ("hy_conv", 9 * WT), ("hy_bias", HY_ORDER * WT),
                  ("xa_norm", KT), ("moe_norm", KT)):
    PAR[_name] = PAR_ROWS
    PAR_ROWS += _k
PAR["freq"], PAR["b1"], PAR["b2"] = PAR_ROWS, PAR_ROWS + 1, PAR_ROWS + 2
PAR_ROWS += 3
assert PAR_ROWS <= P

SLOT, RING = 2048, 6
IN_COLS = 256
IN_ORDER = ([("in_s", 0), ("in_a", 0), ("in_s", 1)] + [("in_h", i) for i in range(6)] + [("in_k", 0)]
            + [("in_a", i) for i in range(1, 6)] + [("in_m", i) for i in range(2)] + [("in_g", i) for i in range(16)])
CHUNKS = (IN_ORDER + [("out_a", 0), ("out_a", 1), ("mla_q", 0), ("mla_kv", 0), ("filter", 0),
                      ("mla_o", 0), ("mla_o", 1)]
          + [("glu", i) for i in range(4)] + [("hy_out", 0), ("hy_out", 1)] + [("mix", i) for i in range(4)]
          + [("xa_q", i) for i in range(2)] + [("xa_kv", i) for i in range(4)] + [("xa_o", i) for i in range(2)])
CHUNK_AT = {c: i for i, c in enumerate(CHUNKS)}
TURN = 2
TURNS = EXPERTS // TURN
CAP = 96
GROUP_TURNS = PER_GROUP // TURN
assert 3 * TURN == RING


def jobs_of(name, *ns):
    return [(name, n) for n in ns]


def attention_jobs(name, heads, between={}, early=0):
    v, sc = jobs_of(name + "_v", 0, 1), jobs_of(name + "_sc", 0, 1, 2)
    jobs = v[:early] + sc + v[early:]
    for h in range(heads):
        jobs.append((name + "_tr", h))
        if h + 3 < heads:
            jobs.append((name + "_sc", h + 3))
        jobs += between.get(h, [])
        if h:
            jobs.append((name + "_pv", h - 1))
    return jobs + [(name + "_pv", heads - 1)]


KF_HEADS = {1 + i: [("kf0", i)] for i in range(4)}
HYENA = (jobs_of("mla_o", 0, 1) + jobs_of("kd0", *range(5)) + jobs_of("kn0", 0) + jobs_of("mla_o", 2, 3)
         + jobs_of("vt0", 0, 1) + jobs_of("vd0", *range(4)) + jobs_of("kf1", *range(4)) + jobs_of("glu", 0, 1)
         + jobs_of("vi0", 0, 1) + jobs_of("glu", 2, 3) + jobs_of("vt1", 0, 1) + jobs_of("kd1", *range(5))
         + jobs_of("kn1", 0) + jobs_of("vd1", *range(4)) + jobs_of("glu", 4, 5) + jobs_of("vi1", 0, 1)
         + jobs_of("glu", 6, 7) + jobs_of("hy_out", *range(4)))
MLA_QK = (jobs_of("mla_q", *range(4)) + [("mla_k", 0), ("mla_qs", 0), ("mla_k", 1), ("mla_qs", 1),
                                         ("mla_k", 2), ("mla_qs", 2), ("mla_k", 3), ("mla_qs", 3)])
JOBS = ([("mix_sum", 0)] + IN_ORDER[:3]
        + [("s5_par", 0)] + IN_ORDER[3:6] + [("s5_b", i) for i in range(4)] + [("s5_c", i) for i in range(4)] + IN_ORDER[6:]
        + [("filt", 0), ("out_a", 0), ("filt", 1), ("mla_sum", 0)] + jobs_of("out_a", 1, 2, 3) + MLA_QK
        + attention_jobs("mla", HEADS, KF_HEADS) + HYENA + [("mix", i) for i in range(4)]
        + [("xa_k", 0), ("xa_sum", 0), ("xa_k", 1), ("xa_q", 0), ("xa_q", 1)]
        + attention_jobs("xa", XH, early=1) + [("xa_o", i) for i in range(4)]
        + [("moe_sum", 0), ("route", 0)] + [("h_tok", i) for i in range(4)] + [("rank", 0)]
        + [("gather", i) for i in range(KT)] + [("back", i) for i in range(2)] + [("cw", 0)])
JOB_AT = {j: i for i, j in enumerate(JOBS)}
BANK, BANK_BEFORE, _last = {}, {}, {}
for _i, _j in enumerate(JOBS):
    BANK[_j] = 4 + _i % 4 if _i < JOB_AT[("filt", 0)] else _i % 8
    BANK_BEFORE[_j] = _last.get(BANK[_j])
    _last[BANK[_j]] = _j
LAST_USE = {c: c for c in CHUNKS}
for _n in ("out_a", "mla_o", "hy_out", "xa_o"):
    for _i in range(2):
        LAST_USE[(_n, _i)] = (_n, 2 * _i + 1)
LAST_USE[("mla_q", 0)] = ("mla_qs", 3)
LAST_USE[("mla_kv", 0)] = ("mla_v", 1)
LAST_USE[("filter", 0)] = ("kf1", 3)
for _i in range(4):
    LAST_USE[("glu", _i)] = ("glu", 4 * (_i // 2) + 2 + _i % 2)
    LAST_USE[("xa_kv", _i)] = ("xa_v", 1)
TILE_SLOTS, TILE_HALVES = {}, 50
for _i in range(ALL_TILES):
    _h = 3 + _i * TILE_HALVES // ALL_TILES
    TILE_SLOTS.setdefault((IN_ORDER[6 + _h // 2], _h % 2), []).append(_i)


class Signal:

    def __init__(self, sem, per_layer, unit=1, base=0):
        self.sem, self.per_layer, self.unit, self.base, self.count = sem, per_layer, unit, base, 0

    def __call__(self, l, n):
        return self.sem, l * (self.per_layer * self.unit) + (self.base + n * self.unit)

    def rise(self):
        self.count += 1
        return self.sem, self.unit

    def last(self, l):
        return self(l, self.count)


SCALAR = dict(root=4, s5_exp=2, s5_sin=2, s5_col=1, s5_bT=4, s5_cT=4, u=4, ph=6, kraw=1, pa=6, latent=2,
              gate=BRANCH * KT, wave=32, turns=64, qcopy=4, knope=4, v=4, exp=24, probT=12, o=12, filt=2, k_root=2,
              k_dft=8, seq=4, gelu=1, glu=4, xa_qk=4, rexp=2, h_tok=4, gather=KT, back=2, cw=1, silu=2 * EXPERTS)
VECTOR = dict(par=2, square=13, h=3 * KT, s5_arg=2, s5_rows=1, s5_b=1, s5_c=4, phase=32, bu_used=32, xs=32, y=8,
              merge=16, lat=4, rope_q=4, k=1, max=12, p=24, filt=2, k_fb=8, k_sq=2, k_sd=4,
              spec=8, z=4, x=12, oh=1, pick=8, flag=1, y_slot=1 + EXPERTS, rmax=1, r12=1, comb=1, hid=2 * EXPERTS)
VECTOR_STEPS, POOL_STEPS = 459, 80
POOL = dict(a=1, hyena=1)


def encoder(nc, a, out):
    with ExitStack() as ctx:
        def sb(name, shape, dt=F32):
            return ctx.enter_context(nc.sbuf_tensor(name, shape, dt))

        def semaphore(name):
            return ctx.enter_context(nc.semaphore(name))

        def signal(name, per_layer, unit=1, base=0):
            return Signal(semaphore(name), per_layer, unit, base)

        ring = sb("ring", [P, RING, SLOT])
        xT = sb("xT", [P, KT, T])
        memT = sb("memT", [P, KT, T])
        hT = sb("hT", [P, KT, T])
        gates = sb("gates", [P, BRANCH * KT * T])
        phyena = sb("phyena", [P, 3 * WT, T + 2])
        pa = sb("pa", [P, 2 * WT * T + WT * (T + 2)])
        u_fwd = sb("u_fwd", [P, WT, T])
        u_bwd = sb("u_bwd", [P, WT, T])
        latent = sb("latent", [P, 4, T])
        krope_raw = sb("krope_raw", [P, 2, T])
        waves_r = sb("waves_r", [P, 2, T])
        rope_t = sb("rope_t", [P, 2, 2, T])
        arena = sb("arena", [P, 8192])
        rstd = sb("rstd", [P, 2, T])
        ident = sb("ident", [P, P])
        swap = sb("swap", [QK, ROPE])
        ones = sb("ones", [P, P])
        zeros = sb("zeros", [P, P])
        dft = sb("dft", [P, TT, NFFT])
        idft = sb("idft", [P, 4, T])
        decay = sb("decay", [P, TT, W])
        clock = sb("clock", [P, T])
        small = sb("small", [P, 20])
        par_all = sb("par_all", [P, DEPTH, P])
        par = sb("par", [P, P])
        ends = sb("ends", [P, 2 * KT])
        filter_w = sb("filter_w", [HY_FO, 3, HY_FO])
        s5_all = sb("s5_all", [ALL_TILES, DEPTH, 2 * P + 2])
        s5_col = sb("s5_col", [P, 4, ALL_TILES])
        route_w = sb("route_w", [P, KT, GROUPS + EXPERTS])
        bias = sb("bias", [1, GROUPS + EXPERTS])
        rt = sb("rt", [P, 400])
        stat = sb("stat", [P, 3, HEADS, 2])
        k_scale = sb("k_scale", [P, WT])
        upto = sb("upto", [P, P])
        crowded = sb("crowded", [1, 1], I32)
        psum = ctx.enter_context(nc.psum_tensor("psum", [P, 8, 512], F32))

        eps = small[:, 0:1]
        half = (small[:, 1:2], small[:, 2:3])
        inv_turns, sin_sign = small[64:96, 3:4], small[64:96, 4:5]
        rank4, rank8 = small[:, 5:9], small[:, 9:17]
        quarter = small[:, 17:18]

        def view(buf, at, *shape):
            v = buf[:, at:at + int(np.prod(shape))]
            names = "abcd"[:len(shape)]
            if len(shape) == 1:
                return v
            return v.rearrange(f"p ({' '.join(names)}) -> p {' '.join(names)}",
                               **{n: s for n, s in zip(names, shape)})

        gate = view(gates, 0, BRANCH * KT, T)
        p_b, p_c, xin = view(pa, 0, WT, T), view(pa, WT * T, WT, T), view(pa, 2 * WT * T, WT, T + 2)
        positions = krope_raw[64:96, 0, :].bitcast(I32)
        embed = krope_raw[0:HY_EMB, 1, :]
        s5_rows = waves_r[0:ALL_TILES].rearrange("p a b -> p (a b)")[:, 0:2 * P + 2]
        s5_w = view(pa, 512, 12, P)[0:ALL_TILES]
        latent_flat = latent[:].rearrange("p a b -> p (a b)")
        par_rows = view(latent_flat, 0, DEPTH, P)
        ends_rows = latent_flat[0:2 * KT, 256:256 + P]
        filter_h = u_bwd[0:HY_FO]
        conv_t = rope_t[:].rearrange("p a b t -> p (a b) t")
        ys = u_fwd
        b_raw = view(gates, 0, 2, ALL_TILES, 16)
        b_blk = view(gates, 1024, 2, ALL_TILES, 2, 16)
        c_raw = view(gates, 3072, 2, 2 * WT, 64)
        c_blk = view(gates, 4096, 2, 2 * WT, 2, 64)
        b_tmp = view(gates, 6144, 2, ALL_TILES, 16)
        bT = view(arena, 0, 4 * WT, P)
        cT = view(arena, 2048, 4 * WT, P)
        wave = view(arena, 4096, 2, 2, T)
        turn_t = view(arena, 5120, 2, T)
        prod = view(arena, 5632, 2, 2, T)
        zst = view(arena, 6656, 2, T)
        xs = view(arena, 7168, 2, 2, T)
        qT = view(arena, 0, HEADS, T)
        kT = view(arena, 2048, HEADS, T)
        v_tok = view(arena, 4096, TT, W)
        prob = view(arena, 5120, 2, TT, T)
        probT = view(arena, 6144, 2, TT, T)
        oT = view(arena, 7168, 4, T)
        k_cos = view(arena, 0, 2, W)
        k_sin = view(arena, 1024, 2, W)
        k_nyq = view(arena, 2048, W)
        k_sd = view(arena, 2560, 2, TT, W)
        seq_tok = view(arena, 4608, TT, W)
        spec = view(arena, 5632, 4, W)
        k_fb = view(pa, 0, 2, TT, W)
        k_sq = view(pa, 2048, TT, W)
        spec_t = view(pa, 2048, 2, W)
        z_hy = u_bwd
        glu_s = (rope_t[:, 1], view(arena, 7680, 2, T))
        mix_t = rope_t[:, 0]
        silu = view(arena, 0, 2, T)
        hid_t = view(arena, 512, 2, T)
        hid = view(arena, 1024, 2, T)
        h_tok = view(arena, 0, TT, D)
        pick = view(arena, 2048, TT, GROUPS, CAP)
        hg = view(arena, 3072, KT, GROUPS * CAP)
        back = view(arena, 6656, GROUPS, T)
        y_slot = view(gates, 4096, GROUPS, D)
        cw_slot = view(gates, 0, EXPERTS)
        merged = hT
        x_sq = view(arena, 5120, KT, T)
        at, r = 0, {}
        for name, n in (("logits", 36), ("gmax", 1), ("gdiff", 4), ("key4", 4), ("m4", 1), ("oh4", 4), ("gsum", 1),
                        ("e4", 32), ("es", 8), ("v1", 1), ("key8", 8), ("m8", 1), ("oh1", 8), ("es2", 8), ("v2", 1),
                        ("oh2", 8), ("ex", 1), ("w1", 1), ("w2", 1), ("c8", 8), ("t8", 8), ("comb", 32), ("rank", 4), ("count", 4)):
            r[name] = view(rt, at, TT, n)
            at += TT * n

        slot_dmas, dmas_upto = [0] * RING, {}
        for i, c in enumerate(CHUNKS):
            slot_dmas[i % RING] += 3 if c[0] == "in_k" else 1
            dmas_upto[c] = slot_dmas[i % RING]
        slot_loaded = [signal(f"slot{s}_loaded", slot_dmas[s] + TURNS, 16) for s in range(RING)]
        consts_loaded, x_loaded, mem_loaded, small_loaded = (semaphore("consts_loaded"), semaphore("x_loaded"),
                                                             semaphore("mem_loaded"), semaphore("small_loaded"))
        mem_step = semaphore("mem_norm_step")
        s5_loaded, route_loaded = signal("s5_matrices_loaded", 4, 16), signal("route_loaded", 7, 16)
        cleared = semaphore("cleared")
        start_pe, start_act, start_dve = semaphore("start_product"), semaphore("start_scalar"), semaphore("start_vector")
        end_pe, end_act, end_dve, stored = (semaphore("end_product"), semaphore("end_scalar"),
                                            semaphore("end_vector"), semaphore("stored"))
        product = signal("product", len(JOBS))
        act = {n: signal("scalar_" + n, k, base=2 * (n == "silu")) for n, k in SCALAR.items()}
        vec = {n: signal("vector_" + n, k, base={"hid": 2, "square": 4, "y_slot": 1}.get(n, 0)) for n, k in VECTOR.items()}
        gps = {n: signal("pool_" + n, k) for n, k in POOL.items()}
        vector_step = signal("vector_step", VECTOR_STEPS)
        pool_step = signal("pool_step", POOL_STEPS)
        s5_bu, s5_y = signal("s5_bu_product", ALL_TILES), signal("s5_y_product", ALL_TILES)
        moe_gate = signal("expert_gate_product", 2 * EXPERTS)
        hid_half = signal("expert_value", 2 * EXPERTS)
        moe_up = signal("expert_up_product", 2 * EXPERTS, base=2 * EXPERTS)
        moe_down = signal("expert_down_product", EXPERTS, base=EXPERTS)
        moe_out = signal("scattered_product", KT // 2)
        dense_cw, dense_cw_out = signal("dense_weight_product", EXPERTS // 2), signal("dense_weight_scalar", EXPERTS // 2)

        freed = {}

        def bank(job):
            return psum[:, BANK[job], :]

        def bank2(job):
            return bank(job).rearrange("p (a b) -> p a b", a=2)

        def done(l, job):
            return product(l, JOB_AT[job] + 1)

        def reads(job, sig):
            freed.setdefault(job, []).append((sig, sig.count))

        def col(name, i, rows=slice(0, P)):
            return par[rows, PAR[name] + i:PAR[name] + i + 1]

        block = ctx.enter_context(nc.Block())

        def load_small(eng, l):
            for name in ("mix_norm", "gate_bias", "conv_a", "s5_d", "mla_q_norm", "mla_kv_norm", "hy_conv",
                         "hy_bias", "xa_norm", "moe_norm"):
                w = a[name][l]
                src = w.rearrange("(k p) -> k p", p=P) if len(w.shape) == 1 else w.rearrange("b (k p) -> (b k) p", p=P)
                eng.dma_start(par_rows[PAR[name]:PAR[name] + src.shape[0], l, :], src).then_inc(small_loaded, 16)
            for name, w in (("freq", "hy_f_freq"), ("b1", "hy_f_b1"), ("b2", "hy_f_b2")):
                eng.dma_start(par_rows[PAR[name]:PAR[name] + 1, l, 0:HY_FO], a[w][l:l + 1]).then_inc(small_loaded, 16)
            for c, n, w in ((0, P, a["s5_lambda_re"][l].rearrange("d (t g) p -> (d t) (g p)", g=2)),
                            (P, P, a["s5_lambda_im"][l].rearrange("d (t g) p -> (d t) (g p)", g=2)),
                            (2 * P, 2, a["s5_log_step"][l].rearrange("d (t g) -> (d t) g", g=2))):
                eng.dma_start(s5_all[:, l, c:c + n], w).then_inc(small_loaded, 16)

        @block.sync
        def _(sp):
            def load(l, i):
                (name, n), s = CHUNKS[i], i % RING
                if name == "in_k":
                    w = a["w_in"][l].rearrange("(k p) c -> p k c", p=P)
                    dst = ring[:, s, 0:KT * 2 * ROPE].rearrange("p (k c) -> p k c", k=KT)
                    for d, c0, c in ((0, COL_KR, 32), (32, COL_KR + 16, 16), (48, COL_KR, 16)):
                        sp.dma_start(dst[:, :, d:d + c], w[:, :, c0:c0 + c]).then_inc(*slot_loaded[s].rise())
                    return
                if name[:3] == "in_":
                    first = {"s": COL_S, "h": COL_H, "a": COL_A, "m": COL_M, "g": COL_G}[name[3]]
                    w, c0, k, c = "w_in", first + n * IN_COLS, KT, IN_COLS
                elif name == "filter":
                    sp.dma_start(ring[0:HY_FO, s, :], a["hy_f_w3"][l]).then_inc(*slot_loaded[s].rise())
                    return
                elif name == "glu":
                    w, c0, k, c = "s5_w_glu", (n % 2) * D + (n // 2) * 512, WT, 512
                else:
                    w, k, c = {"out_a": ("w_out_a", WT, 512), "mla_q": ("mla_w_q_b", 2, HEADS * QK),
                               "mla_kv": ("mla_w_kv_b", 2, HEADS * (NOPE + VD)), "mla_o": ("mla_w_o", WT, 512),
                               "hy_out": ("hy_w_out", WT, 512), "mix": ("w_mix_out", KT, 256),
                               "xa_q": ("xa_w_q", KT, 256), "xa_kv": ("xa_w_kv", KT, 256),
                               "xa_o": ("xa_w_o", WT, 512)}[name]
                    c0 = n * c
                sp.dma_start(ring[:, s, 0:k * c].rearrange("p (k c) -> p k c", k=k),
                             a[w][l].rearrange("(k p) c -> p k c", p=P)[:, :, c0:c0 + c]).then_inc(*slot_loaded[s].rise())

            def expert(l, e, s, gate_free=None, down_free=None):
                if gate_free:
                    sp.wait_ge(*gate_free)
                for j, w in enumerate(("moe_w_gate", "moe_w_up")):
                    sp.dma_start(ring[:, s + j, :].rearrange("p (k c) -> p k c", k=KT),
                                 a[w][l][e].rearrange("(k p) c -> p k c", p=P)).then_inc(*slot_loaded[s + j].rise())
                if down_free:
                    sp.wait_ge(*down_free)
                sp.dma_start(ring[:, s + 2, :].rearrange("p (k c) -> p k c", k=2),
                             a["moe_w_down"][l][e].rearrange("(k p) c -> p k c", p=P)).then_inc(*slot_loaded[s + 2].rise())

            sp.dma_start(ident[:], a["c_ident"]).then_inc(x_loaded, 16)
            sp.dma_start(view(arena, 0, TT, D), a["x"][0].rearrange("(k p) d -> p k d", p=P)).then_inc(x_loaded, 16)
            sp.dma_start(view(arena, 2048, TT, D), a["mem"][0].rearrange("(k p) d -> p k d", p=P)).then_inc(mem_loaded, 16)
            sp.wait_ge(cleared, 3)
            for l in range(DEPTH):
                load_small(sp, l)

            with sp.Fori(0, DEPTH) as l:
                sp.wait_ge(moe_down.sem, l * EXPERTS + EXPERTS)
                for i, chunk in enumerate(CHUNKS):
                    if i >= RING:
                        sp.wait_ge(*done(l, LAST_USE[CHUNKS[i - RING]]))
                    load(l, i)
                sp.wait_ge(*done(l, ("xa_o", 3)))
                for j in range(TURN):
                    expert(l, j, 3 * j)
                with sp.Fori(1, TURNS) as t:
                    for j in range(TURN):
                        expert(l, t * TURN + j, 3 * j,
                               (moe_up.sem, l * (2 * EXPERTS) + t * (2 * TURN) + (2 * EXPERTS - 2 * TURN + 2 * j + 2)),
                               (moe_down.sem, l * EXPERTS + t * TURN + (EXPERTS - TURN + j + 1)))

        @block.gpsimd
        def _(g):
            for t in (par_rows, phyena[:], xin):
                g.memset(t, 0.0).then_inc(cleared, 1)
            for dst, src in ((small[:], a["c_small"]), (swap[:], a["c_swap"]), (upto[:], a["c_upto"]), (clock[:], a["c_clock"]),
                             (dft[:], a["c_dft"]), (idft[:], a["c_idft"]), (decay[:], a["c_decay"]),
                             (embed, a["c_embed"]), (positions, a["positions"].partition_broadcast(ROPE)),
                             (ends_rows[0:KT], a["mem_norm"].rearrange("(k p) -> k p", p=P)),
                             (ends_rows[KT:2 * KT], a["final_norm"].rearrange("(k p) -> k p", p=P))):
                g.dma_start(dst, src).then_inc(consts_loaded, 16)
            g.wait_ge(start_dve, 9)
            g.wait_ge(start_act, 11)
            for k in range(KT):
                g.tensor_tensor(memT[:, k, :], memT[:, k, :], rstd[:, 1, :], ALU.mult).then_inc(mem_step, 1)
                g.wait_ge(mem_step, 2 * k + 1)
                g.tensor_tensor(memT[:, k, :], memT[:, k, :], ends[:, k:k + 1].to_broadcast([P, T]), ALU.mult).then_inc(mem_step, 1)

            with g.Fori(0, DEPTH) as l:
                def step(ins):
                    ins.then_inc(*pool_step.rise())

                def link(ins):
                    ins.then_inc(*pool_step.rise())
                    g.wait_ge(*pool_step.last(l))

                g.wait_ge(*vec["h"](l, KT))
                for ri, w in enumerate(("s5_b_re", "s5_b_im")):
                    g.dma_start(b_raw[:, ri, :, :], a[w][l].rearrange("d (t g) p h -> (g p) (d t) h", g=2)).then_inc(*s5_loaded.rise())
                for ri, w in enumerate(("s5_c_re", "s5_c_im")):
                    g.dma_start(c_raw[:, ri, :, :], a[w][l].rearrange("d (j q) h p -> (q h) (d j) p", q=8)).then_inc(*s5_loaded.rise())

                for dst, src in ((filter_w[0:HY_EMB, 0, :], a["hy_f_w1"][l]), (filter_w[:, 1, :], a["hy_f_w2"][l]),
                                 (filter_w[:, 2, :], a["hy_f_w2"][l]),
                                 (route_w[:, :, 0:GROUPS], a["moe_w_group"][l].rearrange("(k p) c -> p k c", p=P)),
                                 (route_w[:, :, GROUPS:], a["moe_w_expert"][l].rearrange("(k p) c -> p k c", p=P)),
                                 (bias[:, 0:GROUPS], a["moe_b_group"][bass.ds(l, 1)]), (bias[:, GROUPS:], a["moe_b_expert"][bass.ds(l, 1)])):
                    g.dma_start(dst, src).then_inc(*route_loaded.rise())

                def conv(dst, padded, first, name, tiles, then=None):
                    for k in range(3):
                        step(g.tensor_tensor(conv_t[:, k, :], padded[:, first, k:k + T],
                                             col(name, k * tiles + first).to_broadcast([P, T]), ALU.mult))
                    g.wait_ge(*pool_step.last(l))
                    link(g.tensor_tensor(conv_t[:, 0], conv_t[:, 0], conv_t[:, 1], ALU.add))
                    return g.tensor_tensor(dst, conv_t[:, 0], conv_t[:, 2], ALU.add)

                g.wait_ge(*act["ph"](l, 6))
                for i in range(3 * WT):
                    ins = conv(phyena[:, i, 1:T + 1], phyena, i, "hy_conv", 3 * WT)
                    if i < 3 * WT - 1:
                        link(ins)
                    else:
                        ins.then_inc(*gps["hyena"].rise())
                g.wait_ge(*act["pa"](l, 6))
                link(g.tensor_tensor(xin[:, :, 1:T + 1], p_c, xin[:, :, 1:T + 1], ALU.mult))
                for i in range(WT):
                    link(conv(p_c[:, i, :], xin, i, "conv_a", WT))
                g.tensor_tensor(p_b, p_b, p_c, ALU.mult).then_inc(*gps["a"].rise())

        @block.scalar
        def _(sc):
            def evacuate(l, dst, src, job, sig, func=ACT.Identity, last=True, **kw):
                sc.wait_ge(*done(l, job))
                sc.activation(dst, src, func, **kw).then_inc(*sig.rise())
                if last:
                    reads(job, sig)

            for i in range(8):
                sc.wait_ge(start_pe, i + 1)
                t = (xT, memT)[i // 4]
                sc.activation(t[:, 4 * (i % 2):4 * (i % 2) + 4, (i % 4 // 2) * P:(i % 4 // 2 + 1) * P],
                              psum[:, i, :].rearrange("p (k t) -> p k t", k=4), ACT.Identity).then_inc(start_act, 1)
            sc.wait_ge(consts_loaded, 11 * 16)
            sc.wait_ge(start_pe, 9)
            sc.activation(rstd[:, 1, :], psum[:, 2, 0:T], ACT.Sqrt, bias=eps, scale=1.0 / D).then_inc(start_act, 1)
            sc.wait_ge(start_pe, 10)
            sc.activation(par_all[:].rearrange("p l c -> p (l c)"), psum[:, 0, 0:DEPTH * P], ACT.Identity).then_inc(start_act, 1)
            sc.wait_ge(start_pe, 11)
            sc.activation(ends[:], psum[:, 1, 0:2 * KT], ACT.Identity).then_inc(start_act, 1)
            sc.wait_ge(start_dve, 8)
            sc.activation(waves_r[64:96], rope_t[64:96, 0], ACT.Sin, scale=SIN_SCALE).then_inc(start_act, 1)
            sc.sem_inc(act["silu"].sem, 2)

            def root(l, job, width, tiles=1):
                evacuate(l, rstd[:, 0:tiles, :], bank(job)[:, 0:tiles * T].rearrange("p (a t) -> p a t", a=tiles),
                         job, act["root"], ACT.Sqrt, bias=eps, scale=1.0 / width)

            def attention(l, name, heads, scale, first, o_of, early=0):
                def exps(h):
                    sc.wait_ge(*vec["max"](l, first + h + 1))
                    for q in range(TT):
                        if h >= 2:
                            sc.wait_ge(*done(l, (name + "_tr", h - 2)))
                        evacuate(l, prob[:, h % 2, q, :], bank2((name + "_sc", h))[:, q, :], (name + "_sc", h), act["exp"],
                                 ACT.Exp, last=q == TT - 1, bias=stat[:, 0, h, q:q + 1], scale=scale,
                                 accum_out=stat[:, 1, h, q:q + 1])
                def output(h):
                    dst, src = o_of(h, bank((name + "_pv", h)))
                    evacuate(l, dst, src, (name + "_pv", h), act["o"])

                def values(tiles):
                    for i in tiles:
                        evacuate(l, v_tok[:, i, :], bank((name + "_v", i)), (name + "_v", i), act["v"])

                values(range(early))
                exps(0)
                exps(1)
                values(range(early, TT))
                for h in range(heads):
                    if h >= 2:
                        sc.wait_ge(*done(l, (name + "_pv", h - 2)))
                    evacuate(l, probT[:, h % 2], bank2((name + "_tr", h)), (name + "_tr", h), act["probT"])
                    if h + 2 < heads:
                        exps(h + 2)
                    if h:
                        output(h - 1)
                output(heads - 1)

            with sc.Fori(0, DEPTH) as l:
                def in_a(n):
                    dst = (p_b, p_c, xin[:, :, 1:T + 1])[n // 2][:, 2 * (n % 2):2 * (n % 2) + 2, :]
                    evacuate(l, dst, bank2(("in_a", n)), ("in_a", n), act["pa"])

                root(l, ("mix_sum", 0), D)
                sc.wait_ge(*vec["par"](l, 2))
                sc.activation(s5_w[:, 0, 0:2], s5_rows[:, 2 * P:], ACT.Exp).then_inc(*act["s5_exp"].rise())
                sc.wait_ge(*vec["s5_arg"](l, 1))
                sc.activation(s5_w[:, 3, :], s5_w[:, 1, :], ACT.Exp).then_inc(*act["s5_exp"].rise())
                sc.wait_ge(*vec["s5_arg"](l, 2))
                sc.activation(s5_w[:, 7, :], s5_w[:, 5, :], ACT.Sin, scale=SIN_SCALE).then_inc(*act["s5_sin"].rise())
                sc.activation(s5_w[:, 8, :], s5_w[:, 6, :], ACT.Sin, scale=SIN_SCALE).then_inc(*act["s5_sin"].rise())
                for i in range(2):
                    job = ("in_s", i)
                    if i:
                        in_a(0)
                    evacuate(l, u_fwd[:, 2 * i:2 * i + 2, :], bank2(job), job, act["u"], last=False)
                    evacuate(l, u_bwd[:, 2 * i:2 * i + 2, :], bank2(job)[:, :, ::-1], job, act["u"])
                evacuate(l, s5_col[:], bank(("s5_par", 0))[:, 0:P].rearrange("p (a b) -> p a b", a=4), ("s5_par", 0), act["s5_col"])

                def in_h(n):
                    evacuate(l, phyena[:, 2 * n:2 * n + 2, 1:T + 1], bank2(("in_h", n)), ("in_h", n), act["ph"])

                for n in range(3):
                    in_h(n)
                for i in range(4):
                    evacuate(l, bT[:, 4 * i:4 * i + 4, :], bank(("s5_b", i)).rearrange("p (a b) -> p a b", a=4), ("s5_b", i), act["s5_bT"])
                for i in range(4):
                    evacuate(l, cT[:, 4 * i:4 * i + 4, :], bank(("s5_c", i)).rearrange("p (a b) -> p a b", a=4), ("s5_c", i), act["s5_cT"])

                def waves(i):
                    if i >= 2:
                        sc.wait_ge(*vec["xs"](l, i - 1))
                    th = s5_col[:, 1, i:i + 1]
                    sc.activation(wave[:, i % 2, 0, :], clock[:], ACT.Identity, scale=th).then_inc(*act["turns"].rise())
                    sc.activation(wave[:, i % 2, 1, :], clock[:], ACT.Identity, bias=quarter, scale=th).then_inc(*act["turns"].rise())
                    sc.wait_ge(*vec["phase"](l, i + 1))
                    sc.activation(wave[:, i % 2], wave[:, i % 2], ACT.Sin, scale=-SIN_SCALE).then_inc(*act["wave"].rise())

                sc.wait_ge(*act["s5_cT"](l, 4))
                waves(0)
                for job in IN_ORDER[6:]:
                    name, n = job
                    for i in TILE_SLOTS.get((job, 0), []) + TILE_SLOTS.get((job, 1), []):
                        if i + 1 < ALL_TILES:
                            waves(i + 1)
                    if name == "in_k":
                        evacuate(l, krope_raw[64:96], bank2(job)[64:96], job, act["kraw"])
                    elif name == "in_a":
                        in_a(n)
                    elif name == "in_h":
                        in_h(n)
                    elif name == "in_m":
                        evacuate(l, latent[:, 2 * n:2 * n + 2, :], bank2(job), job, act["latent"])
                    else:
                        for j in range(2):
                            evacuate(l, gate[:, 2 * n + j, :], bank2(job)[:, j, :], job, act["gate"], ACT.Sigmoid, last=j == 1,
                                     bias=col("gate_bias", 2 * n + j))
                for i in range(2):
                    sc.wait_ge(*vec["filt"](l, i + 1))
                    sc.activation(filter_h[:, i, :], filter_h[:, 2, :], ACT.Sin, scale=SIN_SCALE).then_inc(*act["filt"].rise())
                root(l, ("mla_sum", 0), LORA, tiles=2)

                for i in range(4):
                    evacuate(l, qT[0:QK, 2 * i:2 * i + 2, :], bank2(("mla_q", i))[0:QK], ("mla_q", i), act["qcopy"])
                for i in range(4):
                    evacuate(l, kT[0:NOPE, 2 * i:2 * i + 2, :], bank2(("mla_k", i))[0:NOPE], ("mla_k", i), act["knope"])
                def o_mla(h, b):
                    rows = slice(VD * (h % 2), VD * (h % 2) + VD)
                    return oT[rows, h // 2, :], b[rows, 0:T]

                attention(l, "mla", HEADS, MLA_SCALE, 0, o_mla)

                sc.wait_ge(*vec["y"](l, 8))
                sc.activation(ys[:], ys[:], ACT.Gelu_apprx_tanh).then_inc(*act["gelu"].rise())

                def tap_spectrum(o):
                    for i, dst in enumerate((k_cos[:, 0], k_cos[:, 1], k_sin[:, 0], k_sin[:, 1])):
                        evacuate(l, dst, bank((f"kd{o}", i)), (f"kd{o}", i), act["k_dft"])
                    evacuate(l, k_scale[:], bank((f"kn{o}", 0))[:, 0:WT], (f"kn{o}", 0), act["k_root"], ACT.Sqrt, bias=eps)

                def signal(o):
                    for i in range(TT):
                        evacuate(l, seq_tok[:, i, :], bank((f"vt{o}", i)), (f"vt{o}", i), act["seq"])

                def glu(i):
                    if i >= 2:
                        sc.wait_ge(*vec["merge"](l, 8 + i - 1))
                    evacuate(l, glu_s[i % 2], bank2(("glu", 2 * i + 1)), ("glu", 2 * i + 1), act["glu"], ACT.Sigmoid)

                tap_spectrum(0)
                signal(0)
                glu(0)
                glu(1)
                signal(1)
                tap_spectrum(1)
                glu(2)
                glu(3)

                def xa_key(n):
                    evacuate(l, kT[:, 2 * n:2 * n + 2, :], bank2(("xa_k", n)), ("xa_k", n), act["xa_qk"])

                xa_key(0)
                root(l, ("xa_sum", 0), D)
                xa_key(1)
                for n in range(2):
                    evacuate(l, qT[:, 2 * n:2 * n + 2, :], bank2(("xa_q", n)), ("xa_q", n), act["xa_qk"])
                attention(l, "xa", XH, XA_SCALE, HEADS, lambda h, b: (oT[:, h, :], b[:, 0:T]), early=1)

                root(l, ("moe_sum", 0), D)
                for i in range(4):
                    evacuate(l, h_tok[:, i // 2, (i % 2) * 512:(i % 2 + 1) * 512], bank(("h_tok", i)), ("h_tok", i), act["h_tok"])
                sc.wait_ge(*vec["rmax"](l, 1))
                sc.activation(r["gdiff"], r["gdiff"], ACT.Exp).then_inc(*act["rexp"].rise())
                sc.wait_ge(*vec["r12"](l, 1))
                sc.activation(r["ex"], r["ex"], ACT.Exp).then_inc(*act["rexp"].rise())
                for k in range(KT):
                    evacuate(l, hg[:, k, :], bank(("gather", k))[:, 0:GROUPS * CAP], ("gather", k), act["gather"])
                for i in range(2):
                    evacuate(l, back[0:CAP, 2 * i:2 * i + 2, :], bank2(("back", i))[0:CAP], ("back", i), act["back"])
                evacuate(l, cw_slot[0:CAP], bank(("cw", 0))[0:CAP, 0:EXPERTS], ("cw", 0), act["cw"])

                def expert_gates(base, t, width):
                    for j in range(TURN):
                        for f in range(2):
                            n = 2 * j + f
                            sc.wait_ge(moe_gate.sem, l * (2 * EXPERTS) + t * (2 * TURN) + (base + n + 1))
                            sc.wait_ge(vec["hid"].sem, l * (2 * EXPERTS) + t * (2 * TURN) + (base + n + 1))
                            sc.activation(silu[:, f, 0:width], psum[:, 2 * f, 0:width], ACT.Silu).then_inc(act["silu"].sem, 1)

                flag = sc.value_load(crowded[0:1, 0:1], min_val=0, max_val=1)
                with sc.If(flag < 1):
                    sc.sem_inc(dense_cw_out.sem, EXPERTS // 2)
                    with sc.Fori(0, TURNS) as t:
                        expert_gates(0, t, CAP)
                with sc.Else():
                    for i in range(EXPERTS // 2):
                        sc.wait_ge(*dense_cw(l, i + 1))
                        sc.activation(gate[:, 2 * i:2 * i + 2, :], psum[:, 4 + i % 4, :].rearrange("p (a b) -> p a b", a=2),
                                      ACT.Identity).then_inc(*dense_cw_out.rise())
                    with sc.Fori(0, TURNS) as t:
                        expert_gates(0, t, T)

            sc.wait_ge(end_pe, 1)
            sc.activation(rstd[:, 0, :], psum[:, 4, 0:T], ACT.Sqrt, bias=eps, scale=1.0 / D).then_inc(end_act, 1)
            o_tok = view(arena, 0, TT, D)
            for n, i in enumerate((0, 2, 1, 3)):
                cols = slice((i % 2) * 512, (i % 2 + 1) * 512)
                sc.wait_ge(end_pe, 2 + n)
                sc.activation(o_tok[:, i // 2, cols], psum[:, i, :], ACT.Identity).then_inc(end_act, 1)
                sc.wait_ge(end_act, 2 + n)
                sc.dma_start(out[0].rearrange("(k p) d -> p k d", p=P)[:, i // 2, cols], o_tok[:, i // 2, cols]).then_inc(stored, 16)
            sc.wait_ge(stored, 4 * 16)

        @block.vector
        def _(v):
            chain = [0]

            def start(ins):
                chain[0] += 1
                ins.then_inc(start_dve, 1)
                v.wait_ge(start_dve, chain[0])

            start(v.memset(ones[:], 1.0))
            start(v.memset(zeros[:], 0.0))
            v.wait_ge(start_act, 4)
            for i in range(4):
                x = xT[:, 2 * i:2 * i + 2, :]
                v.tensor_tensor(x_sq[:, 2 * i:2 * i + 2, :], x, x, ALU.mult).then_inc(vec["square"].sem, 1)
            v.wait_ge(start_act, 8)
            start(v.tensor_tensor(hT[:], memT[:], memT[:], ALU.mult))
            v.wait_ge(consts_loaded, 11 * 16)
            ang, whole = rope_t[64:96, 0], rope_t[64:96, 1]
            start(v.tensor_copy(ang[:, 1, :], positions))
            start(v.tensor_scalar(ang[:, 1, :], ang[:, 1, :], inv_turns, None, ALU.mult))
            start(v.tensor_scalar(ang[:, 0, :], ang[:, 1, :], 0.25, None, ALU.add))
            start(v.tensor_scalar(whole, ang, ROUND, ROUND, ALU.add, ALU.subtract))
            start(v.tensor_tensor(ang, ang, whole, ALU.subtract))
            v.wait_ge(start_act, 9)
            start(v.reciprocal(rstd[:, 1, :], rstd[:, 1, :]))
            v.wait_ge(start_act, 12)
            start(v.tensor_scalar(waves_r[64:96, 1, :], waves_r[64:96, 1, :], sin_sign, None, ALU.mult))
            v.sem_inc(vec["hid"].sem, 2)
            v.sem_inc(vec["y_slot"].sem, 1)

            def tile2(ap, n=2):
                return ap.unsqueeze(1).to_broadcast([ap.shape[0], n, ap.shape[-1]])

            with v.Fori(0, DEPTH) as l:
                def step(ins, *jobs):
                    ins.then_inc(*vector_step.rise())
                    for job in jobs:
                        reads(job, vector_step)

                def link(ins, *jobs):
                    step(ins, *jobs)
                    v.wait_ge(*vector_step.last(l))

                def result(name, ins, *jobs, settle=True):
                    ins.then_inc(*vec[name].rise())
                    for job in jobs:
                        reads(job, vec[name])
                    if settle:
                        v.wait_ge(*vec[name].last(l))

                def square_x(i):
                    x = xT[:, 2 * i:2 * i + 2, :]
                    result("square", v.tensor_tensor(x_sq[:, 2 * i:2 * i + 2, :], x, x, ALU.mult))

                def norm_x(root_n, gain):
                    v.wait_ge(*act["root"](l, root_n))
                    link(v.reciprocal(rstd[:, 0, :], rstd[:, 0, :]))
                    for k in range(KT):
                        result("h", v.scalar_tensor_tensor(hT[:, k, :], xT[:, k, :], col(gain, k), rstd[:, 0, :],
                                                           ALU.mult, ALU.mult), settle=k == KT - 1)

                def add_x(job, i):
                    v.wait_ge(*done(l, job))
                    result("x", v.tensor_tensor(xT[:, 2 * i:2 * i + 2, :], xT[:, 2 * i:2 * i + 2, :], bank2(job), ALU.add), job)
                    square_x(i)

                for c in (0, T + 1):
                    step(v.memset(xin[:, :, c:c + 1], 0.0))
                result("par", v.tensor_copy(par[:], par_all[:, bass.ds(l, 1), :].rearrange("p o a -> p (o a)")))
                result("par", v.tensor_copy(s5_rows, s5_all[:, bass.ds(l, 1), :].rearrange("p o a -> p (o a)")))
                norm_x(1, "mix_norm")

                lre, lim = s5_rows[:, 0:P], s5_rows[:, P:2 * P]

                def w(i):
                    return s5_w[:, i, :]

                v.wait_ge(*act["s5_exp"](l, 1))
                for g in range(2):
                    half_g = slice(64 * g, 64 * g + 64)
                    step(v.tensor_scalar(w(2)[:, half_g], lim[:, half_g], s5_w[:, 0, g:g + 1], INV_TWO_PI, ALU.mult, ALU.mult))
                step(v.tensor_scalar(w(1)[:, 0:64], lre[:, 0:64], s5_w[:, 0, 0:1], None, ALU.mult))
                v.wait_ge(*vector_step.last(l))
                result("s5_arg", v.tensor_scalar(w(1)[:, 64:P], lre[:, 64:P], s5_w[:, 0, 1:2], None, ALU.mult))
                link(v.tensor_scalar(w(4), w(2), ROUND, ROUND, ALU.add, ALU.subtract))
                link(v.tensor_tensor(w(5), w(2), w(4), ALU.subtract))
                link(v.tensor_scalar(w(6), w(5), 0.25, None, ALU.add))
                link(v.tensor_scalar(w(4), w(6), ROUND, ROUND, ALU.add, ALU.subtract))
                result("s5_arg", v.tensor_tensor(w(6), w(6), w(4), ALU.subtract))
                link(v.tensor_tensor(w(11), lre, lre, ALU.mult))
                link(v.tensor_tensor(w(2), lim, lim, ALU.mult))
                link(v.tensor_tensor(w(11), w(11), w(2), ALU.add))
                link(v.reciprocal(w(11), w(11)))
                v.wait_ge(*act["s5_sin"](l, 2))
                link(v.tensor_tensor(w(9), w(3), w(8), ALU.mult))
                link(v.tensor_scalar(w(9), w(9), -1.0, None, ALU.add))
                link(v.tensor_tensor(w(10), w(3), w(7), ALU.mult))
                link(v.tensor_tensor(w(2), w(9), lre, ALU.mult))
                link(v.tensor_tensor(w(4), w(10), lim, ALU.mult))
                link(v.tensor_tensor(w(2), w(2), w(4), ALU.add))
                link(v.tensor_tensor(w(2), w(2), w(11), ALU.mult))
                link(v.tensor_tensor(w(4), w(10), lre, ALU.mult))
                link(v.tensor_tensor(w(1), w(9), lim, ALU.mult))
                link(v.tensor_tensor(w(4), w(4), w(1), ALU.subtract))
                result("s5_rows", v.tensor_tensor(w(4), w(4), w(11), ALU.mult))

                link(v.memset(b_blk, 0.0))
                v.wait_ge(*s5_loaded(l, 4))
                v.wait_ge(*act["s5_col"](l, 1))
                cre, cim = (s5_col[:, i, :].unsqueeze(2).to_broadcast([P, ALL_TILES, 16]) for i in (2, 3))
                for ri in range(2):
                    step(v.tensor_tensor(b_tmp[:, 0], b_raw[:, 0], cre if ri == 0 else cim, ALU.mult))
                    link(v.tensor_tensor(b_tmp[:, 1], b_raw[:, 1], cim if ri == 0 else cre, ALU.mult))
                    for g in range(2):
                        rows = slice(64 * g, 64 * g + 64)
                        ins = v.tensor_tensor(b_blk[rows, ri, :, g, :], b_tmp[rows, 0], b_tmp[rows, 1],
                                              ALU.subtract if ri == 0 else ALU.add)
                        if ri == 1 and g == 1:
                            result("s5_b", ins)
                        else:
                            link(ins)
                for ri in range(2):
                    for g in range(2):
                        result("s5_c", v.tensor_scalar(c_blk[:, ri, :, g, :], c_raw[:, ri], half[g], 1.0 - 2.0 * ri, ALU.mult, ALU.mult))

                def near(i):
                    v.wait_ge(*act["turns"](l, 2 * i + 2))
                    step(v.tensor_scalar(turn_t, wave[:, i % 2], ROUND, ROUND, ALU.add, ALU.subtract))

                def phase(i):
                    result("phase", v.tensor_tensor(wave[:, i % 2], turn_t, wave[:, i % 2], ALU.subtract), settle=False)

                def y_of(g):
                    v.wait_ge(*s5_y(l, 4 * g + 4))
                    y = psum[:, 2 + g % 2, 0:T]
                    if g < WT:
                        result("y", v.scalar_tensor_tensor(ys[:, g, :], u_fwd[:, g, :], col("s5_d", g), y, ALU.mult, ALU.add))
                    else:
                        v.wait_ge(*vec["y"](l, g - WT + 1))
                        result("y", v.tensor_tensor(ys[:, g - WT, :], ys[:, g - WT, :], y[:, ::-1], ALU.add))

                near(0)
                v.wait_ge(*vector_step.last(l))
                phase(0)
                for i in range(ALL_TILES):
                    v.wait_ge(*act["wave"](l, i + 1))
                    v.wait_ge(*s5_bu(l, i + 1))
                    sin, cos = wave[:, i % 2, 0, :], wave[:, i % 2, 1, :]
                    bu = psum[:, i % 2, :].rearrange("p (a b) -> p a b", a=2)
                    step(v.tensor_tensor(prod[:, 0], bu, tile2(cos), ALU.mult))
                    result("bu_used", v.tensor_tensor(prod[:, 1], bu[:, ::-1, :], tile2(sin), ALU.mult), settle=False)
                    if i + 1 < ALL_TILES:
                        near(i + 1)
                    v.wait_ge(*vector_step.last(l))
                    v.wait_ge(*vec["bu_used"].last(l))
                    step(v.tensor_tensor(zst[:, 0], prod[:, 0, 0], prod[:, 1, 0], ALU.add))
                    step(v.tensor_tensor(zst[:, 1], prod[:, 0, 1], prod[:, 1, 1], ALU.subtract))
                    if i + 1 < ALL_TILES:
                        phase(i + 1)
                    v.wait_ge(*vector_step.last(l))
                    decays = s5_col[:, 0, i:i + 1].to_broadcast([P, T])
                    step(v.tensor_tensor_scan(prod[:, 0, 0], decays, zst[:, 0], 0.0, ALU.mult, ALU.add))
                    link(v.tensor_tensor_scan(prod[:, 0, 1], decays, zst[:, 1], 0.0, ALU.mult, ALU.add))
                    step(v.tensor_tensor(zst, prod[:, 0], tile2(cos), ALU.mult))
                    link(v.tensor_tensor(prod[:, 1], prod[:, 0, ::-1, :], tile2(sin), ALU.mult))
                    if i >= 2:
                        v.wait_ge(*s5_y(l, i - 1))
                    step(v.tensor_tensor(xs[:, i % 2, 0], zst[:, 0], prod[:, 1, 0], ALU.subtract))
                    result("xs", v.tensor_tensor(xs[:, i % 2, 1], zst[:, 1], prod[:, 1, 1], ALU.add))
                    if i % 4 == 2 and i > 5:
                        y_of(i // 4 - 1)
                y_of(7)

                def merge(job, b, i):
                    g = gate[:, b * KT + 2 * i:b * KT + 2 * i + 2, :]
                    m = merged[:, 2 * i:2 * i + 2, :]
                    v.wait_ge(*done(l, job))
                    v.wait_ge(*act["gate"](l, KT * (b + 1)))
                    if b == 0:
                        result("merge", v.tensor_tensor(m, g, bank2(job), ALU.mult), job)
                        return
                    if b == 1:
                        v.wait_ge(*act["glu"](l, i + 1))
                        link(v.tensor_tensor(mix_t, bank2(job), glu_s[i % 2], ALU.mult), job)
                        link(v.tensor_tensor(mix_t, mix_t, g, ALU.mult))
                    else:
                        link(v.tensor_tensor(mix_t, g, bank2(job), ALU.mult), job)
                    result("merge", v.tensor_tensor(m, m, mix_t, ALU.add))

                v.wait_ge(*act["latent"](l, 2))
                result("square", v.tensor_tensor(oT, latent[:], latent[:], ALU.mult))
                for i, b in enumerate(("b1", "b2")):
                    v.wait_ge(*done(l, ("filt", i)))
                    arg, whole = filter_h[:, 2, :], filter_h[:, 3, :]
                    rows = slice(0, HY_FO)
                    link(v.tensor_scalar(arg, bank(("filt", i))[rows, 0:T], col(b, 0, rows), col("freq", 0, rows),
                                         ALU.add, ALU.mult), ("filt", i))
                    link(v.tensor_scalar(arg, arg, INV_TWO_PI, None, ALU.mult))
                    link(v.tensor_scalar(whole, arg, ROUND, ROUND, ALU.add, ALU.subtract))
                    result("filt", v.tensor_tensor(arg, arg, whole, ALU.subtract))
                v.wait_ge(*act["root"](l, 2))
                link(v.reciprocal(rstd[:], rstd[:]))
                for k in range(4):
                    result("lat", v.scalar_tensor_tensor(latent[:, k, :], latent[:, k, :],
                                                         col(("mla_q_norm", "mla_kv_norm")[k // 2], k % 2),
                                                         rstd[:, k // 2, :], ALU.mult, ALU.mult))
                cos, sin = waves_r[64:96, 0, :], waves_r[64:96, 1, :]
                one, two = rope_t[64:96, 0], rope_t[64:96, 1]
                step(v.tensor_tensor(one[:, 0, :], krope_raw[64:96, 0, :], cos, ALU.mult))
                link(v.tensor_tensor(two[:, 0, :], krope_raw[64:96, 1, :], sin, ALU.mult))
                result("k", v.tensor_tensor(kT[64:96], tile2(one[:, 0, :], HEADS), tile2(two[:, 0, :], HEADS), ALU.add))
                for i in range(4):
                    for j in ((0, 1), (2, 3), (), ())[i]:
                        merge(("out_a", j), 0, j)
                    v.wait_ge(*act["qcopy"](l, i + 1))
                    link(v.tensor_tensor(one, qT[64:96, 2 * i:2 * i + 2, :], tile2(cos), ALU.mult))
                    v.wait_ge(*done(l, ("mla_qs", i)))
                    link(v.tensor_tensor(two, bank2(("mla_qs", i))[64:96], tile2(sin), ALU.mult), ("mla_qs", i))
                    result("rope_q", v.tensor_tensor(qT[64:96, 2 * i:2 * i + 2, :], one, two, ALU.add))

                def attention(name, heads, scale, first, between=None):
                    def maxima(h):
                        v.wait_ge(*done(l, (name + "_sc", h)))
                        link(v.tensor_reduce(stat[:, 2, h, :], bank2((name + "_sc", h)), X_AXIS, ALU.max))
                        result("max", v.tensor_scalar(stat[:, 0, h, :], stat[:, 2, h, :], -scale, None, ALU.mult))
                    maxima(0)
                    maxima(1)
                    for h in range(heads):
                        v.wait_ge(*act["exp"](l, 2 * (first + h) + 2))
                        link(v.reciprocal(stat[:, 1, h, :], stat[:, 1, h, :]))
                        for q in range(TT):
                            result("p", v.tensor_scalar(prob[:, h % 2, q, :], prob[:, h % 2, q, :], stat[:, 1, h, q:q + 1],
                                                        None, ALU.mult), settle=q == TT - 1)
                        if h + 2 < heads:
                            maxima(h + 2)
                        if between:
                            between(h)

                def decayed(o, i):
                    v.wait_ge(*done(l, (f"kf{o}", i)))
                    result("k_fb", v.tensor_tensor(k_fb[:, i // 2, i % 2, :], bank((f"kf{o}", i)), decay[:, i % 2, :],
                                                   ALU.mult), (f"kf{o}", i))

                attention("mla", HEADS, MLA_SCALE, 0, lambda h: decayed(0, h - 1) if h in KF_HEADS else None)

                def even_odd_taps(o):
                    link(v.memset(k_fb[0:1, 1, 0, :], 0.0))
                    result("k_sd", v.tensor_tensor(k_sd[:, 0], k_fb[:, 0], k_fb[:, 1], ALU.add), settle=False)
                    result("k_sd", v.tensor_tensor(k_sd[:, 1], k_fb[:, 0], k_fb[:, 1], ALU.subtract))

                def squared_taps():
                    step(v.tensor_tensor(k_sq, k_fb[:, 0], k_fb[:, 0], ALU.mult))
                    link(v.tensor_tensor(spec[:, 0:2], k_fb[:, 1], k_fb[:, 1], ALU.mult))
                    result("k_sq", v.tensor_tensor(k_sq, k_sq, spec[:, 0:2], ALU.add))

                def tap_spectrum(o):
                    v.wait_ge(*act["k_dft"](l, 4 * o + 4))
                    link(v.tensor_copy(k_nyq, k_cos[:, 0]))
                    v.wait_ge(*done(l, (f"kd{o}", 4)))
                    step(v.tensor_copy(k_nyq[0:1], bank((f"kd{o}", 4))[0:1]), (f"kd{o}", 4))
                    link(v.memset(k_sin[0:1, 0, :], 0.0))
                    v.wait_ge(*act["k_root"](l, o + 1))
                    link(v.reciprocal(k_scale[:], k_scale[:]))

                def spectrum(o):
                    for i in range(2):
                        c, s = (f"vd{o}", 2 * i), (f"vd{o}", 2 * i + 1)
                        v.wait_ge(*done(l, s))
                        step(v.tensor_tensor(spec[:, i], bank(c), k_cos[:, i], ALU.mult))
                        step(v.tensor_tensor(spec[:, 2 + i], bank(c), k_sin[:, i], ALU.mult), c)
                        step(v.tensor_tensor(spec_t[:, 0], bank(s), k_sin[:, i], ALU.mult))
                        link(v.tensor_tensor(spec_t[:, 1], bank(s), k_nyq if i == 0 else k_cos[:, 1], ALU.mult), s)
                        result("spec", v.tensor_tensor(spec[:, i], spec[:, i], spec_t[:, 0], ALU.subtract), settle=False)
                        result("spec", v.tensor_tensor(spec[:, 2 + i], spec[:, 2 + i], spec_t[:, 1], ALU.add))

                def convolved(o):
                    if o == 0:
                        v.wait_ge(*gps["hyena"](l, 1))
                    for i in range(2):
                        job = (f"vi{o}", i)
                        v.wait_ge(*done(l, job))
                        for j in range(2):
                            ch = 2 * i + j
                            u = phyena[:, ch, 1:T + 1] if o == 0 else z_hy[:, ch, :]
                            link(v.tensor_scalar(mix_t[:, j, :], u, col("hy_bias", o * WT + ch), None, ALU.mult))
                            link(v.scalar_tensor_tensor(mix_t[:, j, :], bank2(job)[:, j, :], k_scale[:, ch:ch + 1],
                                                        mix_t[:, j, :], ALU.mult, ALU.add), *([job] * j))
                        xg = phyena[:, WT * (o + 1) + 2 * i:WT * (o + 1) + 2 * i + 2, 1:T + 1]
                        result("z", v.tensor_tensor(z_hy[:, 2 * i:2 * i + 2, :], xg, mix_t, ALU.mult))

                v.wait_ge(*done(l, ("mla_pv", HEADS - 1)))
                even_odd_taps(0)
                merge(("mla_o", 0), 2, 0)
                squared_taps()
                merge(("mla_o", 1), 2, 1)
                tap_spectrum(0)
                merge(("mla_o", 2), 2, 2)
                merge(("mla_o", 3), 2, 3)
                spectrum(0)
                for i in range(4):
                    decayed(1, i)
                convolved(0)
                even_odd_taps(1)
                merge(("glu", 0), 1, 0)
                squared_taps()
                merge(("glu", 2), 1, 1)
                tap_spectrum(1)
                spectrum(1)
                merge(("glu", 4), 1, 2)
                convolved(1)
                merge(("glu", 6), 1, 3)
                for i in range(4):
                    merge(("hy_out", i), 3, i)
                for i in range(4):
                    add_x(("mix", i), i)

                norm_x(3, "xa_norm")
                attention("xa", XH, XA_SCALE, HEADS)
                for i in range(4):
                    add_x(("xa_o", i), i)

                norm_x(4, "moe_norm")

                def spread_over(ap, n):
                    return ap.to_broadcast([P, TT, n])

                def first_best(best, of, key, m, oh, rank, n):
                    link(v.tensor_reduce(best, of, X_AXIS, ALU.max))
                    link(v.tensor_tensor(key, of, spread_over(best, n), ALU.is_equal))
                    link(v.tensor_tensor(key, key, rank.unsqueeze(1).to_broadcast([P, TT, n]), ALU.mult))
                    link(v.tensor_reduce(m, key, X_AXIS, ALU.max))
                    link(v.tensor_tensor(oh, key, spread_over(m, n), ALU.is_equal))

                v.wait_ge(*done(l, ("route", 0)))
                link(v.tensor_copy(r["logits"], bank(("route", 0))[:, 0:P].rearrange("p (t c) -> p t c", t=TT)[:, :, 0:GROUPS + EXPERTS]),
                     ("route", 0))
                gl = r["logits"][:, :, 0:GROUPS]
                el = r["logits"][:, :, GROUPS:]
                first_best(r["gmax"], gl, r["key4"], r["m4"], r["oh4"], rank4, GROUPS)
                result("oh", v.tensor_scalar(r["oh4"], r["oh4"], 1.0, None, ALU.mult))
                result("rmax", v.tensor_tensor(r["gdiff"], gl, spread_over(r["gmax"], GROUPS), ALU.subtract))
                v.wait_ge(*done(l, ("rank", 0)))
                step(v.tensor_scalar(r["rank"], bank(("rank", 0))[:, 0:TT * GROUPS].rearrange("p (t g) -> p t g", t=TT),
                                     -1.0, None, ALU.add))
                link(v.tensor_copy(r["count"][:, 0, :], bank(("rank", 0))[:, TT * GROUPS:(TT + 1) * GROUPS]), ("rank", 0))
                for t in range(TT):
                    for g in range(GROUPS):
                        result("pick", v.tensor_scalar(pick[:, t, g, :], clock[:, 0:CAP], r["rank"][:, t, g:g + 1],
                                                       r["oh4"][:, t, g:g + 1], ALU.is_equal, ALU.mult), settle=False)
                link(v.tensor_reduce(r["m4"][:, 0, :], r["count"][:, 0, :], X_AXIS, ALU.max))
                result("flag", v.tensor_scalar(crowded[:], r["m4"][0:1, 0, :], float(CAP), None, ALU.is_gt))
                for t in range(TT):
                    e4 = r["e4"][:, t, :].rearrange("p (g e) -> p g e", g=GROUPS)
                    link(v.tensor_tensor(e4, el[:, t, :].rearrange("p (g e) -> p g e", g=GROUPS),
                                         r["oh4"][:, t, :].unsqueeze(2).to_broadcast([P, GROUPS, PER_GROUP]), ALU.mult))
                    link(v.tensor_reduce(r["es"][:, t, :], e4.rearrange("p g e -> p e g"), X_AXIS, ALU.add))
                first_best(r["v1"], r["es"], r["key8"], r["m8"], r["oh1"], rank8, PER_GROUP)
                link(v.scalar_tensor_tensor(r["es2"], r["oh1"], -1e30, r["es"], ALU.mult, ALU.add))
                first_best(r["v2"], r["es2"], r["key8"], r["m8"], r["oh2"], rank8, PER_GROUP)
                result("r12", v.tensor_tensor(r["ex"], r["v2"], r["v1"], ALU.subtract))
                v.wait_ge(*act["rexp"](l, 2))
                link(v.tensor_reduce(r["gsum"], r["gdiff"], X_AXIS, ALU.add))
                link(v.reciprocal(r["gsum"], r["gsum"]))
                link(v.tensor_scalar(r["w1"], r["ex"], 1.0, None, ALU.add))
                link(v.reciprocal(r["w1"], r["w1"]))
                link(v.tensor_tensor(r["w1"], r["w1"], r["gsum"], ALU.mult))
                link(v.tensor_tensor(r["w2"], r["w1"], r["ex"], ALU.mult))
                link(v.tensor_tensor(r["c8"], r["oh1"], spread_over(r["w1"], PER_GROUP), ALU.mult))
                link(v.tensor_tensor(r["t8"], r["oh2"], spread_over(r["w2"], PER_GROUP), ALU.mult))
                link(v.tensor_tensor(r["c8"], r["c8"], r["t8"], ALU.add))
                for t in range(TT):
                    ins = v.tensor_tensor(r["comb"][:, t, :].rearrange("p (g e) -> p g e", g=GROUPS),
                                          r["oh4"][:, t, :].unsqueeze(2).to_broadcast([P, GROUPS, PER_GROUP]),
                                          r["c8"][:, t, :].unsqueeze(1).to_broadcast([P, GROUPS, PER_GROUP]), ALU.mult)
                    if t == 0:
                        link(ins)
                    else:
                        result("comb", ins, settle=False)

                def gate_times_up(dst, done_sem, n, j, t, f, width):
                    base = l * (2 * EXPERTS) + t * (2 * TURN)
                    v.wait_ge(act["silu"].sem, base + (2 + n + 1))
                    v.wait_ge(moe_up.sem, base + (2 * EXPERTS + n + 1))
                    v.tensor_tensor(dst, silu[:, f, 0:width], psum[:, 2 * f + 1, 0:width], ALU.mult).then_inc(done_sem, 1)

                def dense_values(t):
                    for j in range(TURN):
                        for f in range(2):
                            n = 2 * j + f
                            base = l * (2 * EXPERTS) + t * (2 * TURN)
                            v.wait_ge(*dense_cw_out(l, EXPERTS // 2))
                            gate_times_up(hid_t[:, f], hid_half.sem, n, j, t, f, T)
                            v.wait_ge(hid_half.sem, base + (n + 1))
                            v.wait_ge(moe_down.sem, l * EXPERTS + t * TURN + (EXPERTS + j))
                            w = gate[:, bass.ds(t * TURN + j, 1), :].rearrange("p o t -> p (o t)")
                            v.tensor_tensor(hid[:, f], hid_t[:, f], w, ALU.mult).then_inc(vec["hid"].sem, 1)

                flag = v.value_load(crowded[0:1, 0:1], min_val=0, max_val=1)
                with v.If(flag < 1):
                    v.sem_inc(hid_half.sem, 2 * EXPERTS)
                    v.memset(y_slot[0:CAP], 0.0).then_inc(*vec["y_slot"].rise())
                    for g in range(GROUPS):
                        with v.Fori(0, GROUP_TURNS) as t:
                            for j in range(TURN):
                                e = PER_GROUP * g + j
                                v.wait_ge(moe_down.sem, l * EXPERTS + t * TURN + (EXPERTS + e))
                                for f in range(2):
                                    gate_times_up(hid[:, f, 0:CAP], vec["hid"].sem, 2 * e + f, j, t, f, CAP)
                                v.wait_ge(moe_down.sem, l * EXPERTS + t * TURN + (EXPERTS + e + 1))
                                v.wait_ge(vec["y_slot"].sem, l * (1 + EXPERTS) + t * TURN + (1 + e + 1))
                                if g == 0 and j == 0:
                                    v.wait_ge(*act["cw"](l, 1))
                                v.scalar_tensor_tensor(y_slot[0:CAP, g, :], psum[0:CAP, 4 + 2 * j:6 + 2 * j, :].rearrange("p a b -> p (a b)"),
                                                       cw_slot[0:CAP, bass.ds(t * TURN + e, 1)], y_slot[0:CAP, g, :],
                                                       ALU.mult, ALU.add).then_inc(vec["y_slot"].sem, 1)
                with v.Else():
                    v.sem_inc(vec["y_slot"].sem, 1 + EXPERTS)
                    with v.Fori(0, TURNS) as t:
                        dense_values(t)
                v.wait_ge(*moe_down(l, EXPERTS))
                for i in range(4):
                    v.wait_ge(*moe_out(l, i + 1))
                    acc = psum[:, 4 + i, :].rearrange("p (a b) -> p a b", a=2)
                    result("x", v.tensor_tensor(xT[:, 2 * i:2 * i + 2, :], xT[:, 2 * i:2 * i + 2, :], acc, ALU.add))
                    square_x(i)

            v.wait_ge(end_act, 1)
            v.reciprocal(rstd[:, 0, :], rstd[:, 0, :]).then_inc(end_dve, 1)
            v.wait_ge(end_dve, 1)
            for k in range(KT):
                v.scalar_tensor_tensor(hT[:, k, :], xT[:, k, :], ends[:, KT + k:KT + k + 1], rstd[:, 0, :],
                                       ALU.mult, ALU.mult).then_inc(end_dve, 1)

        @block.tensor
        def _(pe):
            pe.sem_inc(moe_up.sem, 2 * EXPERTS)
            pe.sem_inc(moe_down.sem, EXPERTS)
            pe.wait_ge(x_loaded, 2 * 16)
            for i in range(8):
                if i == 4:
                    pe.wait_ge(mem_loaded, 16)
                src = view(arena, 2048 * (i // 4), TT, D)
                for k in range(4):
                    c = (4 * (i % 2) + k) * P
                    ins = pe.transpose(psum[:, i, k * P:(k + 1) * P], src[:, i % 4 // 2, c:c + P], ident[:])
                ins.then_inc(start_pe, 1)
            pe.wait_ge(start_act, 3)
            pe.wait_ge(start_dve, 3)
            for k in range(KT):
                ins = pe.matmul(psum[:, 2, 0:T], ones[:], hT[:, k, :], start=k == 0, stop=k == KT - 1)
            ins.then_inc(start_pe, 1)
            pe.wait_ge(small_loaded, DEPTH * 16 * 16)
            for l in range(DEPTH):
                ins = pe.transpose(psum[:, 0, l * P:(l + 1) * P], par_rows[:, l, :], ident[:])
            ins.then_inc(start_pe, 1)
            pe.wait_ge(consts_loaded, 11 * 16)
            pe.transpose(psum[:, 1, 0:2 * KT], ends_rows, ident[0:2 * KT, 0:2 * KT]).then_inc(start_pe, 1)

            with pe.Fori(0, DEPTH) as l:
                def begin(job):
                    if BANK_BEFORE[job]:
                        for sig, n in freed[BANK_BEFORE[job]]:
                            pe.wait_ge(*sig(l, n))
                    elif BANK[job] < 4:
                        pe.wait_ge(*(vec["bu_used"](l, ALL_TILES) if BANK[job] < 2 else vec["y"](l, 8)))
                    return bank(job)

                def finish(ins):
                    ins.then_inc(*product.rise())

                def chunk(name, n=0):
                    i = CHUNK_AT[(name, n)]
                    pe.wait_ge(*slot_loaded[i % RING](l, dmas_upto[(name, n)]))
                    return ring[:, i % RING, :]

                def split(slot, k, c):
                    return slot[:, 0:k * c].rearrange("p (k c) -> p k c", k=k)

                def project(out, w, rhs, nk, c0, m=P, tile_ready=None):
                    for k in range(nk):
                        if tile_ready and tile_ready(k):
                            pe.wait_ge(*tile_ready(k))
                        ins = pe.matmul(out, w[:, k, c0:c0 + m], rhs[:, k, :], start=k == 0, stop=k == nk - 1)
                    return ins

                def pair(job, w, rhs, nk, c0, tile_ready=None, between=None):
                    b = begin(job)
                    for j in range(2):
                        if between:
                            between(j)
                        ins = project(b[:, j * T:(j + 1) * T], w, rhs, nk, c0 + j * P, tile_ready=None if j else tile_ready)
                    finish(ins)

                def total_x(job, squares):
                    b = begin(job)
                    for k in range(KT):
                        if k % 2 == 0:
                            pe.wait_ge(*vec["square"](l, squares + k // 2 + 1))
                        ins = pe.matmul(b[:, 0:T], ones[:], x_sq[:, k, :], start=k == 0, stop=k == KT - 1)
                    finish(ins)

                def turn(job, tiles):
                    b = begin(job)
                    for j, t in enumerate(tiles):
                        ins = pe.transpose(b[:, j * P:(j + 1) * P], t, ident[:])
                    finish(ins)

                def s5_in(i):
                    d, j, q = i // STATE_TILES, i % STATE_TILES // 4, i % 4
                    rows = slice(32 * q, 32 * q + 32)
                    if i >= 2:
                        pe.wait_ge(*vec["bu_used"](l, i - 1))
                    u = (u_fwd, u_bwd)[d][rows, j, :]
                    for ri in range(2):
                        ins = pe.matmul(psum[:, i % 2, ri * T:(ri + 1) * T], bT[rows, ri * 2 * WT + d * WT + j, :], u,
                                        start=True, stop=True)
                    ins.then_inc(*s5_bu.rise())

                def s5_out(i):
                    d, j, q = i // STATE_TILES, i % STATE_TILES // 4, i % 4
                    rows = slice(32 * q, 32 * q + 32)
                    if i % 4 == 0 and i >= 8:
                        pe.wait_ge(*vec["y"](l, i // 4 - 1))
                    pe.wait_ge(*vec["xs"](l, i + 1))
                    for ri in range(2):
                        ins = pe.matmul(psum[rows, 2 + i // 4 % 2, 0:T], cT[:, ri * 2 * WT + d * WT + j, rows], xs[:, i % 2, ri, :],
                                        start=ri == 0, stop=ri == 1)
                    ins.then_inc(*s5_y.rise())

                def attention(name, heads, rows, first, vd, v_done, values, between=None):
                    def scores(h):
                        b = begin((name + "_sc", h))
                        if name == "mla" and h % 2 == 0:
                            pe.wait_ge(*vec["rope_q"](l, h // 2 + 1))
                        for q in range(TT):
                            ins = pe.matmul(b[:, q * T:(q + 1) * T], qT[0:rows, h, q * P:(q + 1) * P], kT[0:rows, h, :],
                                            start=True, stop=True)
                        finish(ins)
                    def output(h):
                        b = begin((name + "_pv", h))
                        pe.wait_ge(*act["probT"](l, first + h + 1))
                        if h == 0:
                            pe.wait_ge(*act["v"](l, v_done))
                        o = b[vd * h % P:vd * h % P + vd, 0:T]
                        for kt in range(TT):
                            ins = pe.matmul(o, v_tok[:, kt, h * vd:(h + 1) * vd], probT[:, h % 2, kt, :],
                                            start=kt == 0, stop=kt == TT - 1)
                        finish(ins)

                    scores(0)
                    scores(1)
                    scores(2)
                    values()
                    for h in range(heads):
                        b = begin((name + "_tr", h))
                        pe.wait_ge(*vec["p"](l, 2 * (first + h) + 2))
                        for kt in range(TT):
                            for q in range(TT):
                                ins = pe.transpose(b[:, kt * T + q * P:kt * T + (q + 1) * P],
                                                   prob[:, h % 2, q, kt * P:(kt + 1) * P], ident[:])
                        finish(ins)
                        if h + 3 < heads:
                            scores(h + 3)
                        if between:
                            between(h)
                        if h:
                            output(h - 1)
                    output(heads - 1)

                total_x(("mix_sum", 0), -4)
                for job in IN_ORDER[:3]:
                    pair(job, split(chunk(*job), KT, IN_COLS), hT, KT, 0, 
                         tile_ready=(lambda k: vec["h"](l, k + 1)) if job == IN_ORDER[0] else None)
                b = begin(("s5_par", 0))
                pe.wait_ge(*vec["s5_rows"](l, 1))
                for n, i in enumerate((3, 5, 2, 4)):
                    ins = pe.matmul(b[:, n * ALL_TILES:(n + 1) * ALL_TILES], s5_w[:, i, :], ident[0:ALL_TILES, 0:ALL_TILES],
                                    start=True, stop=True)
                finish(ins)
                for job in IN_ORDER[3:6]:
                    pair(job, split(chunk(*job), KT, IN_COLS), hT, KT, 0)
                pe.wait_ge(*vec["s5_b"](l, 1))
                flat = view(gates, 1024, 4 * WT, P)
                for i in range(4):
                    turn(("s5_b", i), [flat[:, 4 * i + j, :] for j in range(4)])
                pe.wait_ge(*vec["s5_c"](l, 4))
                flat = view(gates, 4096, 4 * WT, P)
                for i in range(4):
                    turn(("s5_c", i), [flat[:, 4 * i + j, :] for j in range(4)])
                pe.wait_ge(*act["u"](l, 4))
                for job in IN_ORDER[6:]:
                    slot = chunk(*job)

                    def tiles(j):
                        for i in TILE_SLOTS.get((job, j), []):
                            if i == 0:
                                pe.wait_ge(*act["s5_bT"](l, 4))
                                pe.wait_ge(*act["s5_cT"](l, 4))
                            s5_in(i)
                            if i >= 2:
                                s5_out(i - 2)

                    if job[0] == "in_k":
                        tiles(0)
                        tiles(1)
                        b = begin(job)
                        for j in range(2):
                            ins = project(b[64:96, j * T:(j + 1) * T], split(slot, KT, 2 * ROPE), hT, KT, j * ROPE, ROPE)
                        finish(ins)
                    else:
                        pair(job, split(slot, KT, IN_COLS), hT, KT, 0, between=tiles)
                s5_out(ALL_TILES - 2)
                s5_out(ALL_TILES - 1)

                def filter_layer(i):
                    b = begin(("filt", i))
                    if i == 0:
                        ins = pe.matmul(b[:, 0:T], filter_w[0:HY_EMB, 0:2, :].rearrange("p a b -> p (a b)"), embed, start=True, stop=True)
                    else:
                        pe.wait_ge(*act["filt"](l, 1))
                        ins = pe.matmul(b[:, 0:T], filter_w[:, 1:3, :].rearrange("p a b -> p (a b)"), filter_h[:, 0, :], start=True, stop=True)
                    finish(ins)

                def conv_out(i):
                    pair(("out_a", i), split(chunk("out_a", i // 2), WT, 512), p_b, WT, (i % 2) * 256)

                pe.wait_ge(*route_loaded(l, 7))
                filter_layer(0)
                pe.wait_ge(*gps["a"](l, 1))
                conv_out(0)
                filter_layer(1)
                b = begin(("mla_sum", 0))
                pe.wait_ge(*vec["square"](l, 1))
                for k in range(4):
                    ins = pe.matmul(b[:, k // 2 * T:(k // 2 + 1) * T], ones[:], oT[:, k, :], start=k % 2 == 0, stop=k % 2 == 1)
                finish(ins)
                for i in range(1, 4):
                    conv_out(i)
                pe.wait_ge(*vec["lat"](l, 4))
                wq, wkv = split(chunk("mla_q"), 2, HEADS * QK), split(chunk("mla_kv"), 2, HEADS * (NOPE + VD))
                c_q, c_kv = latent[:, 0:2, :], latent[:, 2:4, :]
                for name, i in MLA_QK:
                    b = begin((name, i))
                    if name == "mla_qs":
                        pe.wait_ge(*act["qcopy"](l, i + 1))
                        ins = pe.matmul(b[64:96, :], swap[:], qT[0:QK, 2 * i:2 * i + 2, :], start=True, stop=True)
                    for j in range(2):
                        if name == "mla_q":
                            ins = project(b[0:QK, j * T:(j + 1) * T], wq, c_q, 2, (2 * i + j) * QK, QK)
                        elif name == "mla_k":
                            ins = project(b[0:NOPE, j * T:(j + 1) * T], wkv, c_kv, 2, (2 * i + j) * (NOPE + VD), NOPE)
                    finish(ins)
                def mla_values():
                    for i in range(TT):
                        b = begin(("mla_v", i))
                        for k in range(2):
                            wv = wkv[:, k, :].rearrange("p (h c) -> p h c", h=HEADS)[:, :, NOPE:]
                            ins = pe.matmul(b, c_kv[:, k, i * P:(i + 1) * P], wv, start=k == 0, stop=k == 1)
                        finish(ins)

                pe.wait_ge(*act["knope"](l, 4))
                pe.wait_ge(*act["qcopy"](l, 4))
                w3 = chunk("filter")

                def filter_taps(o, i):
                    b = begin((f"kf{o}", i))
                    c = (2 * o + i // 2) * W
                    finish(pe.matmul(b, filter_h[:, 1, (i % 2) * P:(i % 2 + 1) * P], w3[0:HY_FO, c:c + W], start=True, stop=True))

                def mla_between(h):
                    if h in KF_HEADS:
                        if h == 1:
                            pe.wait_ge(*act["filt"](l, 2))
                        filter_taps(0, h - 1)

                attention("mla", HEADS, QK, 0, VD, 2, mla_values, mla_between)

                def dft_of(job, f, src):
                    b = begin(job)
                    for t in range(TT):
                        ins = pe.matmul(b, dft[:, t, f * P:(f + 1) * P], src(t), start=t == 0, stop=t == TT - 1)
                    finish(ins)

                def tap_spectrum(o):
                    pe.wait_ge(*vec["k_sd"](l, 2 * o + 2))
                    for i, (f, sd) in enumerate(((0, 0), (1, 0), (2, 1), (3, 1))):
                        dft_of((f"kd{o}", i), f, lambda t: k_sd[:, sd, t, :])
                    b = begin((f"kd{o}", 4))
                    for t in range(TT):
                        ins = pe.matmul(b[0:1, :], dft[:, t, T:T + 1], k_sd[:, 0, t, :], start=t == 0, stop=t == TT - 1)
                    finish(ins)
                    b = begin((f"kn{o}", 0))
                    pe.wait_ge(*vec["k_sq"](l, o + 1))
                    for ch in range(WT):
                        for t in range(TT):
                            ins = pe.matmul(b[:, ch:ch + 1], k_sq[:, t, ch * P:(ch + 1) * P], ones[:, 0:1], start=t == 0, stop=t == TT - 1)
                    finish(ins)

                def turn_signal(o):
                    if o == 0:
                        pe.wait_ge(*gps["hyena"](l, 1))
                    else:
                        pe.wait_ge(*vec["z"](l, 2))
                    for t in range(TT):
                        src = phyena[:, 0:WT, 1:T + 1] if o == 0 else z_hy[:]
                        turn((f"vt{o}", t), [src[:, j, t * P:(t + 1) * P] for j in range(WT)])

                def signal_spectrum(o):
                    pe.wait_ge(*act["seq"](l, 2 * o + 2))
                    for i, f in enumerate((0, 2, 1, 3)):
                        dft_of((f"vd{o}", i), f, lambda t: seq_tok[:, t, :])

                def back_in_time(o):
                    pe.wait_ge(*vec["spec"](l, 4 * o + 4))
                    for i in range(2):
                        b = begin((f"vi{o}", i))
                        for j in range(2):
                            for f in range(4):
                                c = (2 * i + j) * P
                                ins = pe.matmul(b[:, j * T:(j + 1) * T], spec[:, f, c:c + P], idft[:, f, :], start=f == 0, stop=f == 3)
                        finish(ins)

                def glu(i):
                    for g in range(2):
                        pair(("glu", 2 * i + g), split(chunk("glu", 2 * (i // 2) + g), WT, 512), ys, WT, (i % 2) * 256)

                def mla_out(i):
                    pair(("mla_o", i), split(chunk("mla_o", i // 2), WT, 512), oT, WT, (i % 2) * 256,
                         tile_ready=None if i else lambda k: act["o"](l, 2 * k + 2) if k else None)

                mla_out(0)
                mla_out(1)
                tap_spectrum(0)
                mla_out(2)
                mla_out(3)
                turn_signal(0)
                signal_spectrum(0)
                for i in range(4):
                    filter_taps(1, i)
                pe.wait_ge(*act["gelu"](l, 1))
                glu(0)
                back_in_time(0)
                glu(1)
                turn_signal(1)
                tap_spectrum(1)
                signal_spectrum(1)
                glu(2)
                back_in_time(1)
                glu(3)
                pe.wait_ge(*vec["z"](l, 4))
                for i in range(4):
                    pair(("hy_out", i), split(chunk("hy_out", i // 2), WT, 512), z_hy, WT, (i % 2) * 256)

                for i in range(4):
                    pair(("mix", i), split(chunk("mix", i), KT, 256), merged, KT, 0,
                         tile_ready=None if i else lambda k: vec["merge"](l, 12 + k // 2 + 1))

                def xa_keys(n):
                    b = begin(("xa_k", n))
                    for j in range(2):
                        ins = project(b[:, j * T:(j + 1) * T], split(chunk("xa_kv", 2 * n + j), KT, 256), memT, KT, 0)
                    finish(ins)

                pe.wait_ge(mem_step, 2 * KT)
                xa_keys(0)
                total_x(("xa_sum", 0), 1)
                xa_keys(1)
                for n in range(2):
                    pair(("xa_q", n), split(chunk("xa_q", n), KT, 256), hT, KT, 0, 
                         tile_ready=None if n else lambda k: vec["h"](l, KT + k + 1))

                def xa_values(t):
                    b = begin(("xa_v", t))
                    for h in range(XH):
                        w = split(chunk("xa_kv", h), KT, 256)
                        for k in range(KT):
                            ins = pe.matmul(b[:, h * XD:(h + 1) * XD], memT[:, k, t * P:(t + 1) * P], w[:, k, XD:], start=k == 0, stop=k == KT - 1)
                    finish(ins)

                xa_values(0)
                pe.wait_ge(*act["xa_qk"](l, 4))
                attention("xa", XH, XD, HEADS, XD, 4, lambda: xa_values(1))
                for i in range(4):
                    pair(("xa_o", i), split(chunk("xa_o", i // 2), WT, 512), oT, WT, (i % 2) * 256,
                         tile_ready=None if i else lambda k: act["o"](l, HEADS + k + 1))

                total_x(("moe_sum", 0), 5)
                b = begin(("route", 0))
                for t in range(TT):
                    o = b[:, 64 * t:64 * t + GROUPS + EXPERTS]
                    for k in range(KT):
                        if t == 0:
                            pe.wait_ge(*vec["h"](l, 2 * KT + k + 1))
                        pe.matmul(o, hT[:, k, t * P:(t + 1) * P], route_w[:, k, :], start=k == 0, stop=False)
                    ins = pe.matmul(o, ones[0:1, :], bias[:], start=False, stop=True)
                finish(ins)
                for i in range(4):
                    turn(("h_tok", i), [hT[:, 4 * (i % 2) + k, (i // 2) * P:(i // 2 + 1) * P] for k in range(4)])
                b = begin(("rank", 0))
                pe.wait_ge(*vec["oh"](l, 1))
                oh = r["oh4"]
                for c, terms in enumerate((((upto, 0),), ((ones, 0), (upto, 1)), ((ones, 0), (ones, 1)))):
                    for n, (m, t) in enumerate(terms):
                        ins = pe.matmul(b[:, c * GROUPS:(c + 1) * GROUPS], m[:], oh[:, t, :], start=n == 0, stop=n == len(terms) - 1)
                finish(ins)
                pe.wait_ge(*act["h_tok"](l, 4))
                for k in range(KT):
                    b = begin(("gather", k))
                    if k == 0:
                        pe.wait_ge(*vec["pick"](l, 2 * GROUPS))
                    for t in range(TT):
                        ins = pe.matmul(b[:, 0:GROUPS * CAP], h_tok[:, t, k * P:(k + 1) * P], pick[:, t].rearrange("p g s -> p (g s)"),
                                        start=t == 0, stop=t == TT - 1)
                    finish(ins)
                for i in range(2):
                    b = begin(("back", i))
                    for g in range(2):
                        for t in range(TT):
                            ins = pe.transpose(b[0:CAP, g * T + t * P:g * T + (t + 1) * P], pick[:, t, 2 * i + g, :], ident[:])
                    finish(ins)
                b = begin(("cw", 0))
                pe.wait_ge(*vec["comb"](l, 1))
                for g in range(GROUPS):
                    es = slice(PER_GROUP * g, PER_GROUP * (g + 1))
                    for t in range(TT):
                        ins = pe.matmul(b[0:CAP, es], pick[:, t, g, :], r["comb"][:, t, es], start=t == 0, stop=t == TT - 1)
                finish(ins)

                def expert_products(first, t, h_in, width, down):
                    for j in range(TURN):
                        w = []
                        for s in range(3 * j, 3 * j + 3):
                            pe.wait_ge(slot_loaded[s].sem, l * (16 * slot_loaded[s].per_layer) + t * 16
                                       + 16 * (slot_dmas[s] + first // TURN + 1))
                            w.append(split(ring[:, s, :], (KT, KT, 2)[s % 3], (FF, FF, D)[s % 3]))
                        base = l * (2 * EXPERTS) + t * (2 * TURN)
                        for f in range(2):
                            n = 2 * (first + j) + f
                            pe.wait_ge(act["silu"].sem, base + (n + 1))
                            pe.wait_ge(vec["hid"].sem, base + (n + 1))
                            project(psum[:, 2 * f, 0:width], w[0], h_in, KT, f * P).then_inc(moe_gate.sem, 1)
                            project(psum[:, 2 * f + 1, 0:width], w[1], h_in, KT, f * P).then_inc(moe_up.sem, 1)
                        for f in range(2):
                            pe.wait_ge(vec["hid"].sem, base + (2 + 2 * (first + j) + f + 1))
                            ins = down(w[2], f, t, j)
                        ins.then_inc(moe_down.sem, 1)

                flag = pe.value_load(crowded[0:1, 0:1], min_val=0, max_val=1)
                with pe.If(flag < 1):
                    pe.sem_inc(dense_cw.sem, EXPERTS // 2)
                    for g in range(GROUPS):
                        def down(w, f, t, j):
                            if f == 0:
                                pe.wait_ge(vec["y_slot"].sem, l * (1 + EXPERTS) + t * TURN + (1 + PER_GROUP * g + j))
                            for i in range(2):
                                ins = pe.matmul(psum[0:CAP, 4 + 2 * j + i, :], hid[:, f, 0:CAP], w[:, f, i * 512:(i + 1) * 512],
                                                start=f == 0, stop=f == 1)
                            return ins

                        with pe.Fori(0, GROUP_TURNS) as t:
                            if g == 0:
                                pe.wait_ge(*act["gather"](l, KT))
                                pe.wait_ge(*act["cw"](l, 1))
                            expert_products(PER_GROUP * g, t, hg[:, :, g * CAP:(g + 1) * CAP], CAP, down)
                    pe.wait_ge(*act["back"](l, 2))
                    pe.wait_ge(*vec["y_slot"](l, 1 + EXPERTS))
                    for m in range(KT):
                        for g in range(GROUPS):
                            ins = pe.matmul(psum[:, 4 + m // 2, (m % 2) * T:(m % 2 + 1) * T], y_slot[0:CAP, g, m * P:(m + 1) * P],
                                            back[0:CAP, g, :], start=g == 0, stop=g == GROUPS - 1)
                        if m % 2:
                            ins.then_inc(*moe_out.rise())
                with pe.Else():
                    pe.sem_inc(moe_out.sem, KT // 2)
                    pe.wait_ge(*act["cw"](l, 1))
                    for i in range(EXPERTS // 2):
                        if i >= 4:
                            pe.wait_ge(*dense_cw_out(l, i - 3))
                        for j in range(4):
                            ins = pe.matmul(psum[:, 4 + i % 4, j * P:(j + 1) * P],
                                            r["comb"][:, j % 2, 2 * i + j // 2:2 * i + j // 2 + 1].to_broadcast([P, P]), ident[:],
                                            start=True, stop=True)
                        ins.then_inc(*dense_cw.rise())
                    pe.wait_ge(*dense_cw_out(l, EXPERTS // 2))
                    for i in range(4):
                        pe.matmul(psum[:, 4 + i, :], zeros[:], dft[:, 0, :], start=True, stop=True, skip_group_check=True)

                    def down(w, f, t, j):
                        for m in range(KT):
                            ins = pe.matmul(psum[:, 4 + m // 2, (m % 2) * T:(m % 2 + 1) * T], w[:, f, m * P:(m + 1) * P],
                                            hid[:, f, :], start=False, stop=True, skip_group_check=True)
                        return ins

                    with pe.Fori(0, TURNS) as t:
                        expert_products(0, t, hT, T, down)

            pe.wait_ge(*vec["x"](DEPTH - 1, 12))
            for k in range(KT):
                if k % 2 == 0:
                    pe.wait_ge(*vec["square"](DEPTH, k // 2 + 1 - 4))
                ins = pe.matmul(psum[:, 4, 0:T], ones[:], x_sq[:, k, :], start=k == 0, stop=k == KT - 1)
            ins.then_inc(end_pe, 1)
            pe.wait_ge(end_dve, 1 + KT // 2)
            for i in (0, 2, 1, 3):
                if i == 1:
                    pe.wait_ge(end_dve, 1 + KT)
                for k in range(4):
                    ins = pe.transpose(psum[:, i, k * P:(k + 1) * P], hT[:, 4 * (i % 2) + k, (i // 2) * P:(i // 2 + 1) * P], ident[:])
                ins.then_inc(end_pe, 1)

        for sig in [product, vector_step, pool_step, route_loaded, moe_out, dense_cw, dense_cw_out, s5_bu, s5_y, s5_loaded, *act.values(), *vec.values(), *gps.values()]:
            if sig.count != sig.per_layer and sig not in (act["silu"], vec["hid"], vec["y_slot"]):
                raise AssertionError(f"{sig.sem} rises {sig.count} times in a layer, not {sig.per_layer}")




def constants():
    f8 = np.float64
    t = np.arange(T)
    small = np.zeros((P, 20), np.float32)
    small[:, 0] = EPS
    small[:, 1] = (np.arange(P) // 16) % 2 == 0
    small[:, 2] = (np.arange(P) // 16) % 2 == 1
    inv = 1.0 / (10000.0 ** (np.arange(0, ROPE, 2, dtype=f8) / ROPE))
    small[64:96, 3] = np.tile(inv / (2 * np.pi), 2)
    small[64:80, 4], small[80:96, 4] = -1.0, 1.0
    small[:, 5:9] = np.arange(4, 0, -1)
    small[:, 9:17] = np.arange(8, 0, -1)
    small[:, 17] = 0.25
    f = np.arange(T)
    ang = 2 * np.pi * ((t[:, None] * f[None]) % NFFT) / NFFT
    cos, sin = np.cos(ang), np.sin(ang)
    sin[:, 0] = (-1.0) ** t
    dft = np.concatenate([cos, sin], axis=1)
    weight = np.full(2 * T, 2.0 / NFFT)
    weight[0] = weight[T] = 1.0 / NFFT
    idft = dft.T * weight[:, None]
    t_norm = np.arange(T, dtype=np.float32) / np.float32(T - 1)
    bands = np.linspace(1e-4, (HY_EMB - 1) // 2 - 1, (HY_EMB - 1) // 2)
    a = (2 * np.pi / T) * t[:, None] * bands[None]
    embed = np.concatenate([t_norm[:, None], np.cos(a), -np.sin(a)], axis=-1).T
    deltas = np.abs(np.linspace(math.log(1e-2) / 1.5, math.log(1e-2) / 0.3, W))
    decay = np.exp(-t_norm.astype(f8)[:, None] * deltas)
    out = {"c_ident": np.eye(P), "c_upto": np.triu(np.ones((P, P))), "c_swap": np.eye(QK)[:, NOPE + (np.arange(ROPE) + ROPE // 2) % ROPE], "c_small": small, "c_clock": np.tile(t, (P, 1)),
           "c_dft": dft.reshape(TT, P, NFFT).transpose(1, 0, 2), "c_idft": idft.reshape(4, P, T).transpose(1, 0, 2),
           "c_decay": decay.reshape(TT, P, W).transpose(1, 0, 2), "c_embed": embed}
    return {k: np.ascontiguousarray(v.astype(np.float32)) for k, v in out.items()}


def kernel(**inputs):
    import concourse.bacc as _bacc
    from concourse.bass_utils import run_bass_kernel_spmd as _run

    nc = _bacc.Bacc("TRN2", target_bir_lowering=False, num_devices=1)
    arrays, aps = {}, {}
    for name, value in {**inputs, **constants()}.items():
        v = np.ascontiguousarray(value)
        arrays[f"in_{name}"] = v
        aps[name] = nc.dram_tensor(f"in_{name}", v.shape, mybir.dt.from_np(v.dtype), kind="ExternalInput").ap()
    out = nc.dram_tensor("out_0", (1, T, D), F32, kind="ExternalOutput").ap()
    encoder(nc, aps, out)
    r = _run(nc, [arrays], core_ids=[0])
    return r.results[0]["out_0"]
```
